# Optimizing a Trainium2 kernel written in Bass

```python
import math
import jax
import jax.numpy as jnp
from jax import lax
import numpy as np
import jax, jax.numpy as jnp

D_MODEL = 1024
BATCH = 1
SEQ = 256
DEPTH = 2

HEAD_DIM = 64
CONV_CH = 512
CONV_K = 3
FOX_HEADS = 8
FOX_WIDTH = FOX_HEADS * HEAD_DIM
EVEN_IN = 3 * CONV_CH + 3 * FOX_WIDTH + FOX_HEADS
Q_BLOCK = 128
NSA_GROUPS = 4
NSA_HPG = 4
NSA_HEADS = NSA_GROUPS * NSA_HPG
NSA_WIDTH = NSA_HEADS * HEAD_DIM
NSA_KV = NSA_GROUPS * HEAD_DIM
CMP_LEN = 32
CMP_STRIDE = 16
SLC_LEN = 64
SLC_TOPN = 16
WINDOW = 512
SLC_QCHUNK = 16
ODD_IN = NSA_WIDTH + 6 * NSA_KV + 3 * NSA_HEADS
REL_BUCKETS = 32
REL_MAX_DIST = 128
PEER_HEADS = 8
PEER_NKEYS = 128
PEER_EXPERTS = PEER_NKEYS * PEER_NKEYS
PEER_QDIM = 128
PEER_TOPK = 16
PEER_CHUNK = 128
N_EVEN = (DEPTH + 1) // 2
N_ODD = DEPTH // 2
EPS = 1e-6
NEG_INF = -1e30
FORCE_SCORE = 1e6


def rms_norm(x, g):
    xf = x.astype(jnp.float32)
    y = xf * lax.rsqrt(jnp.mean(xf * xf, axis=-1, keepdims=True) + EPS)
    return (y * g.astype(jnp.float32)).astype(x.dtype)

def modulate(h, shift, scale):
    return h * (1 + scale[:, None, :]) + shift[:, None, :]

def masked_softmax(s, mask):
    s = jnp.where(mask, s.astype(jnp.float32), NEG_INF)
    return jax.nn.softmax(s, axis=-1) * mask

def rel_bucket(dist):
    n = jnp.maximum(dist, 0)
    max_exact = REL_BUCKETS // 2
    nf = jnp.maximum(n, 1).astype(jnp.float32)
    large = max_exact + (jnp.log(nf / max_exact) / math.log(REL_MAX_DIST / max_exact)
                         * (REL_BUCKETS - max_exact)).astype(jnp.int32)
    large = jnp.minimum(large, REL_BUCKETS - 1)
    return jnp.where(n < max_exact, n, large)

def short_conv(u, w):
    return lax.conv_general_dilated(
        u, w.astype(u.dtype)[:, None, :], window_strides=(1,), padding=((CONV_K - 1, 0),),
        dimension_numbers=('NWC', 'WIO', 'NWC'), feature_group_count=u.shape[-1])

def fox_attention(q, k, v, logf):
    B, S, H, Dh = q.shape
    nb = S // Q_BLOCK
    cum_t = jnp.cumsum(logf, axis=1).transpose(0, 2, 1)
    kpos = jnp.arange(S)
    scale = Dh ** -0.5
    qb = q.reshape(B, nb, Q_BLOCK, H, Dh).swapaxes(0, 1)
    cb = cum_t.reshape(B, H, nb, Q_BLOCK).transpose(2, 0, 1, 3)
    tb = kpos.reshape(nb, Q_BLOCK)

    def block(args):
        qi, ci, ti = args
        s = jnp.einsum('bqhd,bkhd->bhqk', qi, k).astype(jnp.float32) * scale
        s = s + (ci[..., None] - cum_t[:, :, None, :])
        p = masked_softmax(s, ti[:, None] >= kpos[None, :])
        return jnp.einsum('bhqk,bkhd->bqhd', p.astype(v.dtype), v)

    out = lax.map(block, (qb, cb, tb))
    return out.swapaxes(0, 1).reshape(B, S, H, Dh)

def conv_fox_mixer(h, w_in, b_f, conv_w, q_g, k_g, w_out):
    B, S, _ = h.shape
    splits = list(np.cumsum([CONV_CH] * 3 + [FOX_WIDTH] * 3))
    cb, cc, ch, q, k, v, f = jnp.split(h @ w_in, splits, axis=-1)
    conv_out = cb * short_conv(cc * ch, conv_w)
    q = rms_norm(q.reshape(B, S, FOX_HEADS, HEAD_DIM), q_g)
    k = rms_norm(k.reshape(B, S, FOX_HEADS, HEAD_DIM), k_g)
    v = v.reshape(B, S, FOX_HEADS, HEAD_DIM)
    logf = jax.nn.log_sigmoid((f + b_f).astype(jnp.float32))
    attn = fox_attention(q, k, v, logf).reshape(B, S, FOX_WIDTH)
    return jnp.concatenate([conv_out, attn], axis=-1) @ w_out

def nsa_mixer(h, w_in, b_gate, q_g, k_g, cmp_pos, cmp_w1, cmp_w2, rel_table, w_out):
    B, S, _ = h.shape
    G, J, Dh = NSA_GROUPS, NSA_HPG, HEAD_DIM
    f32 = jnp.float32
    splits = list(np.cumsum([NSA_WIDTH] + [NSA_KV] * 6))
    q, kc, vc, ks, vs, kw, vw, gl = jnp.split(h @ w_in, splits, axis=-1)
    q = rms_norm(q.reshape(B, S, G, J, Dh), q_g)
    kc, vc, ks, vs, kw, vw = [a.reshape(B, S, G, Dh) for a in (kc, vc, ks, vs, kw, vw)]
    ks = rms_norm(ks, k_g[1])
    kw = rms_norm(kw, k_g[2])
    gates = jax.nn.sigmoid((gl + b_gate).astype(f32)).reshape(B, S, G, J, 3).astype(h.dtype)
    tpos = jnp.arange(S)
    table = rel_table.reshape(REL_BUCKETS, G, J)
    scale = Dh ** -0.5

    n_cmp = (S - CMP_LEN) // CMP_STRIDE + 1
    starts = jnp.arange(n_cmp) * CMP_STRIDE
    ends = starts + CMP_LEN - 1
    tok = starts[:, None] + jnp.arange(CMP_LEN)[None, :]

    def compress(a, pos, w1, w2):
        blk = a[:, tok] + pos[:, None, :]
        blk = blk.transpose(0, 1, 3, 2, 4).reshape(B, n_cmp, G, CMP_LEN * Dh)
        return jax.nn.gelu(blk @ w1) @ w2

    Kc = rms_norm(compress(kc, cmp_pos[0], cmp_w1[0], cmp_w2[0]), k_g[0])
    Vc = compress(vc, cmp_pos[1], cmp_w1[1], cmp_w2[1])
    s_c = jnp.einsum('bsgjd,bngd->bgjsn', q, Kc).astype(f32) * scale
    s_c = s_c + table[rel_bucket(tpos[:, None] - ends[None, :])].transpose(2, 3, 0, 1)
    p_c = masked_softmax(s_c, ends[None, :] <= tpos[:, None])
    o_c = jnp.einsum('bgjsn,bngd->bsgjd', p_c.astype(Vc.dtype), Vc)

    n_slc = S // SLC_LEN
    top_n = min(SLC_TOPN, n_slc)
    blk_ids = jnp.arange(n_slc)
    bstart = blk_ids * SLC_LEN
    overlap = ((starts[:, None] < bstart[None, :] + SLC_LEN)
               & (starts[:, None] + CMP_LEN > bstart[None, :])).astype(f32)
    imp = jnp.einsum('bgjsn,nm->bgsm', p_c, overlap)
    cur = tpos // SLC_LEN
    forced = (blk_ids[None, :] == 0) | (blk_ids[None, :] == cur[:, None]) | (blk_ids[None, :] == cur[:, None] - 1)
    imp = jnp.where(forced, FORCE_SCORE, jnp.where(bstart[None, :] <= tpos[:, None], imp, -1.0))
    sel_score, sel_idx = lax.top_k(imp, top_n)
    sel_valid = sel_score >= 0

    Ks = ks.reshape(B, n_slc, SLC_LEN, G, Dh).transpose(0, 3, 1, 2, 4)
    Vs = vs.reshape(B, n_slc, SLC_LEN, G, Dh).transpose(0, 3, 1, 2, 4)
    nq = S // SLC_QCHUNK
    bi = jnp.arange(B)[:, None, None, None]
    gi = jnp.arange(G)[None, :, None, None]

    def slc_chunk(args):
        qi, idx, val, ti = args
        Kg = Ks[bi, gi, idx]
        Vg = Vs[bi, gi, idx]
        kpos = idx[..., None] * SLC_LEN + jnp.arange(SLC_LEN)
        dist = ti[None, None, :, None, None] - kpos
        mask = val[..., None] & (dist >= 0)
        bias = jnp.moveaxis(table[rel_bucket(dist), gi[..., None]], -1, 2)
        s = jnp.einsum('bqgjd,bgqnld->bgjqnl', qi, Kg).astype(f32) * scale + bias
        sh = s.shape
        m = jnp.broadcast_to(mask[:, :, None], sh).reshape(sh[:4] + (-1,))
        p = masked_softmax(s.reshape(sh[:4] + (-1,)), m).reshape(sh)
        return jnp.einsum('bgjqnl,bgqnld->bqgjd', p.astype(Vg.dtype), Vg)

    qs = q.reshape(B, nq, SLC_QCHUNK, G, J, Dh).swapaxes(0, 1)
    idx_s = sel_idx.reshape(B, G, nq, SLC_QCHUNK, top_n).transpose(2, 0, 1, 3, 4)
    val_s = sel_valid.reshape(B, G, nq, SLC_QCHUNK, top_n).transpose(2, 0, 1, 3, 4)
    t_s = tpos.reshape(nq, SLC_QCHUNK)
    o_s = lax.map(slc_chunk, (qs, idx_s, val_s, t_s)).swapaxes(0, 1).reshape(B, S, G, J, Dh)

    kwp = jnp.pad(kw, ((0, 0), (WINDOW, 0), (0, 0), (0, 0)))
    vwp = jnp.pad(vw, ((0, 0), (WINDOW, 0), (0, 0), (0, 0)))
    nb = S // Q_BLOCK
    span = Q_BLOCK + WINDOW
    koff = jnp.arange(span)
    dist_w = jnp.arange(Q_BLOCK)[:, None] + WINDOW - koff[None, :]
    band = (dist_w >= 0) & (dist_w < WINDOW)
    bias_w = table[rel_bucket(dist_w)].transpose(2, 3, 0, 1)

    def win_block(args):
        qi, i = args
        start = i * Q_BLOCK
        kb = lax.dynamic_slice_in_dim(kwp, start, span, axis=1)
        vb = lax.dynamic_slice_in_dim(vwp, start, span, axis=1)
        s = jnp.einsum('bqgjd,bkgd->bgjqk', qi, kb).astype(f32) * scale + bias_w
        mask = band & ((start - WINDOW + koff) >= 0)[None, :]
        p = masked_softmax(s, mask)
        return jnp.einsum('bgjqk,bkgd->bqgjd', p.astype(vb.dtype), vb)

    qw = q.reshape(B, nb, Q_BLOCK, G, J, Dh).swapaxes(0, 1)
    o_w = lax.map(win_block, (qw, jnp.arange(nb))).swapaxes(0, 1).reshape(B, S, G, J, Dh)

    o = gates[..., 0:1] * o_c + gates[..., 1:2] * o_s + gates[..., 2:3] * o_w
    return o.reshape(B, S, NSA_WIDTH) @ w_out

def peer_ffn(h, w_q, sub_keys, u, v):
    B, S, D = h.shape
    T = B * S
    half = PEER_QDIM // 2
    hc = h.reshape(T // PEER_CHUNK, PEER_CHUNK, D)

    def chunk(xc):
        q = (xc @ w_q).reshape(-1, PEER_HEADS, 2, half)
        s = jnp.einsum('thpd,pkd->thpk', q, sub_keys).astype(jnp.float32)
        sv, si = lax.top_k(s, PEER_TOPK)
        cand = (sv[:, :, 0, :, None] + sv[:, :, 1, None, :]).reshape(-1, PEER_HEADS, PEER_TOPK * PEER_TOPK)
        cand_id = (si[:, :, 0, :, None] * PEER_NKEYS + si[:, :, 1, None, :]).reshape(-1, PEER_HEADS, PEER_TOPK * PEER_TOPK)
        cv, ci = lax.top_k(cand, PEER_TOPK)
        eid = jnp.take_along_axis(cand_id, ci, axis=-1)
        g = jax.nn.softmax(cv, axis=-1)
        ue = u[eid]
        ve = v[eid]
        a = jax.nn.gelu(jnp.einsum('td,thkd->thk', xc, ue)).astype(jnp.float32)
        return jnp.einsum('thk,thkd->td', (g * a).astype(ve.dtype), ve)

    return lax.map(chunk, hc).reshape(B, S, D)

def first_inputs(seed: int = 0) -> dict:
    key = jax.random.key(seed)
    ks = jax.random.split(key, 24)
    D = D_MODEL

    def nrm(k, shape, s):
        return jax.random.normal(k, shape, jnp.float32) * s

    return {
        'x': nrm(ks[0], (BATCH, SEQ, D), 1.0),
        'c': nrm(ks[1], (BATCH, D), 1.0),
        'ada_w': nrm(ks[2], (DEPTH, D, 6 * D), 0.5 * D ** -0.5),
        'ada_b': nrm(ks[3], (DEPTH, 6 * D), 0.01),
        'norm_g': 1.0 + nrm(ks[4], (DEPTH, 2, D), 0.05),
        'even_w_in': nrm(ks[5], (N_EVEN, D, EVEN_IN), D ** -0.5),
        'even_b_f': jax.random.uniform(ks[6], (N_EVEN, FOX_HEADS), jnp.float32, 1.0, 6.0),
        'even_conv_w': nrm(ks[7], (N_EVEN, CONV_K, CONV_CH), CONV_K ** -0.5),
        'even_q_g': 1.0 + nrm(ks[8], (N_EVEN, HEAD_DIM), 0.05),
        'even_k_g': 1.0 + nrm(ks[9], (N_EVEN, HEAD_DIM), 0.05),
        'even_w_out': nrm(ks[10], (N_EVEN, CONV_CH + FOX_WIDTH, D), (CONV_CH + FOX_WIDTH) ** -0.5),
        'odd_w_in': nrm(ks[11], (N_ODD, D, ODD_IN), D ** -0.5),
        'odd_b_gate': nrm(ks[12], (N_ODD, 3 * NSA_HEADS), 0.01),
        'odd_q_g': 1.0 + nrm(ks[13], (N_ODD, HEAD_DIM), 0.05),
        'odd_k_g': 1.0 + nrm(ks[14], (N_ODD, 3, HEAD_DIM), 0.05),
        'odd_cmp_pos': nrm(ks[15], (N_ODD, 2, CMP_LEN, HEAD_DIM), 0.1),
        'odd_cmp_w1': nrm(ks[16], (N_ODD, 2, CMP_LEN * HEAD_DIM, HEAD_DIM), (CMP_LEN * HEAD_DIM) ** -0.5),
        'odd_cmp_w2': nrm(ks[17], (N_ODD, 2, HEAD_DIM, HEAD_DIM), HEAD_DIM ** -0.5),
        'odd_w_out': nrm(ks[18], (N_ODD, NSA_WIDTH, D), NSA_WIDTH ** -0.5),
        'rel_table': nrm(ks[19], (REL_BUCKETS, NSA_HEADS), 0.5),
        'peer_w_q': nrm(ks[20], (DEPTH, D, PEER_HEADS * PEER_QDIM), D ** -0.5),
        'peer_keys': nrm(ks[21], (DEPTH, 2, PEER_NKEYS, PEER_QDIM // 2), (PEER_QDIM // 2) ** -0.5),
        'peer_u': nrm(ks[22], (DEPTH, PEER_EXPERTS, D), D ** -0.5),
        'peer_v': nrm(ks[23], (DEPTH, PEER_EXPERTS, D), PEER_HEADS ** -0.5),
    }

def first_block(x, c, ada_w, ada_b, norm_g, even_w_in, even_b_f, even_conv_w, even_q_g, even_k_g,
              even_w_out, odd_w_in, odd_b_gate, odd_q_g, odd_k_g, odd_cmp_pos, odd_cmp_w1, odd_cmp_w2,
              odd_w_out, rel_table, peer_w_q, peer_keys, peer_u, peer_v):
    mods = jnp.einsum('bd,lde->lbe', jax.nn.silu(c), ada_w) + ada_b[:, None, :]
    for layer in range(DEPTH):
        sh1, sc1, g1, sh2, sc2, g2 = jnp.split(mods[layer], 6, axis=-1)
        h = modulate(rms_norm(x, norm_g[layer, 0]), sh1, sc1)
        i = layer // 2
        if layer % 2 == 0:
            y = conv_fox_mixer(h, even_w_in[i], even_b_f[i], even_conv_w[i], even_q_g[i], even_k_g[i],
                               even_w_out[i])
        else:
            y = nsa_mixer(h, odd_w_in[i], odd_b_gate[i], odd_q_g[i], odd_k_g[i], odd_cmp_pos[i],
                          odd_cmp_w1[i], odd_cmp_w2[i], rel_table, odd_w_out[i])
        x = x + g1[:, None, :] * y
        h = modulate(rms_norm(x, norm_g[layer, 1]), sh2, sc2)
        x = x + g2[:, None, :] * peer_ffn(h, peer_w_q[layer], peer_keys[layer], peer_u[layer], peer_v[layer])
    return x


SSD_HEADS = 16
SSD_HEAD_DIM = 64
SSD_WIDTH = SSD_HEADS * SSD_HEAD_DIM
SSD_GROUPS = 4
SSD_STATE = 128
CONV_K_2 = 4
SSD_CHUNK = 128
CONV_DIM = SSD_WIDTH + 2 * SSD_GROUPS * SSD_STATE

ATT_HEADS = 16
ATT_HEAD_DIM = 64
ATT_WIDTH = ATT_HEADS * ATT_HEAD_DIM
ATT_BRANCHES = ((128, 1), (512, 4), (2048, 16))
BAND_BLOCK = 128

MIX_WIDTH = SSD_WIDTH + ATT_WIDTH
IN_PROJ = SSD_WIDTH + CONV_DIM + SSD_HEADS + 3 * ATT_WIDTH
D_FF = 2816


def rms_norm_2(x, w):
    xf = x.astype(jnp.float32)
    y = xf * lax.rsqrt(jnp.mean(xf * xf, axis=-1, keepdims=True) + EPS)
    return (y * w.astype(jnp.float32)).astype(x.dtype)

def swiglu(x, w_gate, w_up, w_down):
    return (jax.nn.silu(x @ w_gate) * (x @ w_up)) @ w_down

def causal_depthwise_conv(x, w, b):
    c = x.shape[-1]
    y = lax.conv_general_dilated(
        x, w[:, None, :], window_strides=(1,), padding=[(CONV_K_2 - 1, 0)],
        dimension_numbers=("NWC", "WIO", "NWC"), feature_group_count=c)
    return y + b

def ssd_mixer(xbc, dt_raw, z, dt_bias, a_log, d_skip, norm_w):
    out_dtype = z.dtype
    b, s, _ = xbc.shape
    H, P, G, N, L = SSD_HEADS, SSD_HEAD_DIM, SSD_GROUPS, SSD_STATE, SSD_CHUNK
    R = H // G
    nc = s // L
    xbc = xbc.astype(jnp.float32)
    xs, bm, cm = jnp.split(xbc, [SSD_WIDTH, SSD_WIDTH + G * N], axis=-1)
    dt = jax.nn.softplus(dt_raw.astype(jnp.float32) + dt_bias.astype(jnp.float32))
    a = -jnp.exp(a_log.astype(jnp.float32))
    xh = xs.reshape(b, s, H, P)
    X = (xh * dt[..., None]).reshape(b, nc, L, G, R, P)
    adt = (dt * a).reshape(b, nc, L, G, R).transpose(0, 3, 4, 1, 2)
    a_cum = jnp.cumsum(adt, axis=-1)
    Bc = bm.reshape(b, nc, L, G, N)
    Cc = cm.reshape(b, nc, L, G, N)
    causal = jnp.tril(jnp.ones((L, L), dtype=bool))
    seg = a_cum[..., :, None] - a_cum[..., None, :]
    lmat = jnp.where(causal, jnp.exp(jnp.where(causal, seg, 0.0)), 0.0)
    cb = jnp.einsum("bclgn,bcsgn->bgcls", Cc, Bc)
    y_diag = jnp.einsum("bgcls,bgrcls,bcsgrp->bclgrp", cb, lmat, X)
    decay_states = jnp.exp(a_cum[..., -1:] - a_cum)
    states = jnp.einsum("bclgn,bgrcl,bclgrp->bcgrpn", Bc, decay_states, X)
    chunk_decay = jnp.exp(a_cum[..., -1])

    def step(h, inp):
        st, dec = inp
        return h * dec[..., None, None] + st, h

    h0 = jnp.zeros((b, G, R, P, N), jnp.float32)
    _, prev = lax.scan(step, h0, (states.transpose(1, 0, 2, 3, 4, 5),
                                  chunk_decay.transpose(3, 0, 1, 2)))
    y_off = jnp.einsum("bclgn,cbgrpn,bgrcl->bclgrp", Cc, prev, jnp.exp(a_cum))
    y = (y_diag + y_off).reshape(b, s, H, P) + xh * d_skip.astype(jnp.float32)[:, None]
    y = y.reshape(b, s, SSD_WIDTH) * jax.nn.silu(z.astype(jnp.float32))
    yg = y.reshape(b, s, G, SSD_WIDTH // G)
    yg = yg * lax.rsqrt(jnp.mean(yg * yg, axis=-1, keepdims=True) + EPS)
    y = yg.reshape(b, s, SSD_WIDTH) * norm_w.astype(jnp.float32)
    return y.astype(out_dtype)

def dilated_branch(q, k, v, dilation, back):
    b, s, h, e = q.shape
    n = s // dilation
    nb = -(-n // BAND_BLOCK)
    npad = nb * BAND_BLOCK
    blk = BAND_BLOCK

    def blocks(t):
        t = t.reshape(b, n, dilation, h, e)
        t = jnp.pad(t, ((0, 0), (0, npad - n), (0, 0), (0, 0), (0, 0)))
        return t.reshape(b, nb, blk, dilation, h, e)

    def with_prev(t):
        prev = jnp.pad(t[:, :-1], ((0, 0), (1, 0), (0, 0), (0, 0), (0, 0), (0, 0)))
        return jnp.concatenate([prev, t], axis=2)

    qb = blocks(q)
    kk = with_prev(blocks(k))
    vv = with_prev(blocks(v))
    scores = jnp.einsum("bnqrhe,bnkrhe->bnrhqk", qb, kk).astype(jnp.float32)
    scores = scores * (1.0 / math.sqrt(e))
    qi = jnp.arange(blk)[:, None]
    kj = jnp.arange(2 * blk)[None, :]
    dist = qi + blk - kj
    bidx = jnp.arange(nb)[:, None, None]
    valid = (dist >= 0) & (dist <= back) & (bidx * blk - blk + kj >= 0)
    scores = jnp.where(valid[None, :, None, None], scores, -jnp.inf)
    m = jnp.max(scores, axis=-1, keepdims=True)
    p = jnp.exp(scores - m)
    den = jnp.sum(p, axis=-1, keepdims=True)
    o = jnp.einsum("bnrhqk,bnkrhe->bnqrhe", (p / den).astype(v.dtype), vv)
    lse = (m + jnp.log(den))[..., 0]
    o = o.reshape(b, npad, dilation, h, e)[:, :n].reshape(b, s, h, e)
    lse = lse.transpose(0, 1, 4, 2, 3).reshape(b, npad, dilation, h)[:, :n].reshape(b, s, h)
    return o, lse

def dilated_attention(q, k, v):
    outs, lses = [], []
    for window, dilation in ATT_BRANCHES:
        o, lse = dilated_branch(q, k, v, dilation, window // dilation)
        outs.append(o)
        lses.append(lse)
    wts = jax.nn.softmax(jnp.stack(lses, axis=0), axis=0)
    y = jnp.einsum("kbsh,kbshe->bshe", wts.astype(q.dtype), jnp.stack(outs, axis=0))
    return y

def second_inputs(seed: int = 0) -> dict:
    key = jax.random.key(seed)
    ks = jax.random.split(key, 24)
    f = jnp.float32

    def normal(k, shape, scale):
        return jax.random.normal(k, shape, f) * scale

    def gain(k, shape):
        return 1.0 + 0.02 * jax.random.normal(k, shape, f)

    dt = jnp.exp(jax.random.uniform(ks[10], (DEPTH, SSD_HEADS), f)
                 * (math.log(0.1) - math.log(0.001)) + math.log(0.001))
    return {
        "x": jax.random.normal(ks[0], (BATCH, SEQ, D_MODEL), f),
        "ffn1_norm": gain(ks[1], (DEPTH, D_MODEL)),
        "ffn1_w_gate": normal(ks[2], (DEPTH, D_MODEL, D_FF), D_MODEL ** -0.5),
        "ffn1_w_up": normal(ks[3], (DEPTH, D_MODEL, D_FF), D_MODEL ** -0.5),
        "ffn1_w_down": normal(ks[4], (DEPTH, D_FF, D_MODEL), D_FF ** -0.5),
        "mix_norm": gain(ks[5], (DEPTH, D_MODEL)),
        "w_in": normal(ks[6], (DEPTH, D_MODEL, IN_PROJ), D_MODEL ** -0.5),
        "conv_w": normal(ks[7], (DEPTH, CONV_K_2, CONV_DIM), CONV_K_2 ** -0.5),
        "conv_b": normal(ks[8], (DEPTH, CONV_DIM), 0.02),
        "dt_bias": dt + jnp.log(-jnp.expm1(-dt)),
        "a_log": jnp.log(jax.random.uniform(ks[11], (DEPTH, SSD_HEADS), f, 1.0, 16.0)),
        "d_skip": gain(ks[12], (DEPTH, SSD_HEADS)),
        "ssd_norm": gain(ks[13], (DEPTH, SSD_WIDTH)),
        "q_norm": gain(ks[14], (DEPTH, ATT_HEAD_DIM)),
        "k_norm": gain(ks[15], (DEPTH, ATT_HEAD_DIM)),
        "w_out": normal(ks[16], (DEPTH, MIX_WIDTH, D_MODEL), MIX_WIDTH ** -0.5),
        "ffn2_norm": gain(ks[17], (DEPTH, D_MODEL)),
        "ffn2_w_gate": normal(ks[18], (DEPTH, D_MODEL, D_FF), D_MODEL ** -0.5),
        "ffn2_w_up": normal(ks[19], (DEPTH, D_MODEL, D_FF), D_MODEL ** -0.5),
        "ffn2_w_down": normal(ks[20], (DEPTH, D_FF, D_MODEL), D_FF ** -0.5),
    }

def second_block(x, ffn1_norm, ffn1_w_gate, ffn1_w_up, ffn1_w_down, mix_norm, w_in,
              conv_w, conv_b, dt_bias, a_log, d_skip, ssd_norm, q_norm, k_norm,
              w_out, ffn2_norm, ffn2_w_gate, ffn2_w_up, ffn2_w_down):
    b, s, _ = x.shape
    splits = np.cumsum([SSD_WIDTH, CONV_DIM, SSD_HEADS, ATT_WIDTH, ATT_WIDTH]).tolist()
    for i in range(DEPTH):
        x = x + 0.5 * swiglu(rms_norm_2(x, ffn1_norm[i]), ffn1_w_gate[i], ffn1_w_up[i], ffn1_w_down[i])
        h = rms_norm_2(x, mix_norm[i])
        proj = h @ w_in[i]
        z, xbc, dt_raw, q, k, v = jnp.split(proj, splits, axis=-1)
        xbc = jax.nn.silu(causal_depthwise_conv(xbc, conv_w[i], conv_b[i]))
        y_ssd = ssd_mixer(xbc, dt_raw, z, dt_bias[i], a_log[i], d_skip[i], ssd_norm[i])
        q = rms_norm_2(q.reshape(b, s, ATT_HEADS, ATT_HEAD_DIM), q_norm[i])
        k = rms_norm_2(k.reshape(b, s, ATT_HEADS, ATT_HEAD_DIM), k_norm[i])
        v = v.reshape(b, s, ATT_HEADS, ATT_HEAD_DIM)
        y_att = dilated_attention(q, k, v).reshape(b, s, ATT_WIDTH)
        x = x + jnp.concatenate([y_ssd, y_att], axis=-1) @ w_out[i]
        x = x + 0.5 * swiglu(rms_norm_2(x, ffn2_norm[i]), ffn2_w_gate[i], ffn2_w_up[i], ffn2_w_down[i])
    return x


def setup_inputs(seed=0):
    out = dict(first_inputs(seed))
    for name, value in second_inputs(seed + 1).items():
        if name != "x":
            out[name + "_2"] = value
    return out


def reference(
    x, c, ada_w, ada_b, norm_g, even_w_in, even_b_f, even_conv_w, even_q_g, even_k_g,
    even_w_out, odd_w_in, odd_b_gate, odd_q_g, odd_k_g, odd_cmp_pos, odd_cmp_w1, odd_cmp_w2,
    odd_w_out, rel_table, peer_w_q, peer_keys, peer_u, peer_v, ffn1_norm_2, ffn1_w_gate_2,
    ffn1_w_up_2, ffn1_w_down_2, mix_norm_2, w_in_2, conv_w_2, conv_b_2, dt_bias_2, a_log_2,
    d_skip_2, ssd_norm_2, q_norm_2, k_norm_2, w_out_2, ffn2_norm_2, ffn2_w_gate_2, ffn2_w_up_2,
    ffn2_w_down_2,
):
    x = first_block(
        x, c, ada_w, ada_b, norm_g, even_w_in, even_b_f, even_conv_w, even_q_g, even_k_g,
        even_w_out, odd_w_in, odd_b_gate, odd_q_g, odd_k_g, odd_cmp_pos, odd_cmp_w1, odd_cmp_w2,
        odd_w_out, rel_table, peer_w_q, peer_keys, peer_u, peer_v,
    )
    return second_block(
        x, ffn1_norm_2, ffn1_w_gate_2, ffn1_w_up_2, ffn1_w_down_2, mix_norm_2, w_in_2, conv_w_2,
        conv_b_2, dt_bias_2, a_log_2, d_skip_2, ssd_norm_2, q_norm_2, k_norm_2, w_out_2,
        ffn2_norm_2, ffn2_w_gate_2, ffn2_w_up_2, ffn2_w_down_2,
    )


_drawn_inputs = setup_inputs


def setup_inputs(seed=0):
    import zlib

    import numpy as np

    out = dict(_drawn_inputs(seed))
    spreads = {}
    factors = {'even_q_g': 7.801,
     'even_k_g': 7.219,
     'odd_b_gate': 8.0,
     'odd_q_g': 8.0,
     'odd_k_g': 8.0,
     'odd_cmp_pos': 3.285,
     'ffn1_norm_2': 4.248,
     'd_skip_2': 110.36,
     'ssd_norm_2': 14.15,
     'q_norm_2': 23.1,
     'k_norm_2': 101.307,
     'ffn2_norm_2': 6.113,
     'conv_b_2': 3.493,
     'dt_bias_2': 2.946,
     'a_log_2': 3.393}
    for name, (base, spread) in spreads.items():
        noise = np.random.default_rng([zlib.crc32(name.encode()), seed]).standard_normal(out[name].shape)
        drawn = base * np.exp(spread * noise) if base else spread * noise
        out[name] = jnp.asarray(drawn.astype(out[name].dtype))
    for name, factor in factors.items():
        out[name] = (out[name] * factor).astype(out[name].dtype)
    return out
```

```python
import numpy as np
import concourse.bass as bass
from concourse import mybir
from contextlib import ExitStack

F32 = mybir.dt.float32
U32 = mybir.dt.uint32
ALU = mybir.AluOpType
ACT = mybir.ActivationFunctionType
AX = mybir.AxisListType

EPS = 1e-6
NEG = -1e30
NR = 8
STAGES = ("mix0", "peer0", "mix1", "peer1", "ffnA0", "ssd0", "ffnB0", "ffnA1", "ssd1", "ffnB1")


def shape_constants():
    p = np.arange(128)
    f = np.float32
    c = {}
    c["ident"] = np.eye(128, dtype=f)
    c["ones"] = np.ones((128, 128), f)
    c["bd64"] = (p[:, None] // 64 == p[None, :] // 64).astype(f)
    c["le"] = (p[:, None] <= p[None, :]).astype(f)
    c["gt"] = (p[:, None] > p[None, :]).astype(f)
    c["iota"] = np.broadcast_to(p.astype(f), (128, 128)).copy()
    dist = np.concatenate([p[:, None] - p[None, :], 128 + p[:, None] - np.arange(256)[None, :]], 1)
    c["causal"] = np.where(dist >= 0, 0.0, NEG).astype(f)
    mult = ((dist >= 0) & (dist <= 128)).astype(f) + ((dist >= 0) & (dist % 4 == 0)) + ((dist >= 0) & (dist % 16 == 0))
    c["dilmask"] = np.where(mult > 0, 0.0, NEG).astype(f)
    c["dilmult"] = mult.astype(f)
    t = np.arange(256)
    ends = np.arange(15) * 16 + 31
    ok = (ends[None, :] <= t[:, None]).reshape(2, 128, 15).transpose(1, 0, 2)
    ok = np.repeat(ok[:, :, None, :], 4, 2).reshape(128, 120)
    c["cmpok"] = ok.astype(f)
    c["cmpneg"] = np.where(ok, 0.0, NEG).astype(f)
    sel = np.zeros((128, 8), f)
    for h in range(8):
        sel[h::32, h] = 1
    c["headsel"] = sel
    c["rowsel"] = (p[:, None] // 32 == np.arange(4)[None, :]).astype(f)
    c["neghalf"] = np.full((128, 1), -0.5, f)
    return c


def rel_buckets(dist):
    n = np.maximum(dist, 0)
    nf = np.maximum(n, 1).astype(np.float32)
    large = 16 + (np.log(nf / np.float32(16)) / np.float32(np.log(8.0)) * np.float32(16)).astype(np.int32)
    return np.where(n < 16, n, np.minimum(large, 31))


def columns(v):
    return v.reshape(-1, 128).T


def packed(i):
    c = shape_constants()
    f = np.float32

    def rows(v, at=0):
        z = np.zeros((128, v.shape[1] if v.ndim > 1 else 1), f)
        z[at:at + v.shape[0]] = v.reshape(v.shape[0], -1)
        return z

    c["c"] = columns(i["c"][0])
    c["normg"] = columns(i["norm_g"])
    c["foxqg"] = np.tile(i["even_q_g"][0], 2)[:, None]
    c["foxkg"] = np.tile(i["even_k_g"][0], 2)[:, None]
    c["convw"] = i["even_conv_w"][0].reshape(3, 4, 128).transpose(2, 1, 0).reshape(128, 12)
    bf = np.zeros((128, 1), f)
    for q in range(4):
        bf[32 * q:32 * q + 8, 0] = i["even_b_f"][0]
    c["bf"] = bf
    c["nsaqg"] = np.tile(i["odd_q_g"][0], 2)[:, None]
    c["nsakg"] = np.tile(i["odd_k_g"][0], (1, 2)).T
    c["bgate"] = rows(i["odd_b_gate"][0][:, None])
    c["pos"] = i["odd_cmp_pos"][0].reshape(2, 16, 2, 64).transpose(2, 3, 0, 1).reshape(128, 32)
    c["w2k"] = rows(np.tile(i["odd_cmp_w2"][0, 0], (1, 2)))
    c["w2v"] = rows(i["odd_cmp_w2"][0, 1])
    for l in range(2):
        k = np.zeros((2, 64, 2, 128), f)
        for p in range(2):
            k[p, :, p, :] = i["peer_keys"][l, p].T
        c[f"keys{l}"] = k.reshape(128, 256)
        c[f"fn1_{l}"] = columns(i["ffn1_norm_2"][l])
        c[f"fn2_{l}"] = columns(i["ffn2_norm_2"][l])
        c[f"mixn_{l}"] = columns(i["mix_norm_2"][l])
        c[f"ssdn_{l}"] = columns(i["ssd_norm_2"][l])
        c[f"dqg_{l}"] = np.tile(i["q_norm_2"][l], 2)[:, None]
        c[f"dkg_{l}"] = np.tile(i["k_norm_2"][l], 2)[:, None]
        c[f"cw_{l}"] = i["conv_w_2"][l].reshape(4, 16, 128).transpose(2, 1, 0).reshape(128, 64)
        c[f"cb_{l}"] = columns(i["conv_b_2"][l])
        c[f"dtb_{l}"] = rows(i["dt_bias_2"][l][:, None])
        c[f"alog_{l}"] = rows(i["a_log_2"][l][:, None])
        c[f"dsk_{l}"] = np.broadcast_to(i["d_skip_2"][l], (128, 16)).copy()
    return c


def stationary(w):
    n = -(-w.shape[1] // 128)
    if n * 128 != w.shape[1]:
        w = np.concatenate([w, np.zeros((w.shape[0], n * 128 - w.shape[1]), w.dtype)], 1)
    return w.reshape(8, 128, n, 128).transpose(2, 1, 0, 3).reshape(n, 128, 1024)


def moving(w):
    return w.reshape(-1, 128, 1024)


def moving512(w):
    return w.reshape(4, 2, 128, 512).transpose(0, 2, 1, 3).reshape(4, 128, 1024)


def lay_out(i):
    i = {k: np.asarray(v) for k, v in i.items()}
    a = {}
    pk = packed(i)
    a["pack"] = np.concatenate(list(pk.values()), 1)
    a["x"] = i["x"][0].reshape(2, 128, 1024)
    a["ada"] = i["ada_w"].reshape(2, 8, 128, 6, 1024).transpose(0, 3, 1, 2, 4).reshape(96, 128, 1024)
    a["adab"] = i["ada_b"].reshape(12, 1, 1024)
    w = i["even_w_in"][0]
    st = stationary(w[:, :2560])
    a["foxst"] = np.concatenate([st[[4 + j, 8 + j, j]] for j in range(4)] + [st[12:20]])
    wf = np.zeros((1024, 128), np.float32)
    for q in range(4):
        wf[:, 32 * q:32 * q + 8] = w[:, 3072:3080]
    a["foxf"] = stationary(wf)
    a["foxv"] = moving512(w[:, 2560:3072])
    a["foxo"] = moving(i["even_w_out"][0])
    w = i["odd_w_in"][0]
    a["nsaq"] = stationary(w[:, :1024])
    kv = w[:, 1024:1536].reshape(1024, 8, 1, 64)
    a["nsac"] = stationary(np.tile(kv, (1, 1, 2, 1)).reshape(1024, 1024))
    a["nsak"] = stationary(np.concatenate([w[:, 1536:1792], w[:, 2048:2304]], 1))
    a["nsav"] = moving512(np.concatenate([w[:, 1792:2048], w[:, 2304:2560]], 1))
    a["nsag"] = stationary(w[:, 2560:2608])
    a["nsaw1"] = i["odd_cmp_w1"][0].reshape(2, 16, 128, 64).transpose(0, 2, 1, 3).reshape(2, 128, 1024)
    a["nsao"] = moving(i["odd_w_out"][0])
    p = np.arange(128)
    dist = np.concatenate([p[:, None] - p[None, :], 128 + p[:, None] - np.arange(256)[None, :]], 1)
    tab = i["rel_table"]
    a["toep"] = tab[rel_buckets(dist)].transpose(0, 2, 1).reshape(128, 16 * 384)
    t = np.arange(256)
    ends = np.arange(15) * 16 + 31
    cb = tab[rel_buckets(t[:, None] - ends[None, :])].reshape(2, 128, 15, 4, 4)
    a["cmpb"] = cb.transpose(1, 3, 0, 4, 2).reshape(128, 480)
    for l in range(2):
        a[f"pq{l}"] = stationary(i["peer_w_q"][l])
        a[f"pu{l}"] = i["peer_u"][l].reshape(128, 128, 8, 128).transpose(1, 3, 2, 0).reshape(128, 128, 1024)
        a[f"pv{l}"] = i["peer_v"][l].reshape(128, 128, 1024).transpose(1, 0, 2)
        for n, s in (("A", "1"), ("B", "2")):
            a[f"fg{n}{l}"] = stationary(i[f"ffn{s}_w_gate_2"][l])
            a[f"fu{n}{l}"] = stationary(i[f"ffn{s}_w_up_2"][l])
            a[f"fd{n}{l}"] = moving(i[f"ffn{s}_w_down_2"][l])
        w = i["w_in_2"][l]
        a[f"sz{l}"] = moving(w[:, :1024])
        a[f"sx{l}"] = stationary(w[:, 1024:3072])
        a[f"sd{l}"] = stationary(w[:, 3072:3088])
        a[f"sqk{l}"] = stationary(w[:, 3088:5136])
        a[f"sv{l}"] = moving(w[:, 5136:6160])
        a[f"so{l}"] = moving(i["w_out_2"][l])
    return {k: np.ascontiguousarray(v, dtype=np.float32) for k, v in a.items()}


def pack_places():
    z = {"c": (1, 1024), "norm_g": (2, 2, 1024), "even_q_g": (1, 64), "even_k_g": (1, 64), "even_conv_w": (1, 3, 512),
         "even_b_f": (1, 8), "odd_q_g": (1, 64), "odd_k_g": (1, 3, 64), "odd_b_gate": (1, 48),
         "odd_cmp_pos": (1, 2, 32, 64), "odd_cmp_w2": (1, 2, 64, 64), "peer_keys": (2, 2, 128, 64),
         "ffn1_norm_2": (2, 1024), "ffn2_norm_2": (2, 1024), "mix_norm_2": (2, 1024), "ssd_norm_2": (2, 1024),
         "q_norm_2": (2, 64), "k_norm_2": (2, 64), "conv_w_2": (2, 4, 2048), "conv_b_2": (2, 2048),
         "dt_bias_2": (2, 16), "a_log_2": (2, 16), "d_skip_2": (2, 16)}
    pk = packed({k: np.zeros(s, np.float32) for k, s in z.items()})
    at, out = 0, {}
    for k, v in pk.items():
        out[k] = (at, v.shape[1])
        at += v.shape[1]
    return out, at


class Counter:

    def __init__(self, new_sem, name):
        self.new_sem, self.name, self.sem, self.n, self.k = new_sem, name, None, 0, 0

    def step(self):
        if self.sem is None or self.n >= 16000:
            self.sem, self.n, self.k = self.new_sem(f"{self.name}{self.k}"), 0, self.k + 1
        self.n += 1
        return (self.sem, self.n)

    def last(self):
        return (self.sem, self.n) if self.sem is not None else None


class Queue:

    def __init__(self, new_sem, name):
        self.ops, self.count, self.done, self.pending = [], Counter(new_sem, name), {}, []

    def wait(self, marks):
        for m in marks:
            if m is None:
                continue
            if isinstance(m, list):
                self.wait(m)
                continue
            sem, n = m
            if self.done.get(id(sem), 0) < n:
                self.done[id(sem)] = n
                self.ops.append(("wait", sem, n))

    def put(self, fn, waits, inc=True):
        self.wait(self.pending)
        self.pending = []
        self.wait(waits)
        mark = self.count.step() if inc else None
        self.ops.append(("do", fn, mark[0] if inc else None))
        return mark

    def dma(self, fn, waits, sem):
        self.wait(self.pending)
        self.pending = []
        self.wait(waits)
        self.ops.append(("dma", fn, sem))

    def emit(self, eng):
        for kind, a, b in self.ops:
            if kind == "wait":
                eng.wait_ge(a, b)
            elif kind == "do":
                ins = a(eng)
                if b is not None:
                    ins.then_inc(b, 1)
            else:
                a(eng).then_inc(b, 16)


def build(nc, ins, out, stages=STAGES):
    places, NPACK = pack_places()
    ctx = ExitStack()
    with ctx:
        def sb(name, cols, dt=F32):
            return ctx.enter_context(nc.sbuf_tensor(name, [128, cols], dt))

        def new_sem(name):
            return ctx.enter_context(nc.semaphore("s_" + name))

        Xt = sb("X", 2048)
        HTt = sb("HT", 2048)
        RINGt = sb("RING", NR * 1024)
        ACCt = sb("ACC", 1024)
        GBt = sb("GB", 1024)
        ARt = sb("AR", 32768)
        CSTt = sb("CST", NPACK)
        STATt = sb("STAT", 256)
        MODt = sb("MOD", 80)
        TIJt = sb("TIJ", 768)
        WTt = sb("WT", 1024)
        OHt = sb("OH", 512)
        X = Xt[:, :].rearrange("p (t n) -> p t n", t=2)
        HT = HTt[:, :].rearrange("p (k t) -> p k t", k=8)
        STAT, MOD = STATt[:, :], MODt[:, :]
        banks = [ctx.enter_context(nc.psum_tensor(f"P{n}", [128, 512], F32)) for n in range(8)]
        Y = [b[:, :] for b in banks[:4]]

        PE, DVE, SC, PO, SP = (Queue(new_sem, n) for n in ("pe", "dve", "act", "pool", "sp"))

        def C(name, a=0, b=None):
            at, n = places[name]
            return CSTt[:, at + a:at + (n if b is None else b)]

        def NH(n):
            at = places["neghalf"][0]
            return CSTt[:, at:at + 1].broadcast_to([128, n])

        def A(off, n):
            return ARt[:, off:off + n]

        def mm(o, l, r, start, stop, w=(), inc=None):
            return PE.put(lambda e: e.matmul(o, l, r, start=start, stop=stop), w, stop if inc is None else inc)

        def tp(o, i, w=(), n=128, inc=True):
            idt = C("ident")[0:n, 0:n]
            return PE.put(lambda e: e.transpose(o, i, idt), w, inc)

        def tt(o, a, b, op, w=(), q=None):
            return (q or DVE).put(lambda e: e.tensor_tensor(o, a, b, op), w)

        def ts(o, a, s1, s2, op0, op1=None, w=(), q=None):
            if op1 is None:
                return (q or DVE).put(lambda e: e.tensor_scalar(o, a, s1, None, op0), w)
            return (q or DVE).put(lambda e: e.tensor_scalar(o, a, s1, s2, op0, op1), w)

        def stt(o, a, s, b, op0, op1, w=()):
            return DVE.put(lambda e: e.scalar_tensor_tensor(out=o, in0=a, scalar=s, in1=b, op0=op0, op1=op1), w)

        def copy(o, a, w=(), q=None):
            return (q or DVE).put(lambda e: e.tensor_copy(o, a), w)

        def red(o, a, op, w=(), neg=False):
            return DVE.put(lambda e: e.tensor_reduce(o, a, AX.X, op, negate=neg), w)

        def rec(o, a, w=()):
            return DVE.put(lambda e: e.reciprocal(o, a), w)

        def mset(o, v, w=(), q=None):
            return (q or DVE).put(lambda e: e.memset(o, v), w)

        def act(o, a, f, w=(), bias=0.0, scale=1.0, acc=None):
            if f == ACT.Copy:
                return SC.put(lambda e: e.activation(o, a, f, scale=scale), w)
            if acc is not None:
                return SC.put(lambda e: e.activation(o, a, f, bias=bias, scale=scale, accum_out=acc), w)
            return SC.put(lambda e: e.activation(o, a, f, bias=bias, scale=scale), w)

        def load(o, i, w=(), sem=None):
            s = sem or new_sem(f"ld{len(loads)}")
            loads.append(s)
            SC.dma(lambda e: e.dma_start(o, i), w, s)
            return (s, 16)

        loads = []

        def fence():
            marks = [q.count.last() for q in (PE, DVE, SC, PO)]
            for q in (PE, DVE, SC, PO):
                q.pending = list(marks)

        stream = []
        ring_sem = [new_sem(f"ring{n}") for n in range(NR)]

        def take(name, idx):
            n = len(stream)
            stream.append([ins[name][idx], None])
            return RINGt[:, (n % NR) * 1024:(n % NR + 1) * 1024], (ring_sem[n % NR], 16 * (n // NR + 1)), n

        def give(n, mark):
            stream[n][1] = mark

        free = [None] * 8
        turn = [0]

        def bank():
            n = 4 + turn[0] % 4
            turn[0] += 1
            return n, banks[n][:, :], free[n]

        sturn = [0]

        def stat(n):
            if sturn[0] + n > 256:
                sturn[0] = 0
            a = STAT[:, sturn[0]:sturn[0] + n]
            sturn[0] += n
            return a

        SP_c = new_sem("pack")
        SP.dma(lambda e: e.dma_start(CSTt[:, :], ins["pack"]), (), SP_c)
        m_pack = (SP_c, 16)
        s_x = new_sem("x")
        for t in range(2):
            SC.dma(lambda e, t=t: e.dma_start(X[:, t, :], ins["x"][t]), (), s_x)
        for q in (PE, DVE, SC, PO):
            q.pending = [m_pack]
        m_x = [(s_x, 32)] * 2

        sc_m = [None]
        silu_c = MOD[:, 64:72]
        acc_free = [None]
        s_ab = new_sem("ab")
        n_ab = [0]
        mod_done = {}
        bg = []

        def ada_piece(p):
            state = {}

            def first():
                m = mset(ACCt[:, :], 0.0, [acc_free[0]], q=PO)
                n_ab[0] += 1
                SC.dma(lambda e: e.dma_start(ACCt[0:1, :], ins["adab"][p]), [m], s_ab)
                state["m"] = (s_ab, 16 * n_ab[0])

            def slot(k):
                def run():
                    w, m, n = take("ada", p * 8 + k)
                    state["m"] = stt(ACCt[:, :], w, silu_c[:, k:k + 1], ACCt[:, :], ALU.mult, ALU.add,
                                     [m, state["m"], sc_m[0]])
                    give(n, state["m"])
                return run

            def last():
                l, kind = divmod(p, 6)
                n, ps, fr = bank()
                if kind in (2, 5):
                    for hf in range(2):
                        if hf:
                            n, ps, fr = bank()
                        m = mm(ps, C("ones"), ACCt[:, hf * 512:hf * 512 + 512], True, True, [fr, state["m"]])
                        acc_free[0] = m
                        free[n] = act(GBt[:, hf * 512:hf * 512 + 512], ps, ACT.Copy, [m, gb_free[0]])
                    mod_done[p] = free[n]
                    return
                for k in range(8):
                    m = mm(ps[:, k:k + 1], ACCt[:, k * 128:k * 128 + 128], C("ones")[:, 0:1], True, True,
                           [fr, state["m"]])
                acc_free[0] = m
                half = kind // 3
                place = MOD[:, 16 * (2 * (l % 2) + half):][:, 0:16]
                if kind % 3 == 0:
                    mod_done[p] = free[n] = copy(place[:, 8:16], ps[:, 0:8], [m])
                else:
                    g = C("normg", (l * 2 + half) * 8, (l * 2 + half) * 8 + 8)
                    mod_done[p] = free[n] = stt(place[:, 0:8], ps[:, 0:8], 1.0, g, ALU.add, ALU.mult, [m])

            return [first] + [slot(k) for k in range(8)] + [last]

        gb_free = [None]

        def background(n=1):
            for _ in range(n):
                if bg:
                    bg.pop(0)()

        XN = 30720

        def make_h(scale, shift, w):
            sts = stat(2)
            xn = A(XN, 2048).rearrange("p (t n) -> p t n", t=2)
            for t in range(2):
                m = act(xn[:, t, :], X[:, t, :], ACT.Square, [m_x[t], w], acc=sts[:, t:t + 1])
            m = ts(sts, sts, 1.0 / 1024, EPS, ALU.mult, ALU.add, [m], q=PO)
            r = stat(2)
            m = tt(r, sts, NH(2), ALU.pow, [m], q=PO)
            mt = [act(xn[:, 0, :], X[:, 0, :], ACT.Copy, [m], scale=r[:, 0:1]),
                  ts(xn[:, 1, :], X[:, 1, :], r[:, 1:2], None, ALU.mult, w=[m])]
            for k2 in range(4):
                n, ps, fr = bank()
                for kk in range(2):
                    k = 2 * k2 + kk
                    for t in range(2):
                        m = tp(ps[:, kk * 256 + t * 128:][:, 0:128], xn[:, t, k * 128:k * 128 + 128], [fr, mt[t]])
                for kk in range(2):
                    k = 2 * k2 + kk
                    src, dst = ps[:, kk * 256:kk * 256 + 256], HT[:, k, :]
                    if k2 % 2 and shift is None:
                        a = act(dst, src, ACT.Copy, [m, w], scale=scale[:, k:k + 1])
                    elif k2 % 2:
                        a = act(dst, src, ACT.Identity, [m, w], scale=scale[:, k:k + 1], bias=shift[:, k:k + 1])
                    elif shift is None:
                        b = ts(dst, src, scale[:, k:k + 1], None, ALU.mult, w=[m, w])
                    else:
                        b = ts(dst, src, scale[:, k:k + 1], shift[:, k:k + 1], ALU.mult, ALU.add, w=[m, w])
                free[n] = a if k2 % 2 else b
            return [a, b]

        def project(name, idx, mh):
            w, m, s = take(name, idx)
            n, ps, fr = bank()
            for k in range(8):
                mk = mm(ps[:, 0:256], w[:, k * 128:k * 128 + 128], HT[:, k, :], k == 0, k == 7, [fr, m, mh])
            give(s, mk)
            return n, ps[:, 0:256], mk

        def rows_out(name, nslots, lhs, w, yfree):
            for k in range(nslots):
                wt, m, s = take(name, k)
                for t in range(2):
                    for hf in range(2):
                        mk = mm(Y[2 * t + hf], lhs(k, t), wt[:, hf * 512:hf * 512 + 512], k == 0, k == nslots - 1,
                                [m, w(k)] + ([free[2 * t + hf]] if k == 0 else []), inc=True)
                give(s, mk)
                background()
            return mk

        def rows512(name, w):
            for s4 in range(4):
                wt, m, s = take(name, s4)
                for kk in range(2):
                    for t in range(2):
                        k = 2 * s4 + kk
                        mk = mm(Y[t], HT[:, k, t * 128:t * 128 + 128], wt[:, kk * 512:kk * 512 + 512], k == 0, k == 7,
                                [m, w, free[t]], inc=True)
                give(s, mk)
            return mk

        later = []

        def run_later(keep=0):
            while len(later) > keep:
                later.pop(0)()

        def head_norm(n, ps, m, dst, gcol, sq, rr, marks, key, w=None):
            a = act(dst, ps, ACT.Copy, [m, w])
            b = act(sq, ps, ACT.Square, [m, w, sq_free.get(id(sq))])
            free[n] = b

            def rest():
                n2, p2, fr = bank()
                mk = mm(p2[:, 0:256], C("bd64"), sq, True, True, [fr, b])
                sq_free[id(sq)] = mk
                c = ts(rr, p2[:, 0:256], 1.0 / 64, EPS, ALU.mult, ALU.add, w=[mk, rr_free.get(id(rr))])
                free[n2] = c
                d = rec(rr, rr, [act(rr, rr, ACT.Sqrt, [c])])
                marks[key] = stt(dst, dst, gcol, rr, ALU.mult, ALU.mult, [d, a])
                rr_free[id(rr)] = marks[key]
            later.append(rest)

        sq_free, rr_free = {}, {}

        def log1p_exp(o, x, t1, t2, t3, w):
            m = act(t1, x, ACT.Abs, w)
            m = act(t1, t1, ACT.Exp, [m], scale=-1.0)
            m = ts(t2, t1, 2.0, None, ALU.add, w=[m])
            m = rec(t2, t2, [m])
            m = tt(t1, t1, t2, ALU.mult, [m])
            m = tt(t2, t1, t1, ALU.mult, [m])
            m = ts(t3, t2, 2.0 / 17, 2.0 / 15, ALU.mult, ALU.add, w=[m])
            for c in (13, 11, 9, 7, 5, 3, 1):
                m = tt(t3, t3, t2, ALU.mult, [m])
                m = ts(t3, t3, 2.0 / c, None, ALU.add, w=[m])
            return tt(o, t3, t1, ALU.mult, [m])

        class Heads:
            def __init__(self, base, nb=3):
                self.S = [A(base + n * 384, 384) for n in range(nb)]
                self.P = [A(base + (nb + n) * 384, 384) for n in range(nb)]
                self.sf, self.pf, self.nb, self.i = [None] * nb, [None] * nb, nb, 0
                self.q = []

            def add(self, scores, mask, v, dst, gate=None, mult=None, wmask=None):
                r = self.i % self.nb
                self.i += 1
                S, P = self.S[r], self.P[r]
                n, ps, fr = bank()
                m = scores(ps, fr)
                st = stat(6)
                m = tt(S, ps[:, 0:384], mask, ALU.add, [m, self.sf[r], wmask])
                free[n] = m
                red(st[:, 0:1], S[:, 0:128], ALU.max, [m], neg=True)
                m = red(st[:, 1:2], S[:, 128:384], ALU.max, [m], neg=True)
                for i, (a, b) in enumerate(((0, 128), (128, 384))):
                    m2 = act(S[:, a:b], S[:, a:b], ACT.Exp, [m], bias=st[:, i:i + 1],
                             acc=None if mult is not None else st[:, 2 + i:3 + i])
                m = m2
                if mult is not None:
                    for i, (a, b) in enumerate(((0, 128), (128, 384))):
                        o, c, u = S[:, a:b], mult[:, a:b], st[:, 2 + i:3 + i]
                        m = DVE.put(lambda e, o=o, c=c, u=u: e.tensor_tensor_reduce(
                            o, o, c, 1.0, 0.0, ALU.mult, ALU.add, u), [m2])
                m = rec(st[:, 4:6], st[:, 2:4], [m])
                if gate is not None:
                    m = tt(st[:, 4:6], st[:, 4:6], gate[0], ALU.mult, [m, gate[1]])
                ts(S[:, 0:128], S[:, 0:128], st[:, 4:5], None, ALU.mult, w=[m], q=PO)
                m = ts(S[:, 128:384], S[:, 128:384], st[:, 5:6], None, ALU.mult, w=[m], q=PO)
                self.q.append([0, r, S, P, m, v, dst])
                self.step()

            def step(self, flush=False):
                while self.q and self.q[0][0] == 1 and (flush or len(self.q) > 2):
                    self.pv(self.q.pop(0))
                for e in self.q:
                    if e[0] == 0 and (flush or e is not self.q[-1]):
                        self.turn(e)
                if flush:
                    while self.q:
                        self.pv(self.q.pop(0))

            def turn(self, e):
                _, r, S, P, m, v, dst = e
                n, ps, fr = bank()
                for c in range(3):
                    mk = tp(ps[:, c * 128:c * 128 + 128], S[:, c * 128:c * 128 + 128], [fr, m])
                self.sf[r] = mk
                e[4] = act(P, ps[:, 0:384], ACT.Copy, [mk, self.pf[r]])
                free[n] = e[4]
                e[0] = 1

            def pv(self, e):
                _, r, S, P, m, v, dst = e
                o, w, first, last, after = dst
                mm(o, v(0), P[:, 0:256], first, False, [m, w], inc=False)
                mk = mm(o[:, 128:256], v(1), P[:, 256:384], False, last, [m], inc=True)
                self.pf[r] = mk
                if after is not None:
                    after(mk)

        def residual(scale, gated, wy, w=None):
            for t in range(2):
                for hf in range(2):
                    x = X[:, t, hf * 512:hf * 512 + 512]
                    y = Y[2 * t + hf]
                    if gated:
                        tmp = A(XN + (2 * t + hf) * 512, 512)
                        m = tt(tmp, y, GBt[:, hf * 512:hf * 512 + 512], ALU.mult, [wy, w])
                        free[2 * t + hf] = m
                        m = tt(x, x, tmp, ALU.add, [m, m_x[t]])
                    else:
                        m = stt(x, y, scale, x, ALU.mult, ALU.add, [wy, m_x[t]])
                        free[2 * t + hf] = m
                m_x[t] = m
            if gated:
                gb_free[0] = m

        def fox():
            mods = MOD[:, 0:16]
            mh = make_h(mods[:, 0:8], mods[:, 8:16], [mod_done[0], mod_done[1]])
            CAT = A(0, 2048).rearrange("p (c t) -> p c t", c=8)
            QT = A(2048, 1024).rearrange("p (c t) -> p c t", c=4)
            KT = A(3072, 1024).rearrange("p (c t) -> p c t", c=4)
            V = A(4096, 1024).rearrange("p (b n) -> p b n", b=2)
            U = [A(5120 + 258 * n, 258) for n in range(2)]
            CC = [A(5640 + 256 * n, 256) for n in range(2)]
            T0 = [A(6152 + 256 * n, 256) for n in range(2)]
            SQ = [A(6664 + 256 * n, 256) for n in range(2)]
            RR = [A(7176 + 256 * n, 256) for n in range(2)]
            FL, FR = A(7688, 256), A(7944, 256)
            RH = [A(8200 + 256 * n, 256) for n in range(2)]
            F = [A(8712 + 256 * n, 256) for n in range(4)]
            cat, qk = {}, {}
            ms = [mset(U[n][:, 0:2], 0.0) for n in range(2)]
            gq = stat(1)
            mg = ts(gq, C("foxqg"), 0.125, None, ALU.mult)
            for j in range(4):
                b = j % 2
                n, ps, m = project("foxst", 3 * j, mh)
                mc = free[n] = act(CC[b], ps, ACT.Copy, [m, cat.get(j - 2)])
                n, ps, m = project("foxst", 3 * j + 1, mh)
                mu = free[n] = tt(U[b][:, 2:258], ps, CC[b], ALU.mult, [m, mc, ms[b], cat.get(j - 2)])
                cw = C("convw", 3 * j, 3 * j + 3)
                m1 = ts(T0[b], U[b][:, 0:256], cw[:, 0:1], None, ALU.mult, w=[mu, cat.get(j - 2)])
                m1 = stt(T0[b], U[b][:, 1:257], cw[:, 1:2], T0[b], ALU.mult, ALU.add, [m1])
                m1 = stt(T0[b], U[b][:, 2:258], cw[:, 2:3], T0[b], ALU.mult, ALU.add, [m1])
                n, ps, m = project("foxst", 3 * j + 2, mh)
                cat[j] = free[n] = tt(CAT[:, j, :], ps, T0[b], ALU.mult, [m, m1])
                background()
            for j in range(8):
                n, ps, m = project("foxst", 12 + j, mh)
                run_later()
                dst = QT[:, j, :] if j < 4 else KT[:, j - 4, :]
                head_norm(n, ps, m, dst, gq if j < 4 else C("foxkg"), SQ[j % 2], RR[j % 2], qk, j, [mg])
                background(2)
            n, ps, m = project("foxf", 0, mh)
            run_later()
            m = free[n] = ts(F[0], ps, C("bf"), None, ALU.add, w=[m])
            m = log1p_exp(F[1], F[0], F[2], F[3], FR, [m])
            m = stt(F[1], F[0], 0.0, F[1], ALU.min, ALU.subtract, [m])
            m2 = mset(F[3], 1.0, [m])
            m = DVE.put(lambda e: e.tensor_tensor_scan(F[2], F[3], F[1], 0.0, ALU.mult, ALU.add), [m, m2])
            mF = []
            for q in (0, 64):
                mF.append(copy(FL[q:q + 32, :], F[2][q:q + 32, :], [m]))
                mF.append(mset(FL[q + 32:q + 64, :], 1.0))
                mF.append(mset(FR[q:q + 32, :], 1.0, [m]))
                mF.append(ts(FR[q + 32:q + 64, :], F[2][q + 32:q + 64, :], -1.0, None, ALU.mult, w=[m]))
            m = rows512("foxv", mh)
            mv = []
            for t in range(2):
                mk = act(V[:, t, :], Y[t], ACT.Copy, [m])
                free[t] = mk
                mv.append(mk)
            H = Heads(10000)
            rh_free = [None, None]
            for h in range(8):
                pr = slice(64 * (h % 2), 64 * (h % 2) + 64)
                r = RH[h % 2][pr, :]
                mr = ts(r, FR[pr, :], C("headsel")[pr, h:h + 1], None, ALU.mult, w=[mF, rh_free[h % 2]])

                def scores(ps, fr, h=h, pr=pr, r=r, mr=mr):
                    w = [fr, qk[h // 2], qk[4 + h // 2]]
                    mm(ps[:, 0:128], QT[pr, h // 2, 0:128], KT[pr, h // 2, 0:128], True, False, w, inc=False)
                    mm(ps[:, 0:128], FL[pr, 0:128], r[:, 0:128], False, True, [mr, mF], inc=False)
                    mm(ps[:, 128:384], QT[pr, h // 2, 128:256], KT[pr, h // 2, :], True, False, inc=False)
                    m = mm(ps[:, 128:384], FL[pr, 128:256], r, False, True)
                    rh_free[h % 2] = m
                    return m

                yb = (h // 2) % 4
                after = None
                if h % 2:
                    def after(mk, h=h, yb=yb):
                        cat[4 + h // 2] = free[yb] = act(CAT[:, 4 + h // 2, :], Y[yb][:, 0:256], ACT.Copy, [mk])
                H.add(scores, C("causal"), lambda kb, h=h: V[:, kb, h * 64:h * 64 + 64],
                      (Y[yb][pr, 0:256], [mv, free[yb]], True, True, after))
            H.step(True)
            mk = rows_out("foxo", 8, lambda k, t: CAT[:, k, t * 128:t * 128 + 128], lambda k: cat[k], None)
            while bg:
                background()
            residual(1.0, True, mk, w=[mod_done[2]])

        def nsa():
            mods = MOD[:, 32:48]
            CAT = A(0, 2048).rearrange("p (c t) -> p c t", c=8)
            QT = A(2048, 2048).rearrange("p (c t) -> p c t", c=8)
            KK = [A(4096 + 512 * n, 512).rearrange("p (c t) -> p c t", c=2) for n in range(4)]
            V = A(6144, 1024).rearrange("p (b n) -> p b n", b=2)
            Z = [A(7168 + 960 * n, 960) for n in range(2)]
            TB = A(9088, 6144).rearrange("p (h k) -> p h k", h=16)
            CB = A(15232, 480)
            G3 = A(15712, 96).rearrange("p (t n) -> p t n", t=2)
            GS = A(15808, 256)
            SQ = [A(16064 + 256 * n, 256) for n in range(2)]
            RR = [A(16576 + 256 * n, 256) for n in range(2)]
            HB = A(17088, 128)
            KC = A(17216, 64)
            H1R = A(17280, 512)
            VC = A(30720 - 1024, 1024).rearrange("p (g j d) -> p g j d", g=4, j=4)
            PC = [A(18048 + 256 * n, 256) for n in range(2)]
            PCT = A(18560, 1024).rearrange("p (g t) -> p g t", g=4)
            mtb = load(TB, ins["toep"].rearrange("p (h k) -> p h k", h=16))
            mcb = load(CB, ins["cmpb"])
            mh = make_h(mods[:, 0:8], mods[:, 8:16], [mod_done[6], mod_done[7]])
            z1 = mset(H1R, 0.0)
            z2 = [mset(PC[n], 0.0) for n in range(2)]
            ca = C("causal").unsqueeze(1).broadcast_to([128, 16, 384])
            mtb = tt(TB, TB, ca, ALU.add, [mtb], q=PO)
            cn = C("cmpneg").unsqueeze(1).broadcast_to([128, 4, 120])
            cb4 = CB.rearrange("p (g n) -> p g n", g=4)
            mcb = tt(cb4, cb4, cn, ALU.add, [mcb], q=PO)
            gq = stat(1)
            mg = ts(gq, C("nsaqg"), 0.125, None, ALU.mult)
            mz = []
            for j in range(8):
                n, ps, m = project("nsac", j, mh)
                kv, g = divmod(j, 4)
                zz = Z[kv].rearrange("p (l g n) -> p l g n", l=16, g=4)
                for par in range(2):
                    pp = slice(64 * par, 64 * par + 64)
                    src = bass_window(ps, pp, par)
                    po = C("pos", 16 * kv, 16 * kv + 16)[pp, :].unsqueeze(2).broadcast_to([64, 16, 15])
                    mk = tt(zz[pp, :, g, :], src, po, ALU.add, [m])
                free[n] = mk
                mz.append(mk)
            n, ps, m = project("nsag", 0, mh)
            m = free[n] = act(GS[0:48, :], ps[0:48, :], ACT.Sigmoid, [m], bias=C("bgate")[0:48, :])
            n, ps, fr = bank()
            for t in range(2):
                mk = tp(ps[:, t * 64:t * 64 + 48], GS[0:48, t * 128:t * 128 + 128], [fr, m], n=48)
            mgate = None
            for t in range(2):
                mgate = free[n] = copy(G3[:, t, :], ps[:, t * 64:t * 64 + 48], [mk])
            qk, kn = {}, {}
            for j in range(8):
                n, ps, m = project("nsaq", j, mh)
                run_later()
                head_norm(n, ps, m, QT[:, j, :], gq, SQ[j % 2], RR[j % 2], qk, j, [mg])
            for j in range(4):
                n, ps, m = project("nsak", j, mh)
                run_later()
                head_norm(n, ps, m, KK[2 * (j // 2)][:, j % 2, :], C("nsakg", 1 + j // 2, 2 + j // 2),
                          SQ[j % 2], RR[j % 2], kn, j)
            for kv in range(2):
                w, mw, s = take("nsaw1", kv)
                n, ps, fr = bank()
                for l in range(16):
                    mk = mm(ps[0:64, 0:60], w[:, l * 64:l * 64 + 64], Z[kv][:, l * 60:l * 60 + 60], l == 0, l == 15,
                            [fr, mw, mz[4 * kv + 3]])
                give(s, mk)
                if kv == 0:
                    run_later()
                    m = free[n] = act(HB[0:64, 0:60], ps[0:64, 0:60], ACT.Gelu_apprx_tanh, [mk])
                    n, ps, fr = bank()
                    m = mm(ps[:, 0:60], C("w2k")[0:64, :], HB[0:64, 0:60], True, True, [fr, m])
                    a = act(KC[:, 0:60], ps[:, 0:60], ACT.Copy, [m])
                    b = free[n] = act(SQ[0][:, 0:60], ps[:, 0:60], ACT.Square, [m, sq_free.get(id(SQ[0]))])
                    n, ps, fr = bank()
                    m = mm(ps[:, 0:60], C("bd64"), SQ[0][:, 0:60], True, True, [fr, b])
                    c = free[n] = ts(RR[0][:, 0:60], ps[:, 0:60], 1.0 / 64, EPS, ALU.mult, ALU.add,
                                     w=[m, rr_free.get(id(RR[0]))])
                    c = rec(RR[0][:, 0:60], RR[0][:, 0:60], [act(RR[0][:, 0:60], RR[0][:, 0:60], ACT.Sqrt, [c])])
                    mkc = stt(KC[:, 0:60], KC[:, 0:60], C("nsakg", 0, 1), RR[0][:, 0:60], ALU.mult, ALU.mult, [a, c])
                else:
                    m = free[n] = act(HB[0:64, 64:124], ps[0:64, 0:60], ACT.Gelu_apprx_tanh, [mk])
                    h1 = H1R[0:64, :].rearrange("p (g j n) -> p g j n", g=4, j=4)
                    for g in range(4):
                        m2 = copy(h1[:, g, :, 0:15],
                                  HB[0:64, 64 + 15 * g:79 + 15 * g].unsqueeze(1).broadcast_to([64, 4, 15]), [m, z1])
                    n, ps, fr = bank()
                    for g in range(4):
                        m = mm(ps[:, g * 64:g * 64 + 64], H1R[0:64, g * 128:g * 128 + 128], C("w2v")[0:64, :], True,
                               True, [fr, m2])
                    for j in range(4):
                        mvc = free[n] = ts(VC[:, :, j, :], ps[:, 0:256].rearrange("p (g d) -> p g d", g=4),
                                           C("rowsel")[:, j:j + 1], None, ALU.mult, w=[m])
            msw = []
            s_sw = new_sem("swap")
            for n in range(2):
                for hf in range(2):
                    o = KK[2 * n + 1][64 * hf:64 * hf + 64, :, :]
                    i = KK[2 * n][64 - 64 * hf:128 - 64 * hf, :, :]
                    SP_late.append((len(stream), o, i, [kn[2 * n], kn[2 * n + 1]], s_sw))
            msw = (s_sw, 64)
            m = rows512("nsav", mh)
            mv = []
            for t in range(2):
                mk = act(V[:, t, :], Y[t], ACT.Copy, [m])
                free[t] = mk
                mv.append(mk)
            mpc = {}
            pcf = [z2[0], z2[1]]
            for g in range(4):
                sc = A(19600 + 128 * (g % 2), 120).rearrange("p (j n) -> p j n", n=15)
                sc3 = A(19600 + 128 * (g % 2), 120).rearrange("p (t j n) -> p t j n", t=2, n=15)
                cb3 = CB[:, g * 120:g * 120 + 120].rearrange("p (t j n) -> p t j n", t=2, n=15)
                ma = []
                for odd in range(2):
                    pr = slice(64 * odd, 64 * odd + 64)
                    n, ps, fr = bank()
                    for j in range(2):
                        for t in range(2):
                            m = mm(ps[:, (t * 2 + j) * 16:][:, 0:15], QT[pr, 2 * g + j, t * 128:t * 128 + 128],
                                   KC[pr, 15 * g:15 * g + 15], True, True, [fr, mkc, qk[7]])
                    pv = ps[:, 0:64].rearrange("p (t j n) -> p t j n", t=2, n=16)[:, :, :, 0:15]
                    free[n] = tt(sc3[:, :, odd:4:2, :], pv, cb3[:, :, odd:4:2, :], ALU.add, [m, mcb])
                    ma.append(free[n])
                m = ma
                s8 = stat(16)
                mx, sm = s8[:, 0:8], s8[:, 8:16]
                m = red(mx, sc, ALU.max, [m], neg=True)
                m = tt(sc, sc, mx.unsqueeze(2).broadcast_to([128, 8, 15]), ALU.add, [m])
                m = act(sc, sc, ACT.Exp, [m])
                m = red(sm, sc, ALU.add, [m])
                m = rec(sm, sm, [m])
                gt = G3[:, :, 12 * g:12 * g + 12].rearrange("p t (j c) -> p t j c", c=3)[:, :, :, 0]
                m = tt(sm.rearrange("p (t j) -> p t j", t=2), sm.rearrange("p (t j) -> p t j", t=2), gt, ALU.mult,
                       [m, mgate])
                m = tt(sc, sc, sm.unsqueeze(2).broadcast_to([128, 8, 15]), ALU.mult, [m])
                pc = PC[g % 2].rearrange("p (j n) -> p j n", n=32)[:, :, 0:15]
                m = tt(pc, sc, C("cmpok").rearrange("p (j n) -> p j n", n=15), ALU.mult, [m, pcf[g % 2]])
                n, ps, fr = bank()
                for t in range(2):
                    mk = tp(ps[:, t * 128:t * 128 + 128], PC[g % 2][:, t * 128:t * 128 + 128], [fr, m])
                pcf[g % 2] = mk
                mpc[g] = free[n] = act(PCT[:, g, :], ps[:, 0:256], ACT.Copy, [mk])
            H = Heads(20000)
            cat = {}
            for h in range(16):
                g, j = divmod(h, 4)
                pr = slice(64 * (h % 2), 64 * (h % 2) + 64)
                yb = (h // 2) % 4
                o = Y[yb][pr, 0:256]
                mmw = [mpc[g], mvc, free[yb]]
                for b in range(2):
                    src = KK[2 * b + (0 if g % 2 == h % 2 else 1)]

                    def scores(ps, fr, h=h, pr=pr, src=src, g=g, b=b):
                        w = [fr, qk[h // 2], kn[2 * b + g // 2], msw]
                        mm(ps[:, 0:128], QT[pr, h // 2, 0:128], src[pr, g // 2, 0:128], True, True, w, inc=False)
                        return mm(ps[:, 128:384], QT[pr, h // 2, 128:256], src[pr, g // 2, :], True, True)

                    after = None
                    if b == 1:
                        def after(mk, h=h, yb=yb, g=g, j=j, o=o):
                            m = mm(o, VC[:, g, j, :], PCT[:, g, :],
                                   False, True, [mpc[g], mvc])
                            if h % 2:
                                cat[h // 2] = free[yb] = act(CAT[:, h // 2, :], Y[yb][:, 0:256], ACT.Copy, [m])
                    gt = G3[:, :, 3 * h + 1 + b]
                    H.add(scores, TB[:, h, :], lambda kb, g=g, b=b: V[:, kb, b * 256 + g * 64:b * 256 + g * 64 + 64],
                          (o, [mv, free[yb]], b == 0, False, after), gate=(gt, mgate), wmask=mtb)
            H.step(True)
            mk = rows_out("nsao", 8, lambda k, t: CAT[:, k, t * 128:t * 128 + 128], lambda k: cat[k], None)
            while bg:
                background()
            residual(1.0, True, mk, w=[mod_done[8]])

        def bass_window(ps, pp, par):
            base = ps[pp, par:par + 1]
            return bass.AP(base.tensor, base.offset, [base.ap[0], [2, 16], [16, 15]])

        SP_late = []

        def peer(l):
            p0 = 6 * l
            mods = MOD[:, 16 * (2 * l + 1):16 * (2 * l + 1) + 16]
            mh = make_h(mods[:, 0:8], mods[:, 8:16], [mod_done[p0 + 3], mod_done[p0 + 4]])
            QT = A(0, 2048).rearrange("p (c t) -> p c t", c=8)
            qd = {}
            for j in range(8):
                n, ps, m = project(f"pq{l}", j, mh)
                qd[j] = free[n] = act(QT[:, j, :], ps, ACT.Copy, [m])
            SI = A(6144, 512).bitcast(U32)
            SV = A(6656, 512)
            SF = A(7168, 512)
            CV = A(7680, 256)
            CI = A(7936, 256).bitcast(U32)
            CA, CBf = A(8192, 256), A(8448, 256)
            CU = A(8704, 256).bitcast(U32)
            EI = A(8960, 256)
            EJ = A(9216, 256)
            GG = A(9472, 256)
            mTI = []
            TI = [TIJt[:, 256 * n:256 * n + 256] for n in range(3)]
            for t in range(2):
                S = A(2048 + 2048 * t, 2048).rearrange("p (s k) -> p s k", s=16)
                CD = A(10240 + 2048 * t, 2048)
                EQ = A(14336 + 4096 * t, 2048).rearrange("p (k a) -> p k a", a=16)
                E2 = A(16384 + 4096 * t, 2048).rearrange("p (k a) -> p k a", a=16)
                ms = []
                for hp in range(4):
                    n, ps, fr = bank()
                    for h in range(2):
                        m = mm(ps[:, h * 256:h * 256 + 256], QT[:, 2 * hp + h, t * 128:t * 128 + 128], C(f"keys{l}"),
                               True, True, [fr, qd[2 * hp + h]])
                    free[n] = act(S[:, 4 * hp:4 * hp + 4, :], ps.rearrange("p (s k) -> p s k", s=4), ACT.Copy, [m])
                    ms.append(free[n])
                sv = SV[:, 256 * t:256 * t + 256].rearrange("p (s k) -> p s k", s=16)
                si = SI[:, 256 * t:256 * t + 256].rearrange("p (s k) -> p s k", s=16)

                def top16(src, v, ix, w):
                    a, b = v[:, 0:8], v[:, 8:16]
                    i0, i1 = ix[:, 0:8], ix[:, 8:16]
                    m = DVE.put(lambda e: e.max(a, src), w)
                    m = DVE.put(lambda e: e.max_index(i0, a, src), [m])
                    m = DVE.put(lambda e: e.match_replace(src, a, src, NEG * 1e6), [m])
                    m = DVE.put(lambda e: e.max(b, src), [m])
                    return DVE.put(lambda e: e.max_index(i1, b, src), [m])

                for s in range(16):
                    m = top16(S[:, s, :], sv[:, s, :], si[:, s, :], [ms[s // 4]])
                sf = SF[:, 256 * t:256 * t + 256]
                mf = copy(sf, SI[:, 256 * t:256 * t + 256], [m])
                sv4 = sv.rearrange("p (h q) k -> p h q k", q=2)
                cd = CD.rearrange("p (h a b) -> p h a b", h=8, a=16)
                m = tt(cd, sv4[:, :, 0, :].unsqueeze(3).broadcast_to([128, 8, 16, 16]),
                       sv4[:, :, 1, :].unsqueeze(2).broadcast_to([128, 8, 16, 16]), ALU.add, [m])
                cv = CV[:, 128 * t:128 * t + 128].rearrange("p (h k) -> p h k", h=8)
                ci = CI[:, 128 * t:128 * t + 128].rearrange("p (h k) -> p h k", h=8)
                mc = m
                for h in range(8):
                    m = top16(CD[:, h * 256:h * 256 + 256], cv[:, h, :], ci[:, h, :], [mc])
                cit, cut = CI[:, 128 * t:128 * t + 128], CU[:, 128 * t:128 * t + 128]
                ca, cb = CA[:, 128 * t:128 * t + 128], CBf[:, 128 * t:128 * t + 128]
                m1 = ts(cut, cit, 4, None, ALU.logical_shift_right, w=[m])
                m1 = copy(ca, cut, [m1])
                m2 = ts(cut, cit, 15, None, ALU.bitwise_and, w=[m1])
                m2 = copy(cb, cut, [m2])
                s4 = sf.rearrange("p (h q k) -> p h q k", h=8, q=2)
                io = C("iota")[:, 0:16].unsqueeze(1).broadcast_to([128, 128, 16])
                for q, (src, dst, eq) in enumerate(((ca, EI, EQ), (cb, EJ, E2))):
                    m = tt(eq, src.unsqueeze(2).broadcast_to([128, 128, 16]), io, ALU.is_equal, [m2])
                    eq4 = eq.rearrange("p (h k) a -> p h k a", h=8)
                    m = tt(eq4, eq4, s4[:, :, q, :].unsqueeze(2).broadcast_to([128, 8, 16, 16]), ALU.mult, [m, mf])
                    me = red(dst[:, 128 * t:128 * t + 128], eq, ALU.add, [m])
                gg = GG[:, 128 * t:128 * t + 128].rearrange("p (h k) -> p h k", h=8)
                m = tt(gg, cv, cv[:, :, 0:1].broadcast_to([128, 8, 16]), ALU.subtract, [me])
                m = act(gg, gg, ACT.Exp, [m])
                st = stat(8)
                m = red(st, gg, ALU.add, [m])
                m = rec(st, st, [m])
                mg = tt(gg, gg, st.unsqueeze(2).broadcast_to([128, 8, 16]), ALU.mult, [m])
                n, ps, fr = bank()
                for q, src in enumerate((EI, EJ, GG)):
                    mk = tp(ps[:, q * 128:q * 128 + 128], src[:, 128 * t:128 * t + 128], [fr, mg])
                for q in range(3):
                    mti = free[n] = copy(TI[q][:, t * 128:t * 128 + 128], ps[:, q * 128:q * 128 + 128], [mk])
                mTI.append(mti)
            fence()
            G = ARt[:, :].rearrange("p (t j) -> p t j", j=128)
            ohf = [None, None]
            io = C("iota")
            for t4 in range(64):
                n, ps, fr = bank()
                for q in range(4):
                    t = 4 * t4 + q
                    b = t % 2
                    o1, o2 = OHt[:, b * 256:b * 256 + 128], OHt[:, b * 256 + 128:b * 256 + 256]
                    a = ts(o1, io, TI[0][:, t:t + 1], None, ALU.is_equal, w=[mTI, ohf[b]])
                    c = ts(o2, io, TI[1][:, t:t + 1], TI[2][:, t:t + 1], ALU.is_equal, ALU.mult, w=[mTI, ohf[b]])
                    ohf[b] = mm(ps[:, q * 128:q * 128 + 128], o1, o2, True, True, [fr, a, c])
                mg = free[n] = act(G[:, 4 * t4:4 * t4 + 4, :], ps.rearrange("p (t j) -> p t j", t=4), ACT.Copy,
                                   [ohf[b]])
            GE = [WTt[:, 256 * n:256 * n + 256] for n in range(2)]
            WT = [WTt[:, 512 + 256 * n:768 + 256 * n] for n in range(2)]
            wtf, gef = [None, None], [None, None]
            wt_m = {}

            def down(j):
                w, m, s = take(f"pv{l}", j)
                b = j % 2
                for t in range(2):
                    for hf in range(2):
                        mk = mm(Y[2 * t + hf], WT[b][:, t * 128:t * 128 + 128], w[:, hf * 512:hf * 512 + 512], j == 0,
                                j == 127, [m, wt_m[j]] + ([free[2 * t + hf]] if j == 0 else []), inc=True)
                give(s, mk)
                wtf[b] = mk
                return mk

            for j in range(128):
                n, ps, mk = project(f"pu{l}", j, mh)
                b = j % 2
                a = free[n] = act(GE[b], ps, ACT.Gelu_apprx_tanh, [mk, gef[b]])
                gef[b] = wt_m[j] = tt(WT[b], GE[b], G[:, :, j], ALU.mult, [a, mg, wtf[b]])
                if j >= 1:
                    down(j - 1)
                background()
                if j == 20:
                    bg.extend(ahead)
                    ahead.clear()
            mk = down(127)
            while bg and mod_done.get(p0 + 5) is None:
                background()
            fence()
            residual(1.0, True, mk, w=[mod_done[p0 + 5]])
            while bg:
                background()

        ahead = []

        def ffn(nm, l):
            mh = make_h(C(f"fn{'1' if nm == 'A' else '2'}_{l}"), None, None)
            AC = A(0, 22 * 256).rearrange("p (c t) -> p c t", c=22)
            SG = [A(6000 + 256 * n, 256) for n in range(2)]
            ma = {}
            for j in range(22):
                n, ps, m = project(f"fg{nm}{l}", j, mh)
                g = free[n] = act(SG[j % 2], ps, ACT.Silu, [m, ma.get(j - 2)])
                n, ps, m = project(f"fu{nm}{l}", j, mh)
                ma[j] = free[n] = tt(AC[:, j, :], ps, SG[j % 2], ALU.mult, [m, g])
            mk = rows_out(f"fd{nm}{l}", 22, lambda k, t: AC[:, k, t * 128:t * 128 + 128], lambda k: ma[k], None)
            residual(0.5, False, mk)

        def ssd(l):
            CAT = A(0, 4096).rearrange("p (c t) -> p c t", c=16)
            XC = A(4096, 4096).rearrange("p (c t) -> p c t", c=16)
            XT = A(8192, 2048).rearrange("p (c n) -> p c n", c=2)
            XD = A(10240, 2048).rearrange("p (c n) -> p c n", c=2)
            ZS = A(12288, 2048).rearrange("p (c n) -> p c n", c=2)
            BT = A(14336, 512)
            ST = A(14848, 1024)
            XE = A(15872, 1024)
            YS = A(16896, 2048).rearrange("p (c n) -> p c n", c=2)
            QT = A(18944, 2048).rearrange("p (c t) -> p c t", c=8)
            KT = A(20992, 2048).rearrange("p (c t) -> p c t", c=8)
            V = A(23040, 2048).rearrange("p (b n) -> p b n", b=2)
            XB = [A(25088 + 260 * n, 259) for n in range(2)]
            T0 = [A(25608 + 256 * n, 256) for n in range(2)]
            SQ = [A(26120 + 256 * n, 256) for n in range(2)]
            RR = [A(26632 + 256 * n, 256) for n in range(2)]
            D = [A(27144 + 256 * n, 256) for n in range(5)]
            DT = A(28424, 64)
            EA = A(28488, 32)
            CM = A(28520, 1024)
            mh = make_h(C(f"mixn_{l}"), None, None)
            an = stat(1)
            ma = act(an[0:16, :], C(f"alog_{l}")[0:16, :], ACT.Exp)
            n, ps, m = project(f"sd{l}", 0, mh)
            x = D[0][0:16, :]
            m = free[n] = ts(x, ps[0:16, :], C(f"dtb_{l}")[0:16, :], None, ALU.add, w=[m])
            m = log1p_exp(D[1][0:16, :], x, D[2][0:16, :], D[3][0:16, :], D[4][0:16, :], [m])
            m = stt(D[0][0:16, :], x, 0.0, D[1][0:16, :], ALU.max, ALU.add, [m])
            mdt = ts(D[1][0:16, :], D[0][0:16, :], an[0:16, :], -1.0, ALU.mult, ALU.mult, w=[m, ma])
            mxc = {}
            mz = [mset(XB[n][:, 0:3], 0.0) for n in range(2)]
            for j in range(16):
                b = j % 2
                n, ps, m = project(f"sx{l}", j, mh)
                if j == 0:
                    n2, p2, fr = bank()
                    for q in range(2):
                        for t in range(2):
                            mk = tp(p2[:, (2 * q + t) * 16:][:, 0:16], D[q][0:16, t * 128:t * 128 + 128], [fr, mdt],
                                    n=16)
                    mDT = free[n2] = copy(DT, p2[:, 0:64], [mk])
                mk = free[n] = act(XB[b][:, 3:259], ps, ACT.Copy, [m, mz[b], mxc.get(j - 2)])
                cw, cb = C(f"cw_{l}", 4 * j, 4 * j + 4), C(f"cb_{l}", j, j + 1)
                mk = ts(T0[b], XB[b][:, 0:256], cw[:, 0:1], cb, ALU.mult, ALU.add, w=[mk, mxc.get(j - 2)])
                for k in range(1, 4):
                    mk = stt(T0[b], XB[b][:, k:k + 256], cw[:, k:k + 1], T0[b], ALU.mult, ALU.add, [mk])
                mxc[j] = act(XC[:, j, :], T0[b], ACT.Silu, [mk])
            dt = DT[:, 0:32].rearrange("p (t h) -> p t h", t=2)
            ad = DT[:, 32:64].rearrange("p (t h) -> p t h", t=2)
            m = rows_out(f"sz{l}", 8, lambda k, t: HT[:, k, t * 128:t * 128 + 128], lambda k: mh, None)
            for t in range(2):
                for hf in range(2):
                    mzs = free[2 * t + hf] = act(ZS[:, t, hf * 512:hf * 512 + 512], Y[2 * t + hf], ACT.Silu, [m])
            mxt = []
            for t in range(2):
                for c4 in range(2):
                    n, ps, fr = bank()
                    for c in range(4):
                        mk = tp(ps[:, c * 128:c * 128 + 128], XC[:, 4 * c4 + c, t * 128:t * 128 + 128],
                                [fr, mxc[4 * c4 + c]])
                    free[n] = act(XT[:, t, c4 * 512:c4 * 512 + 512], ps, ACT.Copy, [mk])
                    mxt.append(free[n])
            n, ps, fr = bank()
            for c in range(4):
                mk = tp(ps[:, c * 128:c * 128 + 128], XC[:, 8 + c, 0:128], [fr, mxc[11]])
            mbt = free[n] = act(BT, ps, ACT.Copy, [mk])
            mxd = []
            for t in range(2):
                mxd.append(tt(XD[:, t, :].rearrange("p (h e) -> p h e", h=16),
                              XT[:, t, :].rearrange("p (h e) -> p h e", h=16),
                              dt[:, t, :].unsqueeze(2).broadcast_to([128, 16, 64]), ALU.mult, [mxt, mDT]))
            n, ps, fr = bank()
            mm(ps[:, 0:16], C("gt"), ad[:, 0, :], True, True, [fr, mDT])
            m = mm(ps[:, 16:32], C("le"), ad[:, 1, :], True, True)
            mea = free[n] = act(EA, ps[:, 0:32], ACT.Exp, [m])
            mxe = tt(XE.rearrange("p (h e) -> p h e", h=16), XD[:, 0, :].rearrange("p (h e) -> p h e", h=16),
                     EA[:, 0:16].unsqueeze(2).broadcast_to([128, 16, 64]), ALU.mult, [mxd[0], mea], q=PO)
            mcm = {}
            for c in range(2):
                n, ps, fr = bank()
                for g in range(4):
                    mk = mm(ps[:, g * 128:g * 128 + 128], XC[:, 8 + g, c * 128:c * 128 + 128],
                            XC[:, 12 + g, c * 128:c * 128 + 128], True, True, [fr, mxc[15]])
                mcm[c] = free[n] = tt(CM[:, c * 512:c * 512 + 512].rearrange("p (g l) -> p g l", g=4),
                                      ps.rearrange("p (g l) -> p g l", g=4),
                                      C("le").unsqueeze(1).broadcast_to([128, 4, 128]), ALU.mult, [mk])
            for hf in range(2):
                n, ps, fr = bank()
                for q in range(2):
                    g = 2 * hf + q
                    mk = mm(ps[:, q * 256:q * 256 + 256], BT[:, g * 128:g * 128 + 128], XE[:, g * 256:g * 256 + 256],
                            True, True, [fr, mbt, mxe])
                mst = free[n] = act(ST[:, hf * 512:hf * 512 + 512], ps, ACT.Copy, [mk])
            WB = [A(29544, 512), A(30056, 512)]
            EB = [A(XN, 512), A(XN + 512, 512)]
            wbf, ebf = [None, None], [None, None]
            todo = []

            def diag(c, g, e, me):
                for r in range(4):
                    h = 4 * g + r
                    yo = Y[2 * c + h // 8][:, (h % 8) * 64:(h % 8) * 64 + 64]
                    mk = mm(yo, e[:, r * 128:r * 128 + 128], XD[:, c, h * 64:h * 64 + 64], True, True,
                            [me, mxd[c]] + [free[2 * c + h // 8]])
                return mk

            mdg = {}
            for i in range(8):
                c, g = divmod(i, 4)
                b = i % 2
                w4 = WB[b].rearrange("p (r s) -> p r s", r=4)
                m = tt(w4, C("gt").unsqueeze(1).broadcast_to([128, 4, 128]),
                       ad[:, c, 4 * g:4 * g + 4].unsqueeze(2).broadcast_to([128, 4, 128]), ALU.mult,
                       [mDT, wbf[b]], q=PO)
                n, ps, fr = bank()
                for r in range(4):
                    mk = mm(ps[:, r * 128:r * 128 + 128], WB[b][:, r * 128:r * 128 + 128], C("le"), True, True,
                            [fr, m])
                wbf[b] = mk
                me = free[n] = act(EB[b], ps, ACT.Exp, [mk, ebf[b]])
                me = tt(EB[b].rearrange("p (r l) -> p r l", r=4), EB[b].rearrange("p (r l) -> p r l", r=4),
                        CM[:, c * 512 + g * 128:c * 512 + g * 128 + 128].unsqueeze(1).broadcast_to([128, 4, 128]),
                        ALU.mult, [me, mcm[c]])
                if todo:
                    i2, args = todo.pop()
                    mdg[i2] = ebf[i2 % 2] = diag(*args)
                todo.append((i, (c, g, EB[b], me)))
            i2, args = todo.pop()
            mdg[i2] = diag(*args)
            dsk = C(f"dsk_{l}").unsqueeze(2).broadcast_to([128, 16, 64])
            mys = []
            for t in range(2):
                mys.append(tt(YS[:, t, :].rearrange("p (h e) -> p h e", h=16),
                              XT[:, t, :].rearrange("p (h e) -> p h e", h=16), dsk, ALU.mult, [mxt], q=PO))
            moff = []
            for hf in range(2):
                n, ps, fr = bank()
                for q in range(2):
                    g = 2 * hf + q
                    mk = mm(ps[:, q * 256:q * 256 + 256], XC[:, 12 + g, 128:256], ST[:, g * 256:g * 256 + 256], True,
                            True, [fr, mst])
                tmp = XE[:, hf * 512:hf * 512 + 512]
                m = free[n] = tt(tmp.rearrange("p (h e) -> p h e", h=8), ps.rearrange("p (h e) -> p h e", h=8),
                                 EA[:, 16 + 8 * hf:24 + 8 * hf].unsqueeze(2).broadcast_to([128, 8, 64]), ALU.mult,
                                 [mk, mea, mst])
                ys = YS[:, 1, hf * 512:hf * 512 + 512]
                moff.append(tt(ys, ys, tmp, ALU.add, [m, mys[1]]))
            st = stat(16)
            m2 = None
            for t in range(2):
                for hf in range(2):
                    ys = YS[:, t, hf * 512:hf * 512 + 512]
                    m = free[2 * t + hf] = tt(ys, ys, Y[2 * t + hf], ALU.add, [mdg[7], mdg[4 * t + 3], mys[t], moff])
                    m = tt(ys, ys, ZS[:, t, hf * 512:hf * 512 + 512], ALU.mult, [m, mzs])
                for g in range(4):
                    m2 = act(XE[:, g * 256:g * 256 + 256], YS[:, t, g * 256:g * 256 + 256], ACT.Square,
                             [m, moff, m2],
                             acc=st[:, 4 * t + g:4 * t + g + 1])
            m = ts(st[:, 0:8], st[:, 0:8], 1.0 / 256, EPS, ALU.mult, ALU.add, w=[m2], q=PO)
            mr = tt(st[:, 8:16], st[:, 0:8], NH(8), ALU.pow, [m], q=PO)
            mn = []
            for t in range(2):
                mn.append(tt(YS[:, t, :].rearrange("p (g e) -> p g e", g=4),
                             YS[:, t, :].rearrange("p (g e) -> p g e", g=4),
                             st[:, 8 + 4 * t:12 + 4 * t].unsqueeze(2).broadcast_to([128, 4, 256]), ALU.mult, [mr],
                             q=PO if t else DVE))
            gq = stat(1)
            mg = ts(gq, C(f"dqg_{l}"), 0.125, None, ALU.mult)
            qk = {}
            for j in range(16):
                n, ps, m = project(f"sqk{l}", j, mh)
                run_later()
                dst = QT[:, j, :] if j < 8 else KT[:, j - 8, :]
                head_norm(n, ps, m, dst, gq if j < 8 else C(f"dkg_{l}"), SQ[j % 2], RR[j % 2], qk, j, [mg])
            cat = {}
            for c2 in range(4):
                n, ps, fr = bank()
                for q in range(2):
                    for t in range(2):
                        c = 2 * c2 + q
                        mk = tp(ps[:, q * 256 + t * 128:][:, 0:128], YS[:, t, c * 128:c * 128 + 128], [fr, mn])
                for q in range(2):
                    c = 2 * c2 + q
                    cat[c] = free[n] = ts(CAT[:, c, :], ps[:, q * 256:q * 256 + 256], C(f"ssdn_{l}")[:, c:c + 1],
                                          None, ALU.mult, w=[mk])
            run_later()
            m = rows_out(f"sv{l}", 8, lambda k, t: HT[:, k, t * 128:t * 128 + 128], lambda k: mh, None)
            for t in range(2):
                for hf in range(2):
                    mv = free[2 * t + hf] = act(V[:, t, hf * 512:hf * 512 + 512], Y[2 * t + hf], ACT.Copy, [m])
            H = Heads(4096)
            H.sf = [[mxc[15], mst, mdg[7], mk, moff]] * 3
            H.pf = [[mdg[7], mst, mk, mk, moff]] * 3
            for h in range(16):
                pr = slice(64 * (h % 2), 64 * (h % 2) + 64)

                def scores(ps, fr, h=h, pr=pr):
                    w = [fr, qk[h // 2], qk[8 + h // 2]]
                    mm(ps[:, 0:128], QT[pr, h // 2, 0:128], KT[pr, h // 2, 0:128], True, True, w, inc=False)
                    return mm(ps[:, 128:384], QT[pr, h // 2, 128:256], KT[pr, h // 2, :], True, True)

                yb = (h // 2) % 4
                after = None
                if h % 2:
                    def after(mk, h=h, yb=yb):
                        cat[8 + h // 2] = free[yb] = act(CAT[:, 8 + h // 2, :], Y[yb][:, 0:256], ACT.Copy, [mk])
                H.add(scores, C("dilmask"), lambda kb, h=h: V[:, kb, h * 64:h * 64 + 64],
                      (Y[yb][pr, 0:256], [mv, free[yb]], True, True, after), mult=C("dilmult"))
            H.step(True)
            mk = rows_out(f"so{l}", 16, lambda k, t: CAT[:, k, t * 128:t * 128 + 128], lambda k: cat[k], None)
            residual(1.0, False, mk)

        need = [s for s in stages]
        if need and need[0] in ("mix0", "peer0", "mix1", "peer1"):
            sg = stat(8)
            m = act(sg, C("c"), ACT.Sigmoid)
            sc_m[0] = tt(silu_c, C("c"), sg, ALU.mult, [m])
        for s in stages:
            l = int(s[-1])
            if s == "mix0":
                for p in (0, 1):
                    for f in ada_piece(p):
                        f()
                for p in (2, 3, 4):
                    bg.extend(ada_piece(p))
                fox()
            elif s == "mix1":
                if stages[0] == "mix1":
                    for p in (6, 7):
                        for f in ada_piece(p):
                            f()
                    for p in (8, 9, 10):
                        bg.extend(ada_piece(p))
                nsa()
            elif s[:4] == "peer":
                if stages[0] == s:
                    for p in (6 * l + 3, 6 * l + 4):
                        for f in ada_piece(p):
                            f()
                if l == 0:
                    bg.extend(ada_piece(5))
                    if "mix1" in stages:
                        for p in (6, 7, 9, 10):
                            ahead.extend(ada_piece(p))
                else:
                    bg.extend(ada_piece(11))
                peer(l)
                if l == 0 and "mix1" in stages:
                    for f in ada_piece(8):
                        bg.append(f)
            elif s[:3] == "ffn":
                ffn(s[3], l)
            else:
                ssd(l)
            fence()
        s_out = new_sem("out")
        for t in range(2):
            o = out.rearrange("a (t p) n -> (a t) p n", p=128)[t]
            SC.pending = []
            SC.dma(lambda e, o=o, t=t: e.dma_start(o, X[:, t, :]), [m_x[t]], s_out)
        SC.ops.append(("wait", s_out, 32))

        late = list(SP_late)
        for n, (src, _) in enumerate(stream):
            while late and late[0][0] <= n - NR + 1:
                _, o, i, w, s = late.pop(0)
                SP.dma(lambda e, o=o, i=i: e.dma_start(o, i), w, s)
            w = [stream[n - NR][1]] if n >= NR else []
            o = RINGt[:, (n % NR) * 1024:(n % NR + 1) * 1024]
            SP.dma(lambda e, o=o, src=src: e.dma_start(o, src), w, ring_sem[n % NR])
        for _, o, i, w, s in late:
            SP.dma(lambda e, o=o, i=i: e.dma_start(o, i), w, s)

        block = ctx.enter_context(nc.Block())

        @block.sync
        def _(eng):
            SP.emit(eng)

        @block.tensor
        def _(eng):
            PE.emit(eng)

        @block.vector
        def _(eng):
            DVE.emit(eng)

        @block.scalar
        def _(eng):
            SC.emit(eng)

        @block.gpsimd
        def _(eng):
            PO.emit(eng)


def kernel(**inputs):
    import concourse.bacc as _bacc
    from concourse.bass_utils import run_bass_kernel_spmd as _run

    nc = _bacc.Bacc("TRN2", target_bir_lowering=False, num_devices=1)
    arrays = lay_out(inputs)
    ins = {k: nc.dram_tensor(f"in_{k}", v.shape, F32, kind="ExternalInput").ap() for k, v in arrays.items()}
    out = nc.dram_tensor("out_x", (1, 256, 1024), F32, kind="ExternalOutput").ap()
    build(nc, ins, out)
    r = _run(nc, [{f"in_{k}": v for k, v in arrays.items()}], core_ids=[0])
    return r.results[0]["out_x"]
```

```python
import numpy as np
import concourse.bass as bass
from concourse import mybir
from contextlib import ExitStack

F32 = mybir.dt.float32
F32R = mybir.dt.float32r
U32 = mybir.dt.uint32
ALU = mybir.AluOpType
ACT = mybir.ActivationFunctionType
AX = mybir.AxisListType

EPS = 1e-6
SECOND_T, PER_SLOT = 44, 3
NEG = -1e30
NR = 3
NHL = 3
AHEAD = 2
WHOLE = ("ada", "nsaw1")
STAGES = ("mix0", "peer0", "mix1", "peer1", "ffnA0", "ssd0", "ffnB0", "ffnA1", "ssd1", "ffnB1")


def shape_constants():
    p = np.arange(128)
    f = np.float32
    c = {}
    c["ident"] = np.eye(128, dtype=f)
    c["ones"] = np.ones((128, 128), f)
    c["bd64"] = (p[:, None] // 64 == p[None, :] // 64).astype(f)
    c["le"] = (p[:, None] <= p[None, :]).astype(f)
    c["gt"] = (p[:, None] > p[None, :]).astype(f)
    c["iota"] = np.broadcast_to(p.astype(f), (128, 128)).copy()
    dist = np.concatenate([p[:, None] - p[None, :], 128 + p[:, None] - np.arange(256)[None, :]], 1)
    c["causal"] = np.where(dist >= 0, 0.0, NEG).astype(f)
    mult = ((dist >= 0) & (dist <= 128)).astype(f) + ((dist >= 0) & (dist % 4 == 0)) + ((dist >= 0) & (dist % 16 == 0))
    c["dilmask"] = np.where(mult > 0, 0.0, NEG).astype(f)
    c["dilmult"] = mult.astype(f)
    t = np.arange(256)
    ends = np.arange(15) * 16 + 31
    ok = (ends[None, :] <= t[:, None]).reshape(2, 128, 15).transpose(1, 0, 2)
    ok = np.repeat(ok[:, :, None, :], 4, 2).reshape(128, 120)
    c["cmpok"] = ok.astype(f)
    c["cmpneg"] = np.where(ok, 0.0, NEG).astype(f)
    sel = np.zeros((128, 8), f)
    for h in range(8):
        sel[h::32, h] = 1
    c["headsel"] = sel
    c["rowsel"] = (p[:, None] // 32 == np.arange(4)[None, :]).astype(f)
    c["neghalf"] = np.full((128, 1), -0.5, f)
    return c


def rel_buckets(dist):
    n = np.maximum(dist, 0)
    nf = np.maximum(n, 1).astype(np.float32)
    large = 16 + (np.log(nf / np.float32(16)) / np.float32(np.log(8.0)) * np.float32(16)).astype(np.int32)
    return np.where(n < 16, n, np.minimum(large, 31))


STAGE_CONSTANTS = ("causal", "dilmask", "dilmult", "cmpok", "cmpneg")


def columns(v):
    return v.reshape(-1, 128).T


def packed(i):
    c = {k: v for k, v in shape_constants().items() if k not in STAGE_CONSTANTS}
    f = np.float32

    def rows(v, at=0):
        z = np.zeros((128, v.shape[1] if v.ndim > 1 else 1), f)
        z[at:at + v.shape[0]] = v.reshape(v.shape[0], -1)
        return z

    c["c"] = columns(i["c"][0])
    c["normg"] = columns(i["norm_g"])
    c["foxqg"] = np.tile(i["even_q_g"][0], 2)[:, None]
    c["foxkg"] = np.tile(i["even_k_g"][0], 2)[:, None]
    c["convw"] = i["even_conv_w"][0].reshape(3, 4, 128).transpose(2, 1, 0).reshape(128, 12)
    bf = np.zeros((128, 1), f)
    for q in range(4):
        bf[32 * q:32 * q + 8, 0] = i["even_b_f"][0]
    c["bf"] = bf
    c["nsaqg"] = np.tile(i["odd_q_g"][0], 2)[:, None]
    c["nsakg"] = np.tile(i["odd_k_g"][0], (1, 2)).T
    c["bgate"] = rows(i["odd_b_gate"][0][:, None])
    c["pos"] = i["odd_cmp_pos"][0].reshape(2, 16, 2, 64).transpose(2, 3, 0, 1).reshape(128, 32)
    c["w2k"] = rows(np.tile(i["odd_cmp_w2"][0, 0], (1, 2)))
    c["w2v"] = rows(i["odd_cmp_w2"][0, 1])
    for l in range(2):
        c[f"fn1_{l}"] = columns(i["ffn1_norm_2"][l])
        c[f"fn2_{l}"] = columns(i["ffn2_norm_2"][l])
        c[f"mixn_{l}"] = columns(i["mix_norm_2"][l])
        c[f"ssdn_{l}"] = columns(i["ssd_norm_2"][l])
        c[f"dqg_{l}"] = np.tile(i["q_norm_2"][l], 2)[:, None]
        c[f"dkg_{l}"] = np.tile(i["k_norm_2"][l], 2)[:, None]
        c[f"cw_{l}"] = i["conv_w_2"][l].reshape(4, 16, 128).transpose(2, 1, 0).reshape(128, 64)
        c[f"cb_{l}"] = columns(i["conv_b_2"][l])
        c[f"dtb_{l}"] = rows(i["dt_bias_2"][l][:, None])
        c[f"alog_{l}"] = rows(i["a_log_2"][l][:, None])
        c[f"dsk_{l}"] = np.broadcast_to(i["d_skip_2"][l], (128, 16)).copy()
    return c


def stationary(w):
    n = -(-w.shape[1] // 128)
    if n * 128 != w.shape[1]:
        w = np.concatenate([w, np.zeros((w.shape[0], n * 128 - w.shape[1]), w.dtype)], 1)
    return w.reshape(8, 128, n, 128).transpose(2, 1, 0, 3).reshape(n, 128, 1024)


def moving(w):
    return w.reshape(-1, 128, 1024)


def moving512(w):
    return w.reshape(4, 2, 128, 512).transpose(0, 2, 1, 3).reshape(4, 128, 1024)


def lay_out(i):
    i = {k: np.asarray(v) for k, v in i.items()}
    a = {}
    pk = packed(i)
    a["pack"] = np.concatenate(list(pk.values()), 1)
    for k, v in shape_constants().items():
        if k in STAGE_CONSTANTS:
            a[k] = v
    a["x"] = i["x"][0].reshape(2, 128, 1024)
    a["ada"] = i["ada_w"].reshape(2, 8, 128, 6, 1024).transpose(0, 3, 1, 2, 4).reshape(96, 128, 1024)
    a["adab"] = i["ada_b"].reshape(12, 1, 1024)
    w = i["even_w_in"][0]
    st = stationary(w[:, :2560])
    a["foxst"] = np.concatenate([st[[4 + j, 8 + j, j]] for j in range(4)] + [st[12:20]])
    wf = np.zeros((1024, 128), np.float32)
    for q in range(4):
        wf[:, 32 * q:32 * q + 8] = w[:, 3072:3080]
    a["foxf"] = stationary(wf)
    a["foxv"] = moving512(w[:, 2560:3072])
    a["foxo"] = moving(i["even_w_out"][0])
    w = i["odd_w_in"][0]
    a["nsaq"] = stationary(w[:, :1024])
    kv = w[:, 1024:1536].reshape(1024, 8, 1, 64)
    a["nsac"] = stationary(np.tile(kv, (1, 1, 2, 1)).reshape(1024, 1024))
    a["nsak"] = stationary(np.concatenate([w[:, 1536:1792], w[:, 2048:2304]], 1))
    a["nsav"] = moving512(np.concatenate([w[:, 1792:2048], w[:, 2304:2560]], 1))
    a["nsag"] = stationary(w[:, 2560:2608])
    a["nsaw1"] = i["odd_cmp_w1"][0].reshape(2, 16, 128, 64).transpose(0, 2, 1, 3).reshape(2, 128, 1024)
    a["nsao"] = moving(i["odd_w_out"][0])
    p = np.arange(128)
    dist = np.concatenate([p[:, None] - p[None, :], 128 + p[:, None] - np.arange(256)[None, :]], 1)
    tab = i["rel_table"]
    a["toep"] = tab[rel_buckets(dist)].transpose(0, 2, 1).reshape(128, 16 * 384)
    t = np.arange(256)
    ends = np.arange(15) * 16 + 31
    cb = tab[rel_buckets(t[:, None] - ends[None, :])].reshape(2, 128, 15, 4, 4)
    a["cmpb"] = cb.transpose(1, 3, 0, 4, 2).reshape(128, 480)
    for l in range(2):
        k = np.zeros((2, 64, 2, 128), np.float32)
        for p in range(2):
            k[p, :, p, :] = i["peer_keys"][l, p].T
        a[f"keys{l}"] = k.reshape(128, 256)
        a[f"pq{l}"] = stationary(i["peer_w_q"][l])
        a[f"pu{l}"] = i["peer_u"][l].reshape(128, 128, 8, 128).transpose(1, 3, 2, 0).reshape(128, 128, 1024)
        a[f"pv{l}"] = i["peer_v"][l].reshape(128, 128, 1024).transpose(1, 0, 2)
        for n, s in (("A", "1"), ("B", "2")):
            a[f"fg{n}{l}"] = stationary(i[f"ffn{s}_w_gate_2"][l])
            a[f"fu{n}{l}"] = stationary(i[f"ffn{s}_w_up_2"][l])
            a[f"fd{n}{l}"] = moving(i[f"ffn{s}_w_down_2"][l])
        w = i["w_in_2"][l]
        a[f"sz{l}"] = moving(w[:, :1024])
        a[f"sx{l}"] = stationary(w[:, 1024:3072])
        a[f"sd{l}"] = stationary(w[:, 3072:3088])
        a[f"sqk{l}"] = stationary(w[:, 3088:5136])
        a[f"sv{l}"] = moving(w[:, 5136:6160])
        a[f"so{l}"] = moving(i["w_out_2"][l])
    return {k: np.ascontiguousarray(v, dtype=np.float32) for k, v in a.items()}


def pack_places():
    z = {"c": (1, 1024), "norm_g": (2, 2, 1024), "even_q_g": (1, 64), "even_k_g": (1, 64), "even_conv_w": (1, 3, 512),
         "even_b_f": (1, 8), "odd_q_g": (1, 64), "odd_k_g": (1, 3, 64), "odd_b_gate": (1, 48),
         "odd_cmp_pos": (1, 2, 32, 64), "odd_cmp_w2": (1, 2, 64, 64),
         "ffn1_norm_2": (2, 1024), "ffn2_norm_2": (2, 1024), "mix_norm_2": (2, 1024), "ssd_norm_2": (2, 1024),
         "q_norm_2": (2, 64), "k_norm_2": (2, 64), "conv_w_2": (2, 4, 2048), "conv_b_2": (2, 2048),
         "dt_bias_2": (2, 16), "a_log_2": (2, 16), "d_skip_2": (2, 16)}
    pk = packed({k: np.zeros(s, np.float32) for k, s in z.items()})
    at, out = 0, {}
    for k, v in pk.items():
        out[k] = (at, v.shape[1])
        at += v.shape[1]
    return out, at


class Counter:

    def __init__(self, new_sem, name):
        self.new_sem, self.name, self.sem, self.n, self.k = new_sem, name, None, 0, 0

    def step(self):
        if self.sem is None or self.n >= 16000:
            self.sem, self.n, self.k = self.new_sem(f"{self.name}{self.k}"), 0, self.k + 1
        self.n += 1
        return (self.sem, self.n)

    def last(self):
        return (self.sem, self.n) if self.sem is not None else None


class Queue:

    def __init__(self, new_sem, name):
        self.ops, self.count, self.done, self.pending = [], Counter(new_sem, name), {}, []

    def wait(self, marks):
        for m in marks:
            if m is None:
                continue
            if isinstance(m, list):
                self.wait(m)
                continue
            sem, n = m
            if self.done.get(id(sem), 0) < n:
                self.done[id(sem)] = n
                self.ops.append(("wait", sem, n))

    def put(self, fn, waits, inc=True, aside=False):
        if not aside:
            self.wait(self.pending)
            self.pending = []
        self.wait(waits)
        mark = self.count.step() if inc else None
        self.ops.append(("do", fn, mark[0] if inc else None))
        return mark

    def dma(self, fn, waits, sem):
        self.wait(self.pending)
        self.pending = []
        self.wait(waits)
        self.ops.append(("dma", fn, sem))

    def emit(self, eng):
        for kind, a, b in self.ops:
            if kind == "wait":
                eng.wait_ge(a, b)
            elif kind == "do":
                ins = a(eng)
                if b is not None:
                    ins.then_inc(b, 1)
            else:
                a(eng).then_inc(b, 16)


class Mark0:
    pass


def build(nc, ins, out, stages=STAGES):
    ctx = ExitStack()
    with ctx:
        tensors = {}

        def new_sem(name):
            return ctx.enter_context(nc.semaphore("s_" + name))

        places, npack = pack_places()
        for name, cols, dt in (("X", 2048, F32), ("HTH", 2048, F32R), ("HTL", 2048, F32R), ("RING", NR * 1024, F32),
                               ("HI", NHL * 1024, F32R), ("LO", NHL * 1024, F32R), ("ACC", 1024, F32),
                               ("CST", npack, F32), ("STAT", 256, F32), ("MOD", 80, F32)):
            tensors[name] = ctx.enter_context(nc.sbuf_tensor(name, [128, cols], dt))
        banks = [ctx.enter_context(nc.psum_tensor(f"P{n}", [128, 512], F32)) for n in range(8)]
        plan = program(nc, ins, out, stages, places, tensors, banks, lambda name: Mark0(), None)[1]
        queues, _ = program(nc, ins, out, stages, places, tensors, banks, new_sem, plan)

        block = ctx.enter_context(nc.Block())

        @block.sync
        def _(eng):
            queues[4].emit(eng)

        @block.tensor
        def _(eng):
            queues[0].emit(eng)

        @block.vector
        def _(eng):
            queues[1].emit(eng)

        @block.scalar
        def _(eng):
            queues[2].emit(eng)

        @block.gpsimd
        def _(eng):
            queues[3].emit(eng)


def program(nc, ins, out, stages, places, tensors, banks, new_sem, plan):
    if True:
        X = tensors["X"][:, :].rearrange("p (t n) -> p t n", t=2)
        HT = [tensors[n][:, :].rearrange("p (k t) -> p k t", k=8) for n in ("HTH", "HTL")]
        RINGt, HIt, LOt, ACCt, CSTt = (tensors[n] for n in ("RING", "HI", "LO", "ACC", "CST"))
        STAT, MOD = tensors["STAT"][:, :], tensors["MOD"][:, :]
        Y = [b[:, :] for b in banks[:4]]

        PE, DVE, SC, PO, SP = (Queue(new_sem, n) for n in ("pe", "dve", "act", "pool", "sp"))
        local = {}

        def C(name, a=0, b=None):
            if name in local:
                return local[name]
            at, n = places[name]
            return CSTt[:, at + a:at + (n if b is None else b)]

        def NH(n):
            at = places["neghalf"][0]
            return CSTt[:, at:at + 1].broadcast_to([128, n])

        def scope(stage, *parts):
            with ExitStack() as c:
                for name, cols, dt in parts:
                    key = f"{stage}_{name}"
                    if key not in tensors:
                        tensors[key] = c.enter_context(nc.sbuf_tensor(key, [128, cols], dt))
            got = [tensors[f"{stage}_{name}"] for name, _, _ in parts]
            arena[0] = got[0]
            return got

        arena = [None]
        GB = [None]

        def A(off, n):
            return arena[0][:, off:off + n]

        def mm(o, l, r, start, stop, w=(), inc=None):
            return PE.put(lambda e: e.matmul(o, l, r, start=start, stop=stop), w, stop if inc is None else inc)

        def tp(o, i, w=(), n=128, inc=True):
            idt = C("ident")[0:n, 0:n]
            return PE.put(lambda e: e.transpose(o, i, idt), w, inc)

        def tt(o, a, b, op, w=(), q=None):
            return (q or DVE).put(lambda e: e.tensor_tensor(o, a, b, op), w)

        def ts(o, a, s1, s2, op0, op1=None, w=(), q=None):
            if op1 is None:
                return (q or DVE).put(lambda e: e.tensor_scalar(o, a, s1, None, op0), w)
            return (q or DVE).put(lambda e: e.tensor_scalar(o, a, s1, s2, op0, op1), w)

        def stt(o, a, s, b, op0, op1, w=()):
            return DVE.put(lambda e: e.scalar_tensor_tensor(out=o, in0=a, scalar=s, in1=b, op0=op0, op1=op1), w)

        def copy(o, a, w=(), q=None):
            return (q or DVE).put(lambda e: e.tensor_copy(o, a), w)

        def red(o, a, op, w=(), neg=False):
            return DVE.put(lambda e: e.tensor_reduce(o, a, AX.X, op, negate=neg), w)

        def rec(o, a, w=()):
            return DVE.put(lambda e: e.reciprocal(o, a), w)

        def f32(a):
            return a.bitcast(F32)

        def split(hi, lo, src, w, q=None):
            h = act(hi, src, ACT.Copy, w)
            return [h, tt(lo, src, f32(hi), ALU.subtract, [h], q=q)]

        def mset(o, v, w=(), q=None):
            return (q or DVE).put(lambda e: e.memset(o, v), w)

        def act(o, a, f, w=(), bias=0.0, scale=1.0, acc=None):
            if f == ACT.Copy:
                return SC.put(lambda e: e.activation(o, a, f, scale=scale), w)
            if acc is not None:
                return SC.put(lambda e: e.activation(o, a, f, bias=bias, scale=scale, accum_out=acc), w)
            return SC.put(lambda e: e.activation(o, a, f, bias=bias, scale=scale), w)

        def load(o, i, w=(), sem=None):
            s = sem or new_sem(f"ld{len(loads)}")
            loads.append(s)
            SC.dma(lambda e: e.dma_start(o, i), w, s)
            return (s, 16)

        loads = []

        def fence():
            marks = [q.count.last() for q in (PE, DVE, SC, PO)]
            for q in (PE, DVE, SC, PO):
                q.pending = list(marks)

        stream, order, halves, hl_free = [], [], {}, {}
        ring_sem = [new_sem(f"ring{n}") for n in range(NR)]
        lo_q = [DVE]

        def raw(n):
            return RINGt[:, (n % NR) * 1024:(n % NR + 1) * 1024], (ring_sem[n % NR], 16 * (n // NR + 1))

        def convert(n):
            name, c, q = plan[n]
            if name in WHOLE or n in halves:
                return
            b = c % NHL
            hi, lo = HIt[:, b * 1024:b * 1024 + 1024], LOt[:, b * 1024:b * 1024 + 1024]
            w, m = raw(n)
            fr = hl_free.get(c - NHL)
            a = SC.put(lambda e: e.activation(hi, w, ACT.Copy), [m, fr], aside=True)
            l = (PO if q else DVE).put(lambda e: e.tensor_tensor(lo, w, f32(hi), ALU.subtract), [m, a, fr],
                                       aside=True)
            halves[n] = (hi, lo, a, l)
            raw_free[n] = l

        raw_free = {}

        def take(name, idx):
            n = len(stream)
            stream.append(ins[name][idx])
            c = sum(order_count)
            order.append((name, c, lo_q[0] is PO))
            if name in WHOLE:
                return raw(n) + (n,)
            order_count[0] += 1
            if plan is None:
                return HIt[:, 0:1024], LOt[:, 0:1024], None, None, n
            for k in range(n, min(n + AHEAD + 1, len(plan))):
                convert(k)
            return halves[n] + (n,)

        order_count = [0]

        def give(n, mark):
            if order[n][0] in WHOLE:
                raw_free[n] = mark
            else:
                hl_free[order[n][1]] = mark

        idle = [4, 5, 6, 7]

        class Free(dict):
            def __setitem__(self, n, mark):
                dict.__setitem__(self, n, mark)
                if n >= 4 and n not in idle:
                    idle.append(n)

        free = Free({n: None for n in range(8)})

        def bank():
            n = idle.pop(0)
            return n, banks[n][:, :], free[n]

        sturn = [0]

        def stat(n):
            if sturn[0] + n > 256:
                sturn[0] = 0
            a = STAT[:, sturn[0]:sturn[0] + n]
            sturn[0] += n
            return a

        SP_c = new_sem("pack")
        SP.dma(lambda e: e.dma_start(CSTt[:, :], ins["pack"]), (), SP_c)
        m_pack = (SP_c, 16)
        s_x = new_sem("x")
        for t in range(2):
            SC.dma(lambda e, t=t: e.dma_start(X[:, t, :], ins["x"][t]), (), s_x)
        for q in (PE, DVE, SC, PO):
            q.pending = [m_pack]
        preload = {}
        m_x = [(s_x, 32)] * 2

        sc_m = [None]
        silu_c = MOD[:, 64:72]
        acc_free = [None]
        s_ab = new_sem("ab")
        n_ab = [0]
        mod_done = {}
        bg = []

        def ada_piece(p):
            state = {}

            def first():
                m = mset(ACCt[:, :], 0.0, [acc_free[0]], q=PO)
                n_ab[0] += 1
                PO.dma(lambda e: e.dma_start(ACCt[0:1, :], ins["adab"][p]), [m], s_ab)
                state["m"] = (s_ab, 16 * n_ab[0])

            def slot(k):
                def run():
                    w, m, n = take("ada", p * 8 + k)
                    state["m"] = stt(ACCt[:, :], w, silu_c[:, k:k + 1], ACCt[:, :], ALU.mult, ALU.add,
                                     [m, state["m"], sc_m[0]])
                    give(n, state["m"])
                return run

            def last():
                l, kind = divmod(p, 6)
                n, ps, fr = bank()
                if kind in (2, 5):
                    for hf in range(2):
                        if hf:
                            n, ps, fr = bank()
                        m = mm(ps, C("ones"), ACCt[:, hf * 512:hf * 512 + 512], True, True, [fr, state["m"]])
                        acc_free[0] = m
                        free[n] = act(GB[0][:, hf * 512:hf * 512 + 512], ps, ACT.Copy, [m])
                    mod_done[p] = free[n]
                    return
                for k in range(8):
                    m = mm(ps[:, k:k + 1], ACCt[:, k * 128:k * 128 + 128], C("ones")[:, 0:1], True, True,
                           [fr, state["m"]])
                acc_free[0] = m
                half = kind // 3
                place = MOD[:, 16 * (2 * (l % 2) + half):][:, 0:16]
                if kind % 3 == 0:
                    mod_done[p] = free[n] = copy(place[:, 8:16], ps[:, 0:8], [m])
                else:
                    g = C("normg", (l * 2 + half) * 8, (l * 2 + half) * 8 + 8)
                    mod_done[p] = free[n] = stt(place[:, 0:8], ps[:, 0:8], 1.0, g, ALU.add, ALU.mult, [m])

            return [first] + [slot(k) for k in range(8)] + [last]

        def background(n=1):
            for _ in range(n):
                if bg:
                    bg.pop(0)()

        XN, HR = 0, 2048
        T00 = 4096

        def make_h(scale, shift, w):
            sts = stat(2)
            xn = A(XN, 2048).rearrange("p (t n) -> p t n", t=2)
            for t in range(2):
                m = act(xn[:, t, :], X[:, t, :], ACT.Square, [m_x[t], w], acc=sts[:, t:t + 1])
            m = ts(sts, sts, 1.0 / 1024, EPS, ALU.mult, ALU.add, [m], q=PO)
            r = stat(2)
            m = tt(r, sts, NH(2), ALU.pow, [m], q=PO)
            mt = [act(xn[:, 0, :], X[:, 0, :], ACT.Copy, [m], scale=r[:, 0:1]),
                  ts(xn[:, 1, :], X[:, 1, :], r[:, 1:2], None, ALU.mult, w=[m])]
            out = []
            for k2 in range(4):
                n, ps, fr = bank()
                for kk in range(2):
                    k = 2 * k2 + kk
                    for t in range(2):
                        m = tp(ps[:, kk * 256 + t * 128:][:, 0:128], xn[:, t, k * 128:k * 128 + 128], [fr, mt[t]])
                raw2 = A(HR + 512 * k2, 512).rearrange("p (k t) -> p k t", k=2)
                for kk in range(2):
                    k = 2 * k2 + kk
                    src, dst = ps[:, kk * 256:kk * 256 + 256], raw2[:, kk, :]
                    if k2 % 2 and shift is None:
                        a = act(dst, src, ACT.Copy, [m, w], scale=scale[:, k:k + 1])
                    elif k2 % 2:
                        a = act(dst, src, ACT.Identity, [m, w], scale=scale[:, k:k + 1], bias=shift[:, k:k + 1])
                    elif shift is None:
                        a = ts(dst, src, scale[:, k:k + 1], None, ALU.mult, w=[m, w])
                    else:
                        a = ts(dst, src, scale[:, k:k + 1], shift[:, k:k + 1], ALU.mult, ALU.add, w=[m, w])
                free[n] = a
                out.append(split(HT[0][:, 2 * k2:2 * k2 + 2, :], HT[1][:, 2 * k2:2 * k2 + 2, :], raw2, [a]))
            return [[o[0] for o in out], [o[1] for o in out]]

        def project(name, idx, mh):
            wh, wl, mh_, ml_, s = take(name, idx)
            n, ps, fr = bank()
            for i, (w, mw, h) in enumerate(((wh, mh_, 0), (wh, mh_, 1), (wl, ml_, 0))):
                for k in range(8):
                    mk = mm(ps[:, 0:256], w[:, k * 128:k * 128 + 128], HT[h][:, k, :], i == 0 and k == 0,
                            i == 2 and k == 7, [fr, mw, mh[h]])
            give(s, mk)
            return n, ps[:, 0:256], mk

        def rows_slot(k, nslots, wt, lhs, w):
            wh, wl, mh_, ml_, s = wt
            for i, (v, mw, h) in enumerate(((wh, mh_, 0), (wh, mh_, 1), (wl, ml_, 0))):
                for t in range(2):
                    for hf in range(2):
                        last = i == 2 and k == nslots - 1
                        mk = mm(Y[2 * t + hf], lhs[h][:, t * 128:t * 128 + 128], v[:, hf * 512:hf * 512 + 512],
                                i == 0 and k == 0, last,
                                [mw, w] + ([free[2 * t + hf]] if i == 0 and k == 0 else []), inc=i == 2)
            give(s, mk)
            return mk

        def rows_out(name, nslots, lhs, w, yfree):
            for k in range(nslots):
                mk = rows_slot(k, nslots, take(name, k), lhs(k), w(k))
                background()
            return mk

        def rows512(name, w):
            for s4 in range(4):
                wh, wl, mh_, ml_, s = take(name, s4)
                for i, (v, mw, h) in enumerate(((wh, mh_, 0), (wh, mh_, 1), (wl, ml_, 0))):
                    for kk in range(2):
                        for t in range(2):
                            k = 2 * s4 + kk
                            mk = mm(Y[t], HT[h][:, k, t * 128:t * 128 + 128], v[:, kk * 512:kk * 512 + 512],
                                    k == 0 and i == 0, k == 7 and i == 2, [mw, w, free[t]], inc=i == 2)
                give(s, mk)
            return mk

        def ht(k):
            return [HT[0][:, k, :], HT[1][:, k, :]]

        later = []

        def run_later(keep=0):
            while len(later) > keep:
                later.pop(0)()

        def head_norm(n, ps, m, dst, gcol, sq, rr, marks, key, w=None):
            a = act(dst, ps, ACT.Copy, [m, w])
            b = act(sq, ps, ACT.Square, [m, w, sq_free.get(id(sq))])
            free[n] = b

            def rest():
                n2, p2, fr = bank()
                mk = mm(p2[:, 0:256], C("bd64"), sq, True, True, [fr, b])
                sq_free[id(sq)] = mk
                c = ts(rr, p2[:, 0:256], 1.0 / 64, EPS, ALU.mult, ALU.add, w=[mk, rr_free.get(id(rr))])
                free[n2] = c
                d = rec(rr, rr, [act(rr, rr, ACT.Sqrt, [c])])
                marks[key] = stt(dst, dst, gcol, rr, ALU.mult, ALU.mult, [d, a])
                rr_free[id(rr)] = marks[key]
            later.append(rest)

        sq_free, rr_free = {}, {}

        def log1p_exp(o, x, t1, t2, t3, w):
            m = act(t1, x, ACT.Abs, w)
            m = act(t1, t1, ACT.Exp, [m], scale=-1.0)
            m = ts(t2, t1, 2.0, None, ALU.add, w=[m])
            m = rec(t2, t2, [m])
            m = tt(t1, t1, t2, ALU.mult, [m])
            m = tt(t2, t1, t1, ALU.mult, [m])
            m = ts(t3, t2, 2.0 / 17, 2.0 / 15, ALU.mult, ALU.add, w=[m])
            for c in (13, 11, 9, 7, 5, 3, 1):
                m = tt(t3, t3, t2, ALU.mult, [m])
                m = ts(t3, t3, 2.0 / c, None, ALU.add, w=[m])
            return tt(o, t3, t1, ALU.mult, [m])

        class Heads:
            def __init__(self, base, nb=3):
                self.S = [A(base + n * 384, 384) for n in range(nb)]
                self.P = [A(base + (nb + n) * 384, 384) for n in range(nb)]
                self.sf, self.pf, self.nb, self.i = [None] * nb, [None] * nb, nb, 0
                self.q = []
                self.rows, self.next = [], None

            def more(self, flush=False):
                if self.rows and (flush or self.i > self.rows[0][1]):
                    k = self.rows.pop(0)[0]
                    name, n, cat_, marks = self.next
                    self.mk = rows_slot(k, n, take(name, k), [cat_[0][:, k, :], cat_[1][:, k, :]], marks[k])
                    background()

            def add(self, scores, mask, v, dst, gate=None, mult=None, wmask=None):
                r = self.i % self.nb
                self.i += 1
                S, P = self.S[r], self.P[r]
                n, ps, fr = bank()
                m = scores(ps, fr)
                st = stat(6)
                m = tt(S, ps[:, 0:384], mask, ALU.add, [m, self.sf[r], wmask])
                free[n] = m
                red(st[:, 0:1], S[:, 0:128], ALU.max, [m], neg=True)
                m = red(st[:, 1:2], S[:, 128:384], ALU.max, [m], neg=True)
                for i, (a, b) in enumerate(((0, 128), (128, 384))):
                    m2 = act(S[:, a:b], S[:, a:b], ACT.Exp, [m], bias=st[:, i:i + 1],
                             acc=None if mult is not None else st[:, 2 + i:3 + i])
                m = m2
                if mult is not None:
                    for i, (a, b) in enumerate(((0, 128), (128, 384))):
                        o, c, u = S[:, a:b], mult[:, a:b], st[:, 2 + i:3 + i]
                        m = DVE.put(lambda e, o=o, c=c, u=u: e.tensor_tensor_reduce(
                            o, o, c, 1.0, 0.0, ALU.mult, ALU.add, u), [m2])
                m = rec(st[:, 4:6], st[:, 2:4], [m])
                if gate is not None:
                    m = tt(st[:, 4:6], st[:, 4:6], gate[0], ALU.mult, [m, gate[1]])
                ts(S[:, 0:128], S[:, 0:128], st[:, 4:5], None, ALU.mult, w=[m], q=PO)
                m = ts(S[:, 128:384], S[:, 128:384], st[:, 5:6], None, ALU.mult, w=[m], q=PO)
                self.q.append([0, r, S, P, m, v, dst])
                self.step()
                self.more()

            def step(self, flush=False):
                while self.q and self.q[0][0] == 1 and (flush or len(self.q) > 2):
                    self.pv(self.q.pop(0))
                for e in self.q:
                    if e[0] == 0 and (flush or e is not self.q[-1]):
                        self.turn(e)
                if flush:
                    while self.q:
                        self.pv(self.q.pop(0))
                    while self.rows:
                        self.more(True)

            def turn(self, e):
                _, r, S, P, m, v, dst = e
                n, ps, fr = bank()
                for c in range(3):
                    mk = tp(ps[:, c * 128:c * 128 + 128], S[:, c * 128:c * 128 + 128], [fr, m])
                self.sf[r] = mk
                e[4] = act(P, ps[:, 0:384], ACT.Copy, [mk, self.pf[r]])
                free[n] = e[4]
                e[0] = 1

            def pv(self, e):
                _, r, S, P, m, v, dst = e
                odd, w, first, last, after = dst
                if not odd and first:
                    self.ob = bank()
                pr = slice(64 * odd, 64 * odd + 64)
                o = self.ob[1][pr, 0:256]
                w = [w, self.ob[2]]
                mm(o, v(0), P[:, 0:256], first, False, [m, w], inc=False)
                mk = mm(o[:, 128:256], v(1), P[:, 256:384], False, last, [m], inc=True)
                self.pf[r] = mk
                if after is not None:
                    after(mk, self.ob[0], self.ob[1], o)

        def residual(scale, gated, wy, w=None):
            for t in range(2):
                for hf in range(2):
                    x = X[:, t, hf * 512:hf * 512 + 512]
                    y = Y[2 * t + hf]
                    if gated:
                        tmp = A(XN + (2 * t + hf) * 512, 512)
                        m = tt(tmp, y, GB[0][:, hf * 512:hf * 512 + 512], ALU.mult, [wy, w])
                        free[2 * t + hf] = m
                        m = tt(x, x, tmp, ALU.add, [m, m_x[t]])
                    else:
                        m = stt(x, y, scale, x, ALU.mult, ALU.add, [wy, m_x[t]])
                        free[2 * t + hf] = m
                m_x[t] = m

        def fox():
            _, *fr_ = scope("fox", ("a", 20000, F32), ("h", 2048, F32R), ("l", 2048, F32R))
            local["causal"] = A(T00 + 9800 - 0, 384) if False else A(19000, 384)
            GB[0] = A(17900, 1024)
            mods = MOD[:, 0:16]
            mca = load(C("causal"), ins["causal"])
            mh = make_h(mods[:, 0:8], mods[:, 8:16], [mod_done[0], mod_done[1]])
            CAT = [f[:, :].rearrange("p (c t) -> p c t", c=8) for f in fr_]
            QT = A(T00 + 2048, 1024).rearrange("p (c t) -> p c t", c=4)
            KT = A(T00 + 3072, 1024).rearrange("p (c t) -> p c t", c=4)
            V = A(T00 + 4096, 1024).rearrange("p (b n) -> p b n", b=2)
            U = [A(T00 + 5120 + 258 * n, 258) for n in range(2)]
            CC = [A(T00 + 5640 + 256 * n, 256) for n in range(2)]
            T0 = [A(T00 + 6152 + 256 * n, 256) for n in range(2)]
            SQ = [A(T00 + 6664 + 256 * n, 256) for n in range(2)]
            RR = [A(T00 + 7176 + 256 * n, 256) for n in range(2)]
            FL, FR = A(T00 + 7688, 256), A(T00 + 7944, 256)
            RH = [A(T00 + 8200 + 256 * n, 256) for n in range(2)]
            F = [A(T00 + 8712 + 256 * n, 256) for n in range(4)]
            cat, qk = {}, {}
            ms = [mset(U[n][:, 0:2], 0.0) for n in range(2)]
            gq = stat(1)
            mg = ts(gq, C("foxqg"), 0.125, None, ALU.mult)
            for j in range(4):
                b = j % 2
                n, ps, m = project("foxst", 3 * j, mh)
                mc = free[n] = act(CC[b], ps, ACT.Copy, [m, cat.get(j - 2)])
                n, ps, m = project("foxst", 3 * j + 1, mh)
                mu = free[n] = tt(U[b][:, 2:258], ps, CC[b], ALU.mult, [m, mc, ms[b], cat.get(j - 2)])
                cw = C("convw", 3 * j, 3 * j + 3)
                m1 = ts(T0[b], U[b][:, 0:256], cw[:, 0:1], None, ALU.mult, w=[mu, cat.get(j - 2)])
                m1 = stt(T0[b], U[b][:, 1:257], cw[:, 1:2], T0[b], ALU.mult, ALU.add, [m1])
                m1 = stt(T0[b], U[b][:, 2:258], cw[:, 2:3], T0[b], ALU.mult, ALU.add, [m1])
                n, ps, m = project("foxst", 3 * j + 2, mh)
                m1 = free[n] = tt(T0[b], ps, T0[b], ALU.mult, [m, m1])
                cat[j] = split(CAT[0][:, j, :], CAT[1][:, j, :], T0[b], [m1])
                background()
            for j in range(8):
                n, ps, m = project("foxst", 12 + j, mh)
                run_later()
                dst = QT[:, j, :] if j < 4 else KT[:, j - 4, :]
                head_norm(n, ps, m, dst, gq if j < 4 else C("foxkg"), SQ[j % 2], RR[j % 2], qk, j, [mg])
                background(2)
            n, ps, m = project("foxf", 0, mh)
            run_later()
            m = free[n] = ts(F[0], ps, C("bf"), None, ALU.add, w=[m])
            m = log1p_exp(F[1], F[0], F[2], F[3], FR, [m])
            m = stt(F[1], F[0], 0.0, F[1], ALU.min, ALU.subtract, [m])
            m2 = mset(F[3], 1.0, [m])
            m = DVE.put(lambda e: e.tensor_tensor_scan(F[2], F[3], F[1], 0.0, ALU.mult, ALU.add), [m, m2])
            mF = []
            for q in (0, 64):
                mF.append(copy(FL[q:q + 32, :], F[2][q:q + 32, :], [m]))
                mF.append(mset(FL[q + 32:q + 64, :], 1.0))
                mF.append(mset(FR[q:q + 32, :], 1.0, [m]))
                mF.append(ts(FR[q + 32:q + 64, :], F[2][q + 32:q + 64, :], -1.0, None, ALU.mult, w=[m]))
            m = rows512("foxv", mh)
            mv = []
            for t in range(2):
                mk = act(V[:, t, :], Y[t], ACT.Copy, [m])
                free[t] = mk
                mv.append(mk)
            H = Heads(T00 + 10000)
            H.next = ("foxo", 8, CAT, cat)
            H.rows = [(k, 1 + k) for k in range(4)]
            rh_free = [None, None]
            for h in range(8):
                pr = slice(64 * (h % 2), 64 * (h % 2) + 64)
                r = RH[h % 2][pr, :]
                mr = ts(r, FR[pr, :], C("headsel")[pr, h:h + 1], None, ALU.mult, w=[mF, rh_free[h % 2]])

                def scores(ps, fr, h=h, pr=pr, r=r, mr=mr):
                    w = [fr, qk[h // 2], qk[4 + h // 2]]
                    mm(ps[:, 0:128], QT[pr, h // 2, 0:128], KT[pr, h // 2, 0:128], True, False, w, inc=False)
                    mm(ps[:, 0:128], FL[pr, 0:128], r[:, 0:128], False, True, [mr, mF], inc=False)
                    mm(ps[:, 128:384], QT[pr, h // 2, 128:256], KT[pr, h // 2, :], True, False, inc=False)
                    m = mm(ps[:, 128:384], FL[pr, 128:256], r, False, True)
                    rh_free[h % 2] = m
                    return m

                after = None
                if h % 2:
                    def after(mk, n, ps, o, h=h):
                        cat[4 + h // 2] = free[n] = split(CAT[0][:, 4 + h // 2, :], CAT[1][:, 4 + h // 2, :],
                                                          ps[:, 0:256], [mk])
                        H.rows.append((4 + h // 2, H.i + 1))
                H.add(scores, C("causal"), lambda kb, h=h: V[:, kb, h * 64:h * 64 + 64],
                      (h % 2, mv, True, True, after), wmask=mca)
            H.step(True)
            mk = H.mk
            while bg:
                background()
            residual(1.0, True, mk, w=[mod_done[2]])

        def nsa():
            mods = MOD[:, 32:48]
            _, *fr_ = scope("nsa", ("a", 30000, F32), ("h", 2048, F32R), ("l", 2048, F32R))
            CAT = [f[:, :].rearrange("p (c t) -> p c t", c=8) for f in fr_]
            GB[0] = A(T00, 1024)
            local["causal"] = A(T00 + 1024, 384)
            local["cmpok"], local["cmpneg"] = A(T00 + 1408, 120), A(T00 + 1528, 120)
            QT = A(T00 + 2048, 2048).rearrange("p (c t) -> p c t", c=8)
            KK = [A(T00 + 4096 + 512 * n, 512).rearrange("p (c t) -> p c t", c=2) for n in range(4)]
            V = A(T00 + 6144, 1024).rearrange("p (b n) -> p b n", b=2)
            Z = [A(T00 + 7168 + 960 * n, 960) for n in range(2)]
            TB = A(T00 + 9088, 6144).rearrange("p (h k) -> p h k", h=16)
            CB = A(T00 + 15232, 480)
            G3 = A(T00 + 15712, 96).rearrange("p (t n) -> p t n", t=2)
            GS = A(T00 + 15808, 256)
            SQ = [A(T00 + 16064 + 256 * n, 256) for n in range(2)]
            RR = [A(T00 + 16576 + 256 * n, 256) for n in range(2)]
            HB = A(T00 + 17088, 128)
            KC = A(T00 + 17216, 64)
            H1R = A(T00 + 17280, 512)
            VC = A(T00 + 22400, 1024).rearrange("p (g j d) -> p g j d", g=4, j=4)
            PC = [A(T00 + 18048 + 256 * n, 256) for n in range(2)]
            PCT = A(T00 + 18560, 1024).rearrange("p (g t) -> p g t", g=4)
            mca = load(C("causal"), ins["causal"])
            mca = [mca, load(C("cmpok"), ins["cmpok"]), load(C("cmpneg"), ins["cmpneg"])]
            mtb = load(TB, ins["toep"].rearrange("p (h k) -> p h k", h=16))
            mcb = load(CB, ins["cmpb"])
            mh = make_h(mods[:, 0:8], mods[:, 8:16], [mod_done[6], mod_done[7]])
            z1 = mset(H1R, 0.0)
            z2 = [mset(PC[n], 0.0) for n in range(2)]
            ca = C("causal").unsqueeze(1).broadcast_to([128, 16, 384])
            mtb = tt(TB, TB, ca, ALU.add, [mtb, mca], q=PO)
            cn = C("cmpneg").unsqueeze(1).broadcast_to([128, 4, 120])
            cb4 = CB.rearrange("p (g n) -> p g n", g=4)
            mcb = tt(cb4, cb4, cn, ALU.add, [mcb, mca], q=PO)
            gq = stat(1)
            mg = ts(gq, C("nsaqg"), 0.125, None, ALU.mult)
            mz = []
            for j in range(8):
                n, ps, m = project("nsac", j, mh)
                kv, g = divmod(j, 4)
                zz = Z[kv].rearrange("p (l g n) -> p l g n", l=16, g=4)
                for par in range(2):
                    pp = slice(64 * par, 64 * par + 64)
                    src = bass_window(ps, pp, par)
                    po = C("pos", 16 * kv, 16 * kv + 16)[pp, :].unsqueeze(2).broadcast_to([64, 16, 15])
                    mk = tt(zz[pp, :, g, :], src, po, ALU.add, [m])
                free[n] = mk
                mz.append(mk)
            n, ps, m = project("nsag", 0, mh)
            m = free[n] = act(GS[0:48, :], ps[0:48, :], ACT.Sigmoid, [m], bias=C("bgate")[0:48, :])
            n, ps, fr = bank()
            for t in range(2):
                mk = tp(ps[:, t * 64:t * 64 + 48], GS[0:48, t * 128:t * 128 + 128], [fr, m], n=48)
            mgate = None
            for t in range(2):
                mgate = free[n] = copy(G3[:, t, :], ps[:, t * 64:t * 64 + 48], [mk])
            qk, kn = {}, {}
            for j in range(8):
                n, ps, m = project("nsaq", j, mh)
                run_later()
                head_norm(n, ps, m, QT[:, j, :], gq, SQ[j % 2], RR[j % 2], qk, j, [mg])
            for j in range(4):
                n, ps, m = project("nsak", j, mh)
                run_later()
                head_norm(n, ps, m, KK[2 * (j // 2)][:, j % 2, :], C("nsakg", 1 + j // 2, 2 + j // 2),
                          SQ[j % 2], RR[j % 2], kn, j)
            for kv in range(2):
                w, mw, s = take("nsaw1", kv)
                n, ps, fr = bank()
                for l in range(16):
                    mk = mm(ps[0:64, 0:60], w[:, l * 64:l * 64 + 64], Z[kv][:, l * 60:l * 60 + 60], l == 0, l == 15,
                            [fr, mw, mz[4 * kv + 3]])
                give(s, mk)
                if kv == 0:
                    run_later()
                    m = free[n] = act(HB[0:64, 0:60], ps[0:64, 0:60], ACT.Gelu_apprx_tanh, [mk])
                    n, ps, fr = bank()
                    m = mm(ps[:, 0:60], C("w2k")[0:64, :], HB[0:64, 0:60], True, True, [fr, m])
                    a = act(KC[:, 0:60], ps[:, 0:60], ACT.Copy, [m])
                    b = free[n] = act(SQ[0][:, 0:60], ps[:, 0:60], ACT.Square, [m, sq_free.get(id(SQ[0]))])
                    n, ps, fr = bank()
                    m = mm(ps[:, 0:60], C("bd64"), SQ[0][:, 0:60], True, True, [fr, b])
                    c = free[n] = ts(RR[0][:, 0:60], ps[:, 0:60], 1.0 / 64, EPS, ALU.mult, ALU.add,
                                     w=[m, rr_free.get(id(RR[0]))])
                    c = rec(RR[0][:, 0:60], RR[0][:, 0:60], [act(RR[0][:, 0:60], RR[0][:, 0:60], ACT.Sqrt, [c])])
                    mkc = stt(KC[:, 0:60], KC[:, 0:60], C("nsakg", 0, 1), RR[0][:, 0:60], ALU.mult, ALU.mult, [a, c])
                else:
                    m = free[n] = act(HB[0:64, 64:124], ps[0:64, 0:60], ACT.Gelu_apprx_tanh, [mk])
                    h1 = H1R[0:64, :].rearrange("p (g j n) -> p g j n", g=4, j=4)
                    for g in range(4):
                        m2 = copy(h1[:, g, :, 0:15],
                                  HB[0:64, 64 + 15 * g:79 + 15 * g].unsqueeze(1).broadcast_to([64, 4, 15]), [m, z1])
                    n, ps, fr = bank()
                    for g in range(4):
                        m = mm(ps[:, g * 64:g * 64 + 64], H1R[0:64, g * 128:g * 128 + 128], C("w2v")[0:64, :], True,
                               True, [fr, m2])
                    for j in range(4):
                        mvc = free[n] = ts(VC[:, :, j, :], ps[:, 0:256].rearrange("p (g d) -> p g d", g=4),
                                           C("rowsel")[:, j:j + 1], None, ALU.mult, w=[m])
            msw = []
            s_sw = new_sem("swap")
            for n in range(2):
                for hf in range(2):
                    o = KK[2 * n + 1][64 * hf:64 * hf + 64, :, :]
                    i = KK[2 * n][64 - 64 * hf:128 - 64 * hf, :, :]
                    PO.dma(lambda e, o=o, i=i: e.dma_start(o, i), [kn[2 * n], kn[2 * n + 1]], s_sw)
            msw = (s_sw, 64)
            m = rows512("nsav", mh)
            mv = []
            for t in range(2):
                mk = act(V[:, t, :], Y[t], ACT.Copy, [m])
                free[t] = mk
                mv.append(mk)
            mpc = {}
            pcf = [z2[0], z2[1]]
            for g in range(4):
                sc = A(T00 + 19600 + 128 * (g % 2), 120).rearrange("p (j n) -> p j n", n=15)
                sc3 = A(T00 + 19600 + 128 * (g % 2), 120).rearrange("p (t j n) -> p t j n", t=2, n=15)
                cb3 = CB[:, g * 120:g * 120 + 120].rearrange("p (t j n) -> p t j n", t=2, n=15)
                ma = []
                for odd in range(2):
                    pr = slice(64 * odd, 64 * odd + 64)
                    n, ps, fr = bank()
                    for j in range(2):
                        for t in range(2):
                            m = mm(ps[:, (t * 2 + j) * 16:][:, 0:15], QT[pr, 2 * g + j, t * 128:t * 128 + 128],
                                   KC[pr, 15 * g:15 * g + 15], True, True, [fr, mkc, qk[7]])
                    pv = ps[:, 0:64].rearrange("p (t j n) -> p t j n", t=2, n=16)[:, :, :, 0:15]
                    free[n] = tt(sc3[:, :, odd:4:2, :], pv, cb3[:, :, odd:4:2, :], ALU.add, [m, mcb])
                    ma.append(free[n])
                m = ma
                s8 = stat(16)
                mx, sm = s8[:, 0:8], s8[:, 8:16]
                m = red(mx, sc, ALU.max, [m], neg=True)
                m = tt(sc, sc, mx.unsqueeze(2).broadcast_to([128, 8, 15]), ALU.add, [m])
                m = act(sc, sc, ACT.Exp, [m])
                m = red(sm, sc, ALU.add, [m])
                m = rec(sm, sm, [m])
                gt = G3[:, :, 12 * g:12 * g + 12].rearrange("p t (j c) -> p t j c", c=3)[:, :, :, 0]
                m = tt(sm.rearrange("p (t j) -> p t j", t=2), sm.rearrange("p (t j) -> p t j", t=2), gt, ALU.mult,
                       [m, mgate])
                m = tt(sc, sc, sm.unsqueeze(2).broadcast_to([128, 8, 15]), ALU.mult, [m])
                pc = PC[g % 2].rearrange("p (j n) -> p j n", n=32)[:, :, 0:15]
                m = tt(pc, sc, C("cmpok").rearrange("p (j n) -> p j n", n=15), ALU.mult, [m, pcf[g % 2]])
                n, ps, fr = bank()
                for t in range(2):
                    mk = tp(ps[:, t * 128:t * 128 + 128], PC[g % 2][:, t * 128:t * 128 + 128], [fr, m])
                pcf[g % 2] = mk
                mpc[g] = free[n] = act(PCT[:, g, :], ps[:, 0:256], ACT.Copy, [mk])
            H = Heads(T00 + 20000)
            cat = {}
            H.next = ("nsao", 8, CAT, cat)
            for h in range(16):
                g, j = divmod(h, 4)
                pr = slice(64 * (h % 2), 64 * (h % 2) + 64)
                for b in range(2):
                    src = KK[2 * b + (0 if g % 2 == h % 2 else 1)]

                    def scores(ps, fr, h=h, pr=pr, src=src, g=g, b=b):
                        w = [fr, qk[h // 2], kn[2 * b + g // 2], msw]
                        mm(ps[:, 0:128], QT[pr, h // 2, 0:128], src[pr, g // 2, 0:128], True, True, w, inc=False)
                        return mm(ps[:, 128:384], QT[pr, h // 2, 128:256], src[pr, g // 2, :], True, True)

                    after = None
                    if b == 1:
                        def after(mk, n, ps, o, h=h, g=g, j=j):
                            m = mm(o, VC[:, g, j, :], PCT[:, g, :], False, True, [mpc[g], mvc])
                            if h % 2:
                                cat[h // 2] = free[n] = split(CAT[0][:, h // 2, :], CAT[1][:, h // 2, :],
                                                              ps[:, 0:256], [m])
                                H.rows.append((h // 2, H.i + 1))
                    gt = G3[:, :, 3 * h + 1 + b]
                    H.add(scores, TB[:, h, :], lambda kb, g=g, b=b: V[:, kb, b * 256 + g * 64:b * 256 + g * 64 + 64],
                          (h % 2, mv, b == 0, False, after), gate=(gt, mgate), wmask=mtb)
            H.step(True)
            mk = H.mk
            while bg:
                background()
            residual(1.0, True, mk, w=[mod_done[8]])

        def bass_window(ps, pp, par):
            base = ps[pp, par:par + 1]
            return bass.AP(base.tensor, base.offset, [base.ap[0], [2, 16], [16, 15]])

        def peer(l):
            p0 = 6 * l
            mods = MOD[:, 16 * (2 * l + 1):16 * (2 * l + 1) + 16]
            _, TIJt, OHt, WHt, WLt = scope(f"peer{l}", ("a", 32768, F32), ("tij", 768, F32), ("oh", 512, F32),
                                           ("wh", 512, F32R), ("wl", 512, F32R))
            B = 16384
            KEYS = A(B, 256)
            mkey = load(KEYS, ins[f"keys{l}"])
            QT = A(T00, 2048).rearrange("p (c t) -> p c t", c=8)
            mh = make_h(mods[:, 0:8], mods[:, 8:16], [mod_done[p0 + 3], mod_done[p0 + 4]])
            qd = {}
            lo_q[0] = PO
            for j in range(8):
                n, ps, m = project(f"pq{l}", j, mh)
                qd[j] = free[n] = act(QT[:, j, :], ps, ACT.Copy, [m])
            SB = [A(T00 + 2048 + 2048 * t, 2048) for t in range(2)]
            EQ = A(0, 2048).rearrange("p (k a) -> p k a", a=16)
            E2 = A(2048, 2048).rearrange("p (k a) -> p k a", a=16)
            SI = A(10240, 512).bitcast(U32)
            SV = A(10752, 512)
            SF = A(11264, 512)
            CV = A(11776, 256)
            CI = A(12032, 256).bitcast(U32)
            CA, CBf = A(12288, 256), A(12544, 256)
            CU = A(12800, 256).bitcast(U32)
            EI = A(13056, 256)
            EJ = A(13312, 256)
            GG = A(13568, 256)
            TI = [TIJt[:, 256 * n:256 * n + 256] for n in range(3)]
            ms = {}
            for t in range(2):
                for hp in range(4):
                    n, ps, fr = bank()
                    for h in range(2):
                        m = mm(ps[:, h * 256:h * 256 + 256], QT[:, 2 * hp + h, t * 128:t * 128 + 128], KEYS,
                               True, True, [fr, qd[2 * hp + h], mkey])
                    S = SB[t].rearrange("p (s k) -> p s k", s=16)
                    ms[t, hp] = free[n] = act(S[:, 4 * hp:4 * hp + 4, :], ps.rearrange("p (s k) -> p s k", s=4),
                                              ACT.Copy, [m])
            last_key = m

            def top16(src, v, ix, w):
                a, b = v[:, 0:8], v[:, 8:16]
                i0, i1 = ix[:, 0:8], ix[:, 8:16]
                m = DVE.put(lambda e: e.max(a, src), w)
                m = DVE.put(lambda e: e.max_index(i0, a, src), [m])
                m = DVE.put(lambda e: e.match_replace(src, a, src, NEG * 1e6), [m])
                m = DVE.put(lambda e: e.max(b, src), [m])
                return DVE.put(lambda e: e.max_index(i1, b, src), [m])

            def experts(t):
                S = SB[t].rearrange("p (s k) -> p s k", s=16)
                sv = SV[:, 256 * t:256 * t + 256].rearrange("p (s k) -> p s k", s=16)
                si = SI[:, 256 * t:256 * t + 256].rearrange("p (s k) -> p s k", s=16)
                for s in range(16):
                    m = top16(S[:, s, :], sv[:, s, :], si[:, s, :], [ms[t, s // 4]])
                sf = SF[:, 256 * t:256 * t + 256]
                mf = copy(sf, SI[:, 256 * t:256 * t + 256], [m])
                sv4 = sv.rearrange("p (h q) k -> p h q k", q=2)
                CD = SB[t]
                m = tt(CD.rearrange("p (h a b) -> p h a b", h=8, a=16),
                       sv4[:, :, 0, :].unsqueeze(3).broadcast_to([128, 8, 16, 16]),
                       sv4[:, :, 1, :].unsqueeze(2).broadcast_to([128, 8, 16, 16]), ALU.add, [m])
                cv = CV[:, 128 * t:128 * t + 128].rearrange("p (h k) -> p h k", h=8)
                ci = CI[:, 128 * t:128 * t + 128].rearrange("p (h k) -> p h k", h=8)
                mc = m
                for h in range(8):
                    m = top16(CD[:, h * 256:h * 256 + 256], cv[:, h, :], ci[:, h, :], [mc])
                cit, cut = CI[:, 128 * t:128 * t + 128], CU[:, 128 * t:128 * t + 128]
                ca, cb = CA[:, 128 * t:128 * t + 128], CBf[:, 128 * t:128 * t + 128]
                m1 = ts(cut, cit, 4, None, ALU.logical_shift_right, w=[m])
                m1 = copy(ca, cut, [m1])
                m2 = ts(cut, cit, 15, None, ALU.bitwise_and, w=[m1])
                m2 = copy(cb, cut, [m2])
                s4 = sf.rearrange("p (h q k) -> p h q k", h=8, q=2)
                io = C("iota")[:, 0:16].unsqueeze(1).broadcast_to([128, 128, 16])
                for q, (src, dst, eq) in enumerate(((ca, EI, EQ), (cb, EJ, E2))):
                    m = tt(eq, src.unsqueeze(2).broadcast_to([128, 128, 16]), io, ALU.is_equal, [m2])
                    eq4 = eq.rearrange("p (h k) a -> p h k a", h=8)
                    m = tt(eq4, eq4, s4[:, :, q, :].unsqueeze(2).broadcast_to([128, 8, 16, 16]), ALU.mult, [m, mf])
                    me = red(dst[:, 128 * t:128 * t + 128], eq, ALU.add, [m])
                gg = GG[:, 128 * t:128 * t + 128].rearrange("p (h k) -> p h k", h=8)
                return gg, tt(gg, cv, cv[:, :, 0:1].broadcast_to([128, 8, 16]), ALU.subtract, [me])

            def softmax(t, gg, m):
                m = act(gg, gg, ACT.Exp, [m])
                st = stat(8)
                m = red(st, gg, ALU.add, [m])
                m = rec(st, st, [m])
                return tt(gg, gg, st.unsqueeze(2).broadcast_to([128, 8, 16]), ALU.mult, [m])

            def turned(t, mg):
                n, ps, fr = bank()
                for q, src in enumerate((EI, EJ, GG)):
                    mk = tp(ps[:, q * 128:q * 128 + 128], src[:, 128 * t:128 * t + 128], [fr, mg])
                for q in range(3):
                    mti = free[n] = copy(TI[q][:, t * 128:t * 128 + 128], ps[:, q * 128:q * 128 + 128], [mk])
                return mti

            G1 = A(0, B).rearrange("p (t j) -> p t j", j=64)
            G2 = A(B, B).rearrange("p (t j) -> p t j", j=64)
            io = C("iota")
            ohf = [None, None]
            mti = []

            def gates(t4, part, dst, w):
                n, ps, fr = bank()
                for q in range(4):
                    t = 4 * t4 + q
                    b = t % 2
                    o1, o2 = OHt[:, b * 256:b * 256 + 128], OHt[:, b * 256 + 128:b * 256 + 256]
                    a = ts(o1, io, TI[0][:, t:t + 1], None, ALU.is_equal, w=[mti, ohf[b]])
                    c = ts(o2, io, TI[1][:, t:t + 1], TI[2][:, t:t + 1], ALU.is_equal, ALU.mult, w=[mti, ohf[b]])
                    ohf[b] = mm(ps[:, q * 128:q * 128 + 128], o1, o2, True, True, [fr, a, c])
                free[n] = act(dst[:, 4 * t4:4 * t4 + 4, :],
                              ps.rearrange("p (t j) -> p t j", t=4)[:, :, 64 * part:64 * part + 64], ACT.Copy,
                              [ohf[b], w])
                return free[n]

            mge = {}

            def up(j, dst, w):
                n, ps, mk = project(f"pu{l}", j, mh)
                free[n] = act(dst, ps, ACT.Gelu_apprx_tanh, [mk, w])
                return free[n]

            t4 = 0
            for j in range(64):
                mge[j] = up(j, A(B + 256 * j, 256), [last_key])
                if j == 0:
                    me = [experts(0), experts(1)]
                if j == SECOND_T:
                    for t in range(2):
                        mti.append(turned(t, softmax(t, *me[t])))
                if j > SECOND_T:
                    for _ in range(PER_SLOT):
                        if t4 < 64:
                            mg1 = gates(t4, 0, G1, mti)
                            t4 += 1
            while t4 < 64:
                mg1 = gates(t4, 0, G1, mti)
                t4 += 1
            WH = [WHt[:, 256 * n:256 * n + 256] for n in range(2)]
            WL = [WLt[:, 256 * n:256 * n + 256] for n in range(2)]
            wtf, wt_m = [None, None], {}

            def weigh(j, ge, g, w):
                b = j % 2
                m = tt(ge, ge, g, ALU.mult, w)
                h = act(WH[b], ge, ACT.Copy, [m, wtf[b]])
                wt_m[j] = [h, tt(WL[b], ge, f32(WH[b]), ALU.subtract, [h])]

            def down(j):
                b = j % 2
                wtf[b] = rows_slot(j, 128, take(f"pv{l}", j), [WH[b], WL[b]], wt_m[j])
                return wtf[b]

            for j in range(64):
                weigh(j, A(B + 256 * j, 256), G1[:, :, j], [mge[j], mg1])
                if j >= 1:
                    down(j - 1)
                mg2 = gates(j, 1, G2, wt_m[j])
            GB[0] = A(HR, 1024)
            GE = [TIJt[:, 256 * n:256 * n + 256] for n in range(3)]
            gef = [ohf, ohf, ohf]
            for q in (PE, DVE, SC, PO):
                q.pending = q.pending + [wt_m[63], mg2]
            for j in range(64, 128):
                lo_q[0] = DVE
                m = up(j, GE[j % 3], gef[j % 3])
                weigh(j, GE[j % 3], G2[:, :, j - 64], [m, mg2])
                gef[j % 3] = wt_m[j]
                lo_q[0] = PO
                down(j - 1)
                lo_q[0] = DVE
                background()
            lo_q[0] = PO
            mk = down(127)
            lo_q[0] = DVE
            while bg:
                background()
            residual(1.0, True, mk, w=[mod_done[p0 + 5], wt_m[127]])

        def ffn(nm, l):
            _, *fr_ = scope(f"ffn{nm}{l}", ("a", 6000, F32), ("h", 22 * 256, F32R), ("l", 22 * 256, F32R))
            AC = [f[:, :].rearrange("p (c t) -> p c t", c=22) for f in fr_]
            mh = make_h(C(f"fn{'1' if nm == 'A' else '2'}_{l}"), None, None)
            SG = [A(T00 + 256 * n, 256) for n in range(2)]
            ma = {}
            for j in range(22):
                n, ps, m = project(f"fg{nm}{l}", j, mh)
                g = free[n] = act(SG[j % 2], ps, ACT.Silu, [m, ma.get(j - 2)])
                n, ps, m = project(f"fu{nm}{l}", j, mh)
                g = free[n] = tt(SG[j % 2], ps, SG[j % 2], ALU.mult, [m, g])
                ma[j] = split(AC[0][:, j, :], AC[1][:, j, :], SG[j % 2], [g])
            mk = rows_out(f"fd{nm}{l}", 22, lambda k: [AC[0][:, k, :], AC[1][:, k, :]], lambda k: ma[k], None)
            residual(0.5, False, mk)

        def ssd(l):
            _, *fr_ = scope(f"ssd{l}", ("a", 26800, F32), ("h", 4096, F32R), ("l", 4096, F32R))
            CAT = [f[:, :].rearrange("p (c t) -> p c t", c=16) for f in fr_]
            XC = A(0, 4096).rearrange("p (c t) -> p c t", c=16)
            XT = A(4096, 2048).rearrange("p (c n) -> p c n", c=2)
            XD = A(6144, 2048).rearrange("p (c n) -> p c n", c=2)
            ZS = A(8192, 2048).rearrange("p (c n) -> p c n", c=2)
            BT = A(10240, 512)
            ST = A(10752, 1024)
            XE = A(11776, 1024)
            YS = A(12800, 2048).rearrange("p (c n) -> p c n", c=2)
            QT = A(14848, 2048).rearrange("p (c t) -> p c t", c=8)
            KT = A(16896, 2048).rearrange("p (c t) -> p c t", c=8)
            V = A(18944, 2048).rearrange("p (b n) -> p b n", b=2)
            XB = [A(20992 + 260 * n, 259) for n in range(2)]
            T0 = [A(21512 + 256 * n, 256) for n in range(2)]
            SQ = [A(22024 + 256 * n, 256) for n in range(2)]
            RR = [A(22536 + 256 * n, 256) for n in range(2)]
            D = [A(23048 + 256 * n, 256) for n in range(5)]
            local["dilmask"], local["dilmult"] = A(23048, 384), A(23432, 384)
            DT = A(24328, 64)
            EA = A(24392, 32)
            CM = A(20992, 1024)
            mh = make_h(C(f"mixn_{l}"), None, None)
            an = stat(1)
            ma = act(an[0:16, :], C(f"alog_{l}")[0:16, :], ACT.Exp)
            n, ps, m = project(f"sd{l}", 0, mh)
            x = D[0][0:16, :]
            m = free[n] = ts(x, ps[0:16, :], C(f"dtb_{l}")[0:16, :], None, ALU.add, w=[m])
            m = log1p_exp(D[1][0:16, :], x, D[2][0:16, :], D[3][0:16, :], D[4][0:16, :], [m])
            m = stt(D[0][0:16, :], x, 0.0, D[1][0:16, :], ALU.max, ALU.add, [m])
            mdt = ts(D[1][0:16, :], D[0][0:16, :], an[0:16, :], -1.0, ALU.mult, ALU.mult, w=[m, ma])
            mxc = {}
            mz = [mset(XB[n][:, 0:3], 0.0) for n in range(2)]
            for j in range(16):
                b = j % 2
                n, ps, m = project(f"sx{l}", j, mh)
                if j == 0:
                    n2, p2, fr = bank()
                    for q in range(2):
                        for t in range(2):
                            mk = tp(p2[:, (2 * q + t) * 16:][:, 0:16], D[q][0:16, t * 128:t * 128 + 128], [fr, mdt],
                                    n=16)
                    mDT = free[n2] = copy(DT, p2[:, 0:64], [mk])
                mk = free[n] = act(XB[b][:, 3:259], ps, ACT.Copy, [m, mz[b], mxc.get(j - 2)])
                cw, cb = C(f"cw_{l}", 4 * j, 4 * j + 4), C(f"cb_{l}", j, j + 1)
                mk = ts(T0[b], XB[b][:, 0:256], cw[:, 0:1], cb, ALU.mult, ALU.add, w=[mk, mxc.get(j - 2)])
                for k in range(1, 4):
                    mk = stt(T0[b], XB[b][:, k:k + 256], cw[:, k:k + 1], T0[b], ALU.mult, ALU.add, [mk])
                mxc[j] = act(XC[:, j, :], T0[b], ACT.Silu, [mk])
            dt = DT[:, 0:32].rearrange("p (t h) -> p t h", t=2)
            ad = DT[:, 32:64].rearrange("p (t h) -> p t h", t=2)
            m = rows_out(f"sz{l}", 8, ht, lambda k: mh, None)
            for t in range(2):
                for hf in range(2):
                    mzs = free[2 * t + hf] = act(ZS[:, t, hf * 512:hf * 512 + 512], Y[2 * t + hf], ACT.Silu, [m])
            mxt = []
            for t in range(2):
                for c4 in range(2):
                    n, ps, fr = bank()
                    for c in range(4):
                        mk = tp(ps[:, c * 128:c * 128 + 128], XC[:, 4 * c4 + c, t * 128:t * 128 + 128],
                                [fr, mxc[4 * c4 + c]])
                    free[n] = act(XT[:, t, c4 * 512:c4 * 512 + 512], ps, ACT.Copy, [mk])
                    mxt.append(free[n])
            n, ps, fr = bank()
            for c in range(4):
                mk = tp(ps[:, c * 128:c * 128 + 128], XC[:, 8 + c, 0:128], [fr, mxc[11]])
            mbt = free[n] = act(BT, ps, ACT.Copy, [mk])
            mxd = []
            for t in range(2):
                mxd.append(tt(XD[:, t, :].rearrange("p (h e) -> p h e", h=16),
                              XT[:, t, :].rearrange("p (h e) -> p h e", h=16),
                              dt[:, t, :].unsqueeze(2).broadcast_to([128, 16, 64]), ALU.mult, [mxt, mDT]))
            n, ps, fr = bank()
            mm(ps[:, 0:16], C("gt"), ad[:, 0, :], True, True, [fr, mDT])
            m = mm(ps[:, 16:32], C("le"), ad[:, 1, :], True, True)
            mea = free[n] = act(EA, ps[:, 0:32], ACT.Exp, [m])
            mxe = tt(XE.rearrange("p (h e) -> p h e", h=16), XD[:, 0, :].rearrange("p (h e) -> p h e", h=16),
                     EA[:, 0:16].unsqueeze(2).broadcast_to([128, 16, 64]), ALU.mult, [mxd[0], mea], q=PO)
            mcm = {}
            for c in range(2):
                n, ps, fr = bank()
                for g in range(4):
                    mk = mm(ps[:, g * 128:g * 128 + 128], XC[:, 8 + g, c * 128:c * 128 + 128],
                            XC[:, 12 + g, c * 128:c * 128 + 128], True, True, [fr, mxc[15]])
                mcm[c] = free[n] = tt(CM[:, c * 512:c * 512 + 512].rearrange("p (g l) -> p g l", g=4),
                                      ps.rearrange("p (g l) -> p g l", g=4),
                                      C("le").unsqueeze(1).broadcast_to([128, 4, 128]), ALU.mult, [mk])
            for hf in range(2):
                n, ps, fr = bank()
                for q in range(2):
                    g = 2 * hf + q
                    mk = mm(ps[:, q * 256:q * 256 + 256], BT[:, g * 128:g * 128 + 128], XE[:, g * 256:g * 256 + 256],
                            True, True, [fr, mbt, mxe])
                mst = free[n] = act(ST[:, hf * 512:hf * 512 + 512], ps, ACT.Copy, [mk])
            gq = stat(1)
            mg = ts(gq, C(f"dqg_{l}"), 0.125, None, ALU.mult)
            qk, qkj = {}, [0]

            def qk_slot():
                j = qkj[0]
                if j == 16:
                    return
                qkj[0] += 1
                n, ps, m = project(f"sqk{l}", j, mh)
                run_later()
                dst = QT[:, j, :] if j < 8 else KT[:, j - 8, :]
                head_norm(n, ps, m, dst, gq if j < 8 else C(f"dkg_{l}"), SQ[j % 2], RR[j % 2], qk, j, [mg])

            WB = [A(24576, 512), A(25088, 512)]
            EB = [A(25600, 512), A(26112, 512)]
            wbf, ebf = [None, None], [None, None]
            todo = []

            def diag(c, g, e, me):
                for r in range(4):
                    h = 4 * g + r
                    yo = Y[2 * c + h // 8][:, (h % 8) * 64:(h % 8) * 64 + 64]
                    mk = mm(yo, e[:, r * 128:r * 128 + 128], XD[:, c, h * 64:h * 64 + 64], True, True,
                            [me, mxd[c]] + [free[2 * c + h // 8]])
                return mk

            mdg = {}
            for i in range(8):
                c, g = divmod(i, 4)
                b = i % 2
                w4 = WB[b].rearrange("p (r s) -> p r s", r=4)
                m = tt(w4, C("gt").unsqueeze(1).broadcast_to([128, 4, 128]),
                       ad[:, c, 4 * g:4 * g + 4].unsqueeze(2).broadcast_to([128, 4, 128]), ALU.mult,
                       [mDT, wbf[b]], q=PO)
                n, ps, fr = bank()
                for r in range(4):
                    mk = mm(ps[:, r * 128:r * 128 + 128], WB[b][:, r * 128:r * 128 + 128], C("le"), True, True,
                            [fr, m])
                wbf[b] = mk
                me = free[n] = act(EB[b], ps, ACT.Exp, [mk, ebf[b]])
                me = tt(EB[b].rearrange("p (r l) -> p r l", r=4), EB[b].rearrange("p (r l) -> p r l", r=4),
                        CM[:, c * 512 + g * 128:c * 512 + g * 128 + 128].unsqueeze(1).broadcast_to([128, 4, 128]),
                        ALU.mult, [me, mcm[c]])
                if todo:
                    i2, args = todo.pop()
                    mdg[i2] = ebf[i2 % 2] = diag(*args)
                todo.append((i, (c, g, EB[b], me)))
                qk_slot()
            i2, args = todo.pop()
            mdg[i2] = diag(*args)
            dsk = C(f"dsk_{l}").unsqueeze(2).broadcast_to([128, 16, 64])
            mys = []
            for t in range(2):
                mys.append(tt(YS[:, t, :].rearrange("p (h e) -> p h e", h=16),
                              XT[:, t, :].rearrange("p (h e) -> p h e", h=16), dsk, ALU.mult, [mxt], q=PO))
            moff = []
            qk_slot()
            for hf in range(2):
                n, ps, fr = bank()
                for q in range(2):
                    g = 2 * hf + q
                    mk = mm(ps[:, q * 256:q * 256 + 256], XC[:, 12 + g, 128:256], ST[:, g * 256:g * 256 + 256], True,
                            True, [fr, mst])
                tmp = XE[:, hf * 512:hf * 512 + 512]
                m = free[n] = tt(tmp.rearrange("p (h e) -> p h e", h=8), ps.rearrange("p (h e) -> p h e", h=8),
                                 EA[:, 16 + 8 * hf:24 + 8 * hf].unsqueeze(2).broadcast_to([128, 8, 64]), ALU.mult,
                                 [mk, mea, mst])
                ys = YS[:, 1, hf * 512:hf * 512 + 512]
                moff.append(tt(ys, ys, tmp, ALU.add, [m, mys[1]]))
            st = stat(16)
            m2 = None
            for t in range(2):
                for hf in range(2):
                    ys = YS[:, t, hf * 512:hf * 512 + 512]
                    m = free[2 * t + hf] = tt(ys, ys, Y[2 * t + hf], ALU.add, [mdg[7], mdg[4 * t + 3], mys[t], moff])
                    m = tt(ys, ys, ZS[:, t, hf * 512:hf * 512 + 512], ALU.mult, [m, mzs])
                for g in range(4):
                    m2 = act(XE[:, g * 256:g * 256 + 256], YS[:, t, g * 256:g * 256 + 256], ACT.Square,
                             [m, moff, m2],
                             acc=st[:, 4 * t + g:4 * t + g + 1])
            m = ts(st[:, 0:8], st[:, 0:8], 1.0 / 256, EPS, ALU.mult, ALU.add, w=[m2], q=PO)
            mr = tt(st[:, 8:16], st[:, 0:8], NH(8), ALU.pow, [m], q=PO)
            mn = []
            for t in range(2):
                mn.append(tt(YS[:, t, :].rearrange("p (g e) -> p g e", g=4),
                             YS[:, t, :].rearrange("p (g e) -> p g e", g=4),
                             st[:, 8 + 4 * t:12 + 4 * t].unsqueeze(2).broadcast_to([128, 4, 256]), ALU.mult, [mr],
                             q=PO if t else DVE))
            while qkj[0] < 16:
                qk_slot()
            cat = {}
            for c2 in range(4):
                n, ps, fr = bank()
                for q in range(2):
                    for t in range(2):
                        c = 2 * c2 + q
                        mk = tp(ps[:, q * 256 + t * 128:][:, 0:128], YS[:, t, c * 128:c * 128 + 128], [fr, mn])
                for q in range(2):
                    c = 2 * c2 + q
                    src, g1 = ps[:, q * 256:q * 256 + 256], C(f"ssdn_{l}")[:, c:c + 1]
                    a = act(CAT[0][:, c, :], src, ACT.Copy, [mk], scale=g1)
                    b = free[n] = stt(CAT[1][:, c, :], src, g1, f32(CAT[0][:, c, :]), ALU.mult, ALU.subtract, [a])
                    mk = [mk, b]
                    cat[c] = [a, b]
            run_later()
            m = rows_out(f"sv{l}", 8, ht, lambda k: mh, None)
            for t in range(2):
                for hf in range(2):
                    mv = free[2 * t + hf] = act(V[:, t, hf * 512:hf * 512 + 512], Y[2 * t + hf], ACT.Copy, [m])
            H = Heads(0)
            H.next = (f"so{l}", 16, CAT, cat)
            H.rows = [(k, k) for k in range(8)]
            H.sf = [[mxc[15], mst, mdg[7], mk, moff]] * 3
            H.pf = [[mdg[7], mst, mk, mk, moff]] * 3
            mdm = [load(C("dilmask"), ins["dilmask"], [mDT, mdt]), load(C("dilmult"), ins["dilmult"], [mDT, mdt])]
            for h in range(16):
                pr = slice(64 * (h % 2), 64 * (h % 2) + 64)

                def scores(ps, fr, h=h, pr=pr):
                    w = [fr, qk[h // 2], qk[8 + h // 2]]
                    mm(ps[:, 0:128], QT[pr, h // 2, 0:128], KT[pr, h // 2, 0:128], True, True, w, inc=False)
                    return mm(ps[:, 128:384], QT[pr, h // 2, 128:256], KT[pr, h // 2, :], True, True)

                after = None
                if h % 2:
                    def after(mk, n, ps, o, h=h):
                        cat[8 + h // 2] = free[n] = split(CAT[0][:, 8 + h // 2, :], CAT[1][:, 8 + h // 2, :],
                                                          ps[:, 0:256], [mk])
                        H.rows.append((8 + h // 2, H.i + 1))
                H.add(scores, C("dilmask"), lambda kb, h=h: V[:, kb, h * 64:h * 64 + 64],
                      (h % 2, mv, True, True, after), mult=C("dilmult"), wmask=mdm)
            H.step(True)
            mk = H.mk
            residual(1.0, False, mk)

        need = [s for s in stages]
        if need and need[0] in ("mix0", "peer0", "mix1", "peer1"):
            sg = stat(8)
            m = act(sg, C("c"), ACT.Sigmoid)
            sc_m[0] = tt(silu_c, C("c"), sg, ALU.mult, [m])
        for s in stages:
            l = int(s[-1])
            lo_q[0] = DVE if s[:3] == "ffn" else PO
            if s == "mix0":
                for p in (0, 1):
                    for f in ada_piece(p):
                        f()
                for p in (2, 3, 4):
                    bg.extend(ada_piece(p))
                fox()
            elif s == "mix1":
                if stages[0] == "mix1":
                    for p in (6, 7):
                        for f in ada_piece(p):
                            f()
                    for p in (8, 9, 10):
                        bg.extend(ada_piece(p))
                nsa()
            elif s[:4] == "peer":
                p0 = 6 * l
                if stages[0] == s:
                    for p in (6 * l + 3, 6 * l + 4):
                        for f in ada_piece(p):
                            f()
                bg.extend(ada_piece(p0 + 5))
                if l == 0 and "mix1" in stages:
                    for p in (6, 7, 9, 10):
                        bg.extend(ada_piece(p))
                peer(l)
                if l == 0 and "mix1" in stages:
                    bg.extend(ada_piece(8))
            elif s[:3] == "ffn":
                ffn(s[3], l)
            else:
                ssd(l)
            fence()
        s_out = new_sem("out")
        for t in range(2):
            o = out.rearrange("a (t p) n -> (a t) p n", p=128)[t]
            SC.pending = []
            SC.dma(lambda e, o=o, t=t: e.dma_start(o, X[:, t, :]), [m_x[t]], s_out)
        SC.ops.append(("wait", s_out, 32))

        for n, src in enumerate(stream):
            w = [raw_free.get(n - NR)]
            o = RINGt[:, (n % NR) * 1024:(n % NR + 1) * 1024]
            SP.dma(lambda e, o=o, src=src: e.dma_start(o, src), w, ring_sem[n % NR])
        return (PE, DVE, SC, PO, SP), order


def kernel(**inputs):
    import concourse.bacc as _bacc
    from concourse.bass_utils import run_bass_kernel_spmd as _run

    nc = _bacc.Bacc("TRN2", target_bir_lowering=False, num_devices=1)
    arrays = lay_out(inputs)
    ins = {k: nc.dram_tensor(f"in_{k}", v.shape, F32, kind="ExternalInput").ap() for k, v in arrays.items()}
    out = nc.dram_tensor("out_x", (1, 256, 1024), F32, kind="ExternalOutput").ap()
    build(nc, ins, out)
    r = _run(nc, [{f"in_{k}": v for k, v in arrays.items()}], core_ids=[0])
    return r.results[0]["out_x"]
```

```python
import numpy as np
import concourse.bass as bass
from concourse import mybir
from contextlib import ExitStack

F32 = mybir.dt.float32
F32R = mybir.dt.float32r
U32 = mybir.dt.uint32
ALU = mybir.AluOpType
ACT = mybir.ActivationFunctionType
AX = mybir.AxisListType

EPS = 1e-6
NEG = -1e30
NR = 4
NHL = 3
AHEAD = 2
LAG = 2
SECOND_T = 42
WAT = (0, 2)
WHOLE = ("ada", "nsaw1")
STAGES = ("mix0", "peer0", "mix1", "peer1", "ffnA0", "ssd0", "ffnB0", "ffnA1", "ssd1", "ffnB1")


def shape_constants():
    p = np.arange(128)
    f = np.float32
    c = {}
    c["ident"] = np.eye(128, dtype=f)
    c["ones"] = np.ones((128, 128), f)
    c["bd64"] = (p[:, None] // 64 == p[None, :] // 64).astype(f)
    c["le"] = (p[:, None] <= p[None, :]).astype(f)
    c["gt"] = (p[:, None] > p[None, :]).astype(f)
    c["iota"] = np.broadcast_to(p.astype(f), (128, 128)).copy()
    dist = np.concatenate([p[:, None] - p[None, :], 128 + p[:, None] - np.arange(256)[None, :]], 1)
    c["causal"] = np.where(dist >= 0, 0.0, NEG).astype(f)
    mult = ((dist >= 0) & (dist <= 128)).astype(f) + ((dist >= 0) & (dist % 4 == 0)) + ((dist >= 0) & (dist % 16 == 0))
    c["dilmask"] = np.where(mult > 0, 0.0, NEG).astype(f)
    c["dilmult"] = mult.astype(f)
    t = np.arange(256)
    ends = np.arange(15) * 16 + 31
    ok = (ends[None, :] <= t[:, None]).reshape(2, 128, 15).transpose(1, 0, 2)
    ok = np.repeat(ok[:, :, None, :], 4, 2).reshape(128, 120)
    c["cmpok"] = ok.astype(f)
    c["cmpneg"] = np.where(ok, 0.0, NEG).astype(f)
    sel = np.zeros((128, 8), f)
    for h in range(8):
        sel[h::32, h] = 1
    c["headsel"] = sel
    c["rowsel"] = (p[:, None] // 32 == np.arange(4)[None, :]).astype(f)
    c["neghalf"] = np.full((128, 1), -0.5, f)
    return c


def rel_buckets(dist):
    n = np.maximum(dist, 0)
    nf = np.maximum(n, 1).astype(np.float32)
    large = 16 + (np.log(nf / np.float32(16)) / np.float32(np.log(8.0)) * np.float32(16)).astype(np.int32)
    return np.where(n < 16, n, np.minimum(large, 31))


STAGE_CONSTANTS = ("causal", "dilmask", "dilmult", "cmpok", "cmpneg")
PACKS = {"all": ("ident", "ones", "iota", "neghalf", "c", "normg"),
         "fox": ("bd64", "headsel", "foxqg", "foxkg", "convw", "bf"),
         "nsa": ("bd64", "rowsel", "nsaqg", "nsakg", "bgate", "pos", "w2k", "w2v")}
for _l in range(2):
    PACKS[f"ffnA{_l}"] = (f"fn1_{_l}",)
    PACKS[f"ffnB{_l}"] = (f"fn2_{_l}",)
    PACKS[f"ssd{_l}"] = ("bd64", f"mixn_{_l}", f"ssdn_{_l}", f"dqg_{_l}", f"dkg_{_l}", f"cw_{_l}", f"cb_{_l}",
                         f"dtb_{_l}", f"alog_{_l}", f"dsk_{_l}")


def columns(v):
    return v.reshape(-1, 128).T


def packed(i):
    c = {k: v for k, v in shape_constants().items() if k not in STAGE_CONSTANTS}
    f = np.float32

    def rows(v, at=0):
        z = np.zeros((128, v.shape[1] if v.ndim > 1 else 1), f)
        z[at:at + v.shape[0]] = v.reshape(v.shape[0], -1)
        return z

    c["c"] = columns(i["c"][0])
    c["normg"] = columns(i["norm_g"])
    c["foxqg"] = np.tile(i["even_q_g"][0], 2)[:, None]
    c["foxkg"] = np.tile(i["even_k_g"][0], 2)[:, None]
    c["convw"] = i["even_conv_w"][0].reshape(3, 4, 128).transpose(2, 1, 0).reshape(128, 12)
    bf = np.zeros((128, 1), f)
    for q in range(4):
        bf[32 * q:32 * q + 8, 0] = i["even_b_f"][0]
    c["bf"] = bf
    c["nsaqg"] = np.tile(i["odd_q_g"][0], 2)[:, None]
    c["nsakg"] = np.tile(i["odd_k_g"][0], (1, 2)).T
    c["bgate"] = rows(i["odd_b_gate"][0][:, None])
    c["pos"] = i["odd_cmp_pos"][0].reshape(2, 16, 2, 64).transpose(2, 3, 0, 1).reshape(128, 32)
    c["w2k"] = rows(np.tile(i["odd_cmp_w2"][0, 0], (1, 2)))
    c["w2v"] = rows(i["odd_cmp_w2"][0, 1])
    for l in range(2):
        c[f"fn1_{l}"] = columns(i["ffn1_norm_2"][l])
        c[f"fn2_{l}"] = columns(i["ffn2_norm_2"][l])
        c[f"mixn_{l}"] = columns(i["mix_norm_2"][l])
        c[f"ssdn_{l}"] = columns(i["ssd_norm_2"][l])
        c[f"dqg_{l}"] = np.tile(i["q_norm_2"][l], 2)[:, None]
        c[f"dkg_{l}"] = np.tile(i["k_norm_2"][l], 2)[:, None]
        c[f"cw_{l}"] = i["conv_w_2"][l].reshape(4, 16, 128).transpose(2, 1, 0).reshape(128, 64)
        c[f"cb_{l}"] = columns(i["conv_b_2"][l])
        c[f"dtb_{l}"] = rows(i["dt_bias_2"][l][:, None])
        c[f"alog_{l}"] = rows(i["a_log_2"][l][:, None])
        c[f"dsk_{l}"] = np.broadcast_to(i["d_skip_2"][l], (128, 16)).copy()
    return c


def stationary(w):
    n = -(-w.shape[1] // 128)
    if n * 128 != w.shape[1]:
        w = np.concatenate([w, np.zeros((w.shape[0], n * 128 - w.shape[1]), w.dtype)], 1)
    return w.reshape(8, 128, n, 128).transpose(2, 1, 0, 3).reshape(n, 128, 1024)


def moving(w):
    return w.reshape(-1, 128, 1024)


def moving512(w):
    return w.reshape(4, 2, 128, 512).transpose(0, 2, 1, 3).reshape(4, 128, 1024)


def lay_out(i):
    i = {k: np.asarray(v) for k, v in i.items()}
    a = {}
    pk = packed(i)
    for k, names in PACKS.items():
        a[f"pack_{k}"] = np.concatenate([pk[n] for n in names], 1)
    a["legt"] = np.concatenate([pk["le"], pk["gt"]], 1)
    for k, v in shape_constants().items():
        if k in STAGE_CONSTANTS:
            a[k] = v
    a["x"] = i["x"][0].reshape(2, 128, 1024)
    a["ada"] = i["ada_w"].reshape(2, 8, 128, 6, 1024).transpose(0, 3, 1, 2, 4).reshape(96, 128, 1024)
    a["adab"] = i["ada_b"].reshape(12, 1, 1024)
    w = i["even_w_in"][0]
    st = stationary(w[:, :2560])
    a["foxst"] = np.concatenate([st[[4 + j, 8 + j, j]] for j in range(4)] + [st[12:20]])
    wf = np.zeros((1024, 128), np.float32)
    for q in range(4):
        wf[:, 32 * q:32 * q + 8] = w[:, 3072:3080]
    a["foxf"] = stationary(wf)
    a["foxv"] = moving512(w[:, 2560:3072])
    a["foxo"] = moving(i["even_w_out"][0])
    w = i["odd_w_in"][0]
    a["nsaq"] = stationary(w[:, :1024])
    kv = w[:, 1024:1536].reshape(1024, 8, 1, 64)
    a["nsac"] = stationary(np.tile(kv, (1, 1, 2, 1)).reshape(1024, 1024))
    a["nsak"] = stationary(np.concatenate([w[:, 1536:1792], w[:, 2048:2304]], 1))
    a["nsav"] = moving512(np.concatenate([w[:, 1792:2048], w[:, 2304:2560]], 1))
    a["nsag"] = stationary(w[:, 2560:2608])
    a["nsaw1"] = i["odd_cmp_w1"][0].reshape(2, 16, 128, 64).transpose(0, 2, 1, 3).reshape(2, 128, 1024)
    a["nsao"] = moving(i["odd_w_out"][0])
    p = np.arange(128)
    dist = np.concatenate([p[:, None] - p[None, :], 128 + p[:, None] - np.arange(256)[None, :]], 1)
    tab = i["rel_table"]
    a["toep"] = tab[rel_buckets(dist)].transpose(0, 2, 1).reshape(128, 16 * 384)
    t = np.arange(256)
    ends = np.arange(15) * 16 + 31
    cb = tab[rel_buckets(t[:, None] - ends[None, :])].reshape(2, 128, 15, 4, 4)
    a["cmpb"] = cb.transpose(1, 3, 0, 4, 2).reshape(128, 480)
    for l in range(2):
        k = np.zeros((2, 64, 2, 128), np.float32)
        for p in range(2):
            k[p, :, p, :] = i["peer_keys"][l, p].T
        a[f"keys{l}"] = k.reshape(128, 256)
        a[f"pq{l}"] = stationary(i["peer_w_q"][l])
        a[f"pu{l}"] = i["peer_u"][l].reshape(128, 128, 8, 128).transpose(1, 3, 2, 0).reshape(128, 128, 1024)
        a[f"pv{l}"] = i["peer_v"][l].reshape(128, 128, 1024).transpose(1, 0, 2)
        for n, s in (("A", "1"), ("B", "2")):
            a[f"fg{n}{l}"] = stationary(i[f"ffn{s}_w_gate_2"][l])
            a[f"fu{n}{l}"] = stationary(i[f"ffn{s}_w_up_2"][l])
            a[f"fd{n}{l}"] = moving(i[f"ffn{s}_w_down_2"][l])
        w = i["w_in_2"][l]
        a[f"sz{l}"] = moving(w[:, :1024])
        a[f"sx{l}"] = stationary(w[:, 1024:3072])
        a[f"sd{l}"] = stationary(w[:, 3072:3088])
        a[f"sqk{l}"] = stationary(w[:, 3088:5136])
        a[f"sv{l}"] = moving(w[:, 5136:6160])
        a[f"so{l}"] = moving(i["w_out_2"][l])
    return {k: np.ascontiguousarray(v, dtype=np.float32) for k, v in a.items()}


def pack_places():
    z = {"c": (1, 1024), "norm_g": (2, 2, 1024), "even_q_g": (1, 64), "even_k_g": (1, 64), "even_conv_w": (1, 3, 512),
         "even_b_f": (1, 8), "odd_q_g": (1, 64), "odd_k_g": (1, 3, 64), "odd_b_gate": (1, 48),
         "odd_cmp_pos": (1, 2, 32, 64), "odd_cmp_w2": (1, 2, 64, 64),
         "ffn1_norm_2": (2, 1024), "ffn2_norm_2": (2, 1024), "mix_norm_2": (2, 1024), "ssd_norm_2": (2, 1024),
         "q_norm_2": (2, 64), "k_norm_2": (2, 64), "conv_w_2": (2, 4, 2048), "conv_b_2": (2, 2048),
         "dt_bias_2": (2, 16), "a_log_2": (2, 16), "d_skip_2": (2, 16)}
    pk = packed({k: np.zeros(s, np.float32) for k, s in z.items()})
    out = {}
    for stage, names in PACKS.items():
        at, out[stage] = 0, {}
        for k in names:
            out[stage][k] = (at, pk[k].shape[1])
            at += pk[k].shape[1]
        out[stage]["width"] = at
    return out


class Counter:

    def __init__(self, new_sem, name):
        self.new_sem, self.name, self.sem, self.n, self.k = new_sem, name, None, 0, 0

    def step(self):
        if self.sem is None or self.n >= 16000:
            self.sem, self.n, self.k = self.new_sem(f"{self.name}{self.k}"), 0, self.k + 1
        self.n += 1
        return (self.sem, self.n)

    def last(self):
        return (self.sem, self.n) if self.sem is not None else None


class Queue:

    def __init__(self, new_sem, name):
        self.ops, self.count, self.done, self.pending = [], Counter(new_sem, name), {}, []

    def wait(self, marks):
        for m in marks:
            if m is None:
                continue
            if isinstance(m, list):
                self.wait(m)
                continue
            sem, n = m
            if self.done.get(id(sem), 0) < n:
                self.done[id(sem)] = n
                self.ops.append(("wait", sem, n))

    def put(self, fn, waits, inc=True, aside=False):
        if not aside:
            self.wait(self.pending)
            self.pending = []
        self.wait(waits)
        mark = self.count.step() if inc else None
        self.ops.append(("do", fn, mark[0] if inc else None))
        return mark

    def dma(self, fn, waits, sem):
        self.wait(self.pending)
        self.pending = []
        self.wait(waits)
        self.ops.append(("dma", fn, sem))

    def emit(self, eng):
        for kind, a, b in self.ops:
            if kind == "wait":
                eng.wait_ge(a, b)
            elif kind == "do":
                ins = a(eng)
                if b is not None:
                    ins.then_inc(b, 1)
            else:
                a(eng).then_inc(b, 16)


class Mark0:
    pass


def build(nc, ins, out, stages=STAGES):
    ctx = ExitStack()
    with ctx:
        tensors = {}

        def new_sem(name):
            return ctx.enter_context(nc.semaphore("s_" + name))

        places = pack_places()
        for name, cols, dt in (("X", 2048, F32), ("HTH", 2048, F32R), ("HTL", 2048, F32R), ("RING", NR * 1024, F32),
                               ("HI", NHL * 1024, F32R), ("LO", NHL * 1024, F32R), ("ACC", 1024, F32),
                               ("CST", places["all"]["width"], F32), ("STAT", 192, F32), ("MOD", 80, F32)):
            tensors[name] = ctx.enter_context(nc.sbuf_tensor(name, [128, cols], dt))
        banks = [ctx.enter_context(nc.psum_tensor(f"P{n}", [128, 512], F32)) for n in range(8)]
        plan = program(nc, ins, out, stages, places, tensors, banks, lambda name: Mark0(), None)[1]
        queues, _ = program(nc, ins, out, stages, places, tensors, banks, new_sem, plan)

        block = ctx.enter_context(nc.Block())

        @block.sync
        def _(eng):
            queues[4].emit(eng)

        @block.tensor
        def _(eng):
            queues[0].emit(eng)

        @block.vector
        def _(eng):
            queues[1].emit(eng)

        @block.scalar
        def _(eng):
            queues[2].emit(eng)

        @block.gpsimd
        def _(eng):
            queues[3].emit(eng)


def program(nc, ins, out, stages, places, tensors, banks, new_sem, plan):
    X = tensors["X"][:, :].rearrange("p (t n) -> p t n", t=2)
    HT = [tensors[n][:, :].rearrange("p (k t) -> p k t", k=8) for n in ("HTH", "HTL")]
    RINGt, HIt, LOt, ACCt, CSTt = (tensors[n] for n in ("RING", "HI", "LO", "ACC", "CST"))
    STAT, MOD = tensors["STAT"][:, :], tensors["MOD"][:, :]
    Y = [b[:, :] for b in banks[:4]]

    PE, DVE, SC, PO, SP = (Queue(new_sem, n) for n in ("pe", "dve", "act", "pool", "sp"))
    local = {}

    def C(name, a=0, b=None):
        if name in local:
            n = local[name].shape[-1]
            return local[name][:, a:n if b is None else b]
        at, n = places["all"][name]
        return CSTt[:, at + a:at + (n if b is None else b)]

    def NH(n):
        at = places["all"]["neghalf"][0]
        return CSTt[:, at:at + 1].broadcast_to([128, n])

    def scope(stage, *parts):
        with ExitStack() as c:
            for name, cols, dt in parts:
                key = f"{stage}_{name}"
                if key not in tensors:
                    tensors[key] = c.enter_context(nc.sbuf_tensor(key, [128, cols], dt))
        got = [tensors[f"{stage}_{name}"] for name, _, _ in parts]
        arena[0] = got[0]
        return got

    def stage_pack(stage, at):
        local.clear()
        width = places[stage]["width"]
        for k, v in places[stage].items():
            if k != "width":
                local[k] = A(at + v[0], v[1])
        pack_mark[0] = load(A(at, width), ins[f"pack_{stage}"])

    pack_mark = [None]
    arena = [None]
    GB = [None]

    def A(off, n):
        return arena[0][:, off:off + n]

    def mm(o, l, r, start, stop, w=(), inc=None):
        return PE.put(lambda e: e.matmul(o, l, r, start=start, stop=stop), w, stop if inc is None else inc)

    def tp(o, i, w=(), n=128, inc=True):
        idt = C("ident")[0:n, 0:n]
        return PE.put(lambda e: e.transpose(o, i, idt), w, inc)

    def tt(o, a, b, op, w=(), q=None):
        return (q or DVE).put(lambda e: e.tensor_tensor(o, a, b, op), w)

    def ts(o, a, s1, s2, op0, op1=None, w=(), q=None):
        if op1 is None:
            return (q or DVE).put(lambda e: e.tensor_scalar(o, a, s1, None, op0), w)
        return (q or DVE).put(lambda e: e.tensor_scalar(o, a, s1, s2, op0, op1), w)

    def stt(o, a, s, b, op0, op1, w=()):
        return DVE.put(lambda e: e.scalar_tensor_tensor(out=o, in0=a, scalar=s, in1=b, op0=op0, op1=op1), w)

    def copy(o, a, w=(), q=None):
        return (q or DVE).put(lambda e: e.tensor_copy(o, a), w)

    def red(o, a, op, w=(), neg=False):
        return DVE.put(lambda e: e.tensor_reduce(o, a, AX.X, op, negate=neg), w)

    def rec(o, a, w=()):
        return DVE.put(lambda e: e.reciprocal(o, a), w)

    def f32(a):
        return a.bitcast(F32)

    def split(hi, lo, src, w, q=None):
        h = act(hi, src, ACT.Copy, w)
        return [h, tt(lo, src, f32(hi), ALU.subtract, [h], q=q)]

    def mset(o, v, w=(), q=None):
        return (q or DVE).put(lambda e: e.memset(o, v), w)

    def act(o, a, f, w=(), bias=0.0, scale=1.0, acc=None):
        if f == ACT.Copy:
            return SC.put(lambda e: e.activation(o, a, f, scale=scale), w)
        if acc is not None:
            return SC.put(lambda e: e.activation(o, a, f, bias=bias, scale=scale, accum_out=acc), w)
        return SC.put(lambda e: e.activation(o, a, f, bias=bias, scale=scale), w)

    def load(o, i, w=(), sem=None):
        s = sem or new_sem(f"ld{len(loads)}")
        loads.append(s)
        SC.dma(lambda e: e.dma_start(o, i), w, s)
        return (s, 16)

    loads = []

    def fence():
        marks = [q.count.last() for q in (PE, DVE, SC, PO)]
        for q in (PE, DVE, SC, PO):
            q.pending = list(marks)

    stream, order, halves, hl_free = [], [], {}, {}
    ring_sem = [new_sem(f"ring{n}") for n in range(NR)]
    lo_q = [DVE]

    def raw(n):
        return RINGt[:, (n % NR) * 1024:(n % NR + 1) * 1024], (ring_sem[n % NR], 16 * (n // NR + 1))

    def convert(n):
        name, c, q = plan[n]
        if name in WHOLE or n in halves:
            return
        b = c % NHL
        hi, lo = HIt[:, b * 1024:b * 1024 + 1024], LOt[:, b * 1024:b * 1024 + 1024]
        w, m = raw(n)
        fr = hl_free.get(c - NHL)
        a = SC.put(lambda e: e.activation(hi, w, ACT.Copy), [m, fr], aside=True)
        l = (PO if q else DVE).put(lambda e: e.tensor_tensor(lo, w, f32(hi), ALU.subtract), [m, a, fr],
                                   aside=True)
        halves[n] = (hi, lo, a, l)
        raw_free[n] = l

    raw_free = {}

    def take(name, idx):
        n = len(stream)
        stream.append(ins[name][idx])
        c = sum(order_count)
        order.append((name, c, lo_q[0] is PO))
        if name in WHOLE:
            return raw(n) + (n,)
        order_count[0] += 1
        if plan is None:
            return HIt[:, 0:1024], LOt[:, 0:1024], None, None, n
        for k in range(n, min(n + AHEAD + 1, len(plan))):
            convert(k)
        return halves[n] + (n,)

    order_count = [0]

    def give(n, mark):
        if order[n][0] in WHOLE:
            raw_free[n] = mark
        else:
            hl_free[order[n][1]] = mark

    idle = [4, 5, 6, 7]

    class Free(dict):
        def __setitem__(self, n, mark):
            dict.__setitem__(self, n, mark)
            if n >= 4 and n not in idle:
                idle.append(n)

    free = Free({n: None for n in range(8)})

    def bank():
        n = idle.pop(0)
        return n, banks[n][:, :], free[n]

    sturn = [0]

    def stat(n):
        if sturn[0] + n > 192:
            sturn[0] = 0
        a = STAT[:, sturn[0]:sturn[0] + n]
        sturn[0] += n
        return a

    SP_c = new_sem("pack_all")
    SP.dma(lambda e: e.dma_start(CSTt[:, :], ins["pack_all"]), (), SP_c)
    m_pack = (SP_c, 16)
    s_x = new_sem("x")
    for t in range(2):
        SC.dma(lambda e, t=t: e.dma_start(X[:, t, :], ins["x"][t]), (), s_x)
    for q in (PE, DVE, SC, PO):
        q.pending = [m_pack]
    m_x = [(s_x, 32)] * 2

    sc_m = [None]
    silu_c = MOD[:, 64:72]
    acc_free = [None]
    mod_done = {}
    bg = []

    def ada_piece(p, acc=None):
        state = {}
        own = acc is not None
        acc = acc if own else ACCt[:, :]

        def first():
            m = mset(acc, 0.0, [None if own else acc_free[0]], q=PO)
            s_ab = new_sem(f"ab{p}")
            PO.dma(lambda e: e.dma_start(acc[0:1, :], ins["adab"][p]), [m], s_ab)
            state["m"] = (s_ab, 16)

        def slot(k):
            def run():
                w, m, n = take("ada", p * 8 + k)
                state["m"] = stt(acc, w, silu_c[:, k:k + 1], acc, ALU.mult, ALU.add,
                                 [m, state["m"], sc_m[0]])
                give(n, state["m"])
            return run

        def last():
            l, kind = divmod(p, 6)
            n, ps, fr = bank()
            if kind in (2, 5):
                for hf in range(2):
                    if hf:
                        n, ps, fr = bank()
                    m = mm(ps, C("ones"), acc[:, hf * 512:hf * 512 + 512], True, True, [fr, state["m"]])
                    acc_free[0] = m
                    free[n] = act(GB[0][:, hf * 512:hf * 512 + 512], ps, ACT.Copy, [m])
                mod_done[p] = free[n]
                return
            for k in range(8):
                m = mm(ps[:, k:k + 1], acc[:, k * 128:k * 128 + 128], C("ones")[:, 0:1], True, True,
                       [fr, state["m"]])
            acc_free[0] = m
            half = kind // 3
            place = MOD[:, 16 * (2 * (l % 2) + half):][:, 0:16]
            if kind % 3 == 0:
                mod_done[p] = free[n] = copy(place[:, 8:16], ps[:, 0:8], [m])
            else:
                g = C("normg", (l * 2 + half) * 8, (l * 2 + half) * 8 + 8)
                mod_done[p] = free[n] = stt(place[:, 0:8], ps[:, 0:8], 1.0, g, ALU.add, ALU.mult, [m])

        return [first] + [slot(k) for k in range(8)] + [last]

    def background(n=1):
        for _ in range(n):
            if bg:
                bg.pop(0)()

    XN, HR = 0, 2048
    T00 = 4096

    def make_h(scale, shift, w):
        sts = stat(2)
        xn = A(XN, 2048).rearrange("p (t n) -> p t n", t=2)
        r = stat(2)
        mt = []
        for t in range(2):
            m = act(xn[:, t, :], X[:, t, :], ACT.Square, [m_x[t], w], acc=sts[:, t:t + 1])
            m = ts(sts[:, t:t + 1], sts[:, t:t + 1], 1.0 / 1024, EPS, ALU.mult, ALU.add, [m], q=PO)
            mt.append(tt(r[:, t:t + 1], sts[:, t:t + 1], NH(1), ALU.pow, [m], q=PO))
        mt = [ts(xn[:, 0, :], X[:, 0, :], r[:, 0:1], None, ALU.mult, w=[mt[0]]),
              act(xn[:, 1, :], X[:, 1, :], ACT.Copy, [mt[1]], scale=r[:, 1:2])]
        if pack_mark[0] is not None:
            for q in (PE, DVE, SC, PO):
                q.pending = q.pending + [pack_mark[0]]
            pack_mark[0] = None
        out = []
        got = [bank() for _ in range(4)]
        done = {}
        for t in range(2):
            for k in range(8):
                n, ps, fr = got[k // 2]
                done[k // 2] = tp(ps[:, k % 2 * 256 + t * 128:][:, 0:128], xn[:, t, k * 128:k * 128 + 128],
                                  [fr, mt[t]])
        def moved(k2):
            n, ps, fr = got[k2]
            m = done[k2]
            for k in (2 * k2, 2 * k2 + 1):
                src, dst = ps[:, k % 2 * 256:k % 2 * 256 + 256], A(HR + 256 * k, 256)
                if k2 % 2 and shift is None:
                    a = act(dst, src, ACT.Copy, [m, w], scale=scale[:, k:k + 1])
                elif k2 % 2:
                    a = act(dst, src, ACT.Identity, [m, w], scale=scale[:, k:k + 1], bias=shift[:, k:k + 1])
                elif shift is None:
                    a = ts(dst, src, scale[:, k:k + 1], None, ALU.mult, w=[m, w])
                else:
                    a = ts(dst, src, scale[:, k:k + 1], shift[:, k:k + 1], ALU.mult, ALU.add, w=[m, w])
            free[n] = a
            return a

        out = {}

        def parted(k2, a):
            out[k2] = split(HT[0][:, 2 * k2:2 * k2 + 2, :], HT[1][:, 2 * k2:2 * k2 + 2, :],
                            A(HR + 512 * k2, 512).rearrange("p (k t) -> p k t", k=2), [a])

        a = [moved(0), moved(1), moved(2)]
        parted(0, a[0])
        a.append(moved(3))
        for k2 in range(1, 4):
            parted(k2, a[k2])
        return [[out[k2][q] for k2 in range(4)] for q in range(2)]

    def project(name, idx, mh, between=None):
        wh, wl, mh_, ml_, s = take(name, idx)
        n, ps, fr = bank()
        for i, (w, mw, h) in enumerate(((wh, mh_, 0), (wh, mh_, 1), (wl, ml_, 0))):
            for k in range(8):
                mk = mm(ps[:, 0:256], w[:, k * 128:k * 128 + 128], HT[h][:, k, :], i == 0 and k == 0,
                        i == 2 and k == 7, [fr, mw, mh[h][k // 2]])
                if between is not None and k % 4 == 3:
                    between()
        give(s, mk)
        return n, ps[:, 0:256], mk

    def rows_slot(k, nslots, wt, lhs, w, between=None):
        wh, wl, mh_, ml_, s = wt
        parts = ((wh, mh_, 0), (wh, mh_, 1), (wl, ml_, 0))
        todo = [(i, t, hf) for i in range(3) for t in range(2) for hf in range(2)]
        if k == nslots - 1:
            todo.sort(key=lambda e: e[1])
        for turn, (i, t, hf) in enumerate(todo):
            v, mw, h = parts[i]
            mk = mm(Y[2 * t + hf], lhs[h][:, t * 128:t * 128 + 128], v[:, hf * 512:hf * 512 + 512],
                    i == 0 and k == 0, i == 2 and k == nslots - 1,
                    [mw, w] + ([free[2 * t + hf]] if i == 0 and k == 0 else []), inc=i == 2)
            if i == 2:
                y_done[2 * t + hf] = mk
            if between is not None and turn % 3 == 1:
                between()
        give(s, mk)
        return mk

    y_done = {}

    def rows_out(name, nslots, lhs, w):
        for k in range(nslots):
            mk = rows_slot(k, nslots, take(name, k), lhs(k), w(k))
            background()
        return mk

    def rows512(name, w):
        for s4 in range(4):
            wh, wl, mh_, ml_, s = take(name, s4)
            for i, (v, mw, h) in enumerate(((wh, mh_, 0), (wh, mh_, 1), (wl, ml_, 0))):
                for kk in range(2):
                    for t in range(2):
                        k = 2 * s4 + kk
                        mk = mm(Y[t], HT[h][:, k, t * 128:t * 128 + 128], v[:, kk * 512:kk * 512 + 512],
                                k == 0 and i == 0, k == 7 and i == 2, [mw, w, free[t]], inc=i == 2)
            give(s, mk)
        return mk

    def ht(k):
        return [HT[0][:, k, :], HT[1][:, k, :]]

    later = []

    def run_later(keep=0):
        while len(later) > keep:
            later.pop(0)()

    def head_norm(n, ps, m, dst, gcol, sq, rr, marks, key, w=None):
        a = act(dst, ps, ACT.Copy, [m, w])
        b = act(sq, ps, ACT.Square, [m, w, sq_free.get(id(sq))])
        free[n] = b

        def rest():
            n2, p2, fr = bank()
            mk = mm(p2[:, 0:256], C("bd64"), sq, True, True, [fr, b])
            sq_free[id(sq)] = mk
            c = ts(rr, p2[:, 0:256], 1.0 / 64, EPS, ALU.mult, ALU.add, w=[mk, rr_free.get(id(rr))])
            free[n2] = c
            d = rec(rr, rr, [act(rr, rr, ACT.Sqrt, [c])])
            marks[key] = stt(dst, dst, gcol, rr, ALU.mult, ALU.mult, [d, a])
            rr_free[id(rr)] = marks[key]
        later.append(rest)

    sq_free, rr_free = {}, {}

    def log1p_exp(o, x, t1, t2, t3, w):
        m = act(t1, x, ACT.Abs, w)
        m = act(t1, t1, ACT.Exp, [m], scale=-1.0)
        m = ts(t2, t1, 2.0, None, ALU.add, w=[m])
        m = rec(t2, t2, [m])
        m = tt(t1, t1, t2, ALU.mult, [m])
        m = tt(t2, t1, t1, ALU.mult, [m])
        m = ts(t3, t2, 2.0 / 17, 2.0 / 15, ALU.mult, ALU.add, w=[m])
        for c in (13, 11, 9, 7, 5, 3, 1):
            m = tt(t3, t3, t2, ALU.mult, [m])
            m = ts(t3, t3, 2.0 / c, None, ALU.add, w=[m])
        return tt(o, t3, t1, ALU.mult, [m])

    class Heads:
        def __init__(self, base, nb=4):
            self.S = [A(base + n * 384, 384) for n in range(nb)]
            self.P = [A(base + (nb + n) * 384, 384) for n in range(nb)]
            self.sf, self.pf, self.nb, self.i = [None] * nb, [None] * nb, nb, 0
            self.q = []
            self.rows, self.next = [], None

        def more(self, flush=False):
            if self.rows and (flush or self.i > self.rows[0][1]):
                k = self.rows.pop(0)[0]
                name, n, cat_, marks = self.next
                self.mk = rows_slot(k, n, take(name, k), [cat_[0][:, k, :], cat_[1][:, k, :]], marks[k])
                background()

        def add(self, scores, mask, v, dst, gate=None, mult=None, wmask=None):
            r = self.i % self.nb
            self.i += 1
            S, P = self.S[r], self.P[r]
            n, ps, fr = bank()
            m = scores(ps, fr)
            st = stat(6)
            m = tt(S, ps[:, 0:384], mask, ALU.add, [m, self.sf[r], wmask])
            free[n] = m
            red(st[:, 0:1], S[:, 0:128], ALU.max, [m], neg=True)
            m = red(st[:, 1:2], S[:, 128:384], ALU.max, [m], neg=True)
            for i, (a, b) in enumerate(((0, 128), (128, 384))):
                m2 = act(S[:, a:b], S[:, a:b], ACT.Exp, [m], bias=st[:, i:i + 1],
                         acc=None if mult is not None else st[:, 2 + i:3 + i])
            m = m2
            if mult is not None:
                for i, (a, b) in enumerate(((0, 128), (128, 384))):
                    o, c, u = S[:, a:b], mult[:, a:b], st[:, 2 + i:3 + i]
                    m = DVE.put(lambda e, o=o, c=c, u=u: e.tensor_tensor_reduce(
                        o, o, c, 1.0, 0.0, ALU.mult, ALU.add, u), [m2])
            m = rec(st[:, 4:6], st[:, 2:4], [m])
            if gate is not None:
                m = tt(st[:, 4:6], st[:, 4:6], gate[0], ALU.mult, [m, gate[1]])
            ts(S[:, 0:128], S[:, 0:128], st[:, 4:5], None, ALU.mult, w=[m], q=PO)
            m = ts(S[:, 128:384], S[:, 128:384], st[:, 5:6], None, ALU.mult, w=[m], q=PO)
            self.q.append([0, r, S, P, m, v, dst])
            self.step()
            self.more()

        def step(self, flush=False):
            if flush:
                for e in self.q:
                    if e[0] == 0:
                        self.turn(e)
                while self.q:
                    self.pv(self.q.pop(0))
                while self.rows:
                    self.more(True)
                return
            if len(self.q) > LAG + 1:
                self.pv(self.q.pop(0))
            if len(self.q) > LAG:
                self.turn(self.q[-1 - LAG])

        def turn(self, e):
            _, r, S, P, m, v, dst = e
            n, ps, fr = bank()
            for c in range(3):
                mk = tp(ps[:, c * 128:c * 128 + 128], S[:, c * 128:c * 128 + 128], [fr, m])
            self.sf[r] = mk
            e[4] = act(P, ps[:, 0:384], ACT.Copy, [mk, self.pf[r]])
            free[n] = e[4]
            e[0] = 1

        def pv(self, e):
            _, r, S, P, m, v, dst = e
            odd, w, first, last, after = dst
            if not odd and first:
                self.ob = bank()
            pr = slice(64 * odd, 64 * odd + 64)
            o = self.ob[1][pr, 0:256]
            w = [w, self.ob[2]]
            mm(o, v(0), P[:, 0:256], first, False, [m, w], inc=False)
            mk = mm(o[:, 128:256], v(1), P[:, 256:384], False, last, [m], inc=True)
            self.pf[r] = mk
            if after is not None:
                after(mk, self.ob[0], self.ob[1], o)

    def residual(scale, gated, wy, w=None):
        for t in range(2):
            for hf in range(2):
                x = X[:, t, hf * 512:hf * 512 + 512]
                y = Y[2 * t + hf]
                if gated:
                    tmp = A(XN + (2 * t + hf) * 512, 512)
                    m = tt(tmp, y, GB[0][:, hf * 512:hf * 512 + 512], ALU.mult, [y_done[2 * t + hf], w])
                    free[2 * t + hf] = m
                    m = tt(x, x, tmp, ALU.add, [m, m_x[t]])
                else:
                    m = stt(x, y, scale, x, ALU.mult, ALU.add, [y_done[2 * t + hf], m_x[t]])
                    free[2 * t + hf] = m
            m_x[t] = m

    def fox():
        _, *fr_ = scope("fox", ("a", 20000, F32), ("h", 2048, F32R), ("l", 2048, F32R))
        stage_pack("fox", 19500)
        local["causal"] = A(19000, 384)
        GB[0] = A(17900, 1024)
        mods = MOD[:, 0:16]
        mca = load(C("causal"), ins["causal"])
        mh = make_h(mods[:, 0:8], mods[:, 8:16], [mod_done[0], mod_done[1]])
        CAT = [f[:, :].rearrange("p (c t) -> p c t", c=8) for f in fr_]
        QT = A(T00 + 2048, 1024).rearrange("p (c t) -> p c t", c=4)
        KT = A(T00 + 3072, 1024).rearrange("p (c t) -> p c t", c=4)
        V = A(T00 + 4096, 1024).rearrange("p (b n) -> p b n", b=2)
        U = [A(T00 + 5120 + 258 * n, 258) for n in range(2)]
        CC = [A(T00 + 5640 + 256 * n, 256) for n in range(2)]
        T0 = [A(T00 + 6152 + 256 * n, 256) for n in range(2)]
        SQ = [A(T00 + 6664 + 256 * n, 256) for n in range(2)]
        RR = [A(T00 + 7176 + 256 * n, 256) for n in range(2)]
        FL, FR = A(T00 + 7688, 256), A(T00 + 7944, 256)
        RH = [A(T00 + 8200 + 256 * n, 256) for n in range(2)]
        F = [A(T00 + 8712 + 256 * n, 256) for n in range(4)]
        cat, qk = {}, {}
        ms = [mset(U[n][:, 0:2], 0.0) for n in range(2)]
        gq = stat(1)
        mg = ts(gq, C("foxqg"), 0.125, None, ALU.mult)
        for j in range(4):
            b = j % 2
            n, ps, m = project("foxst", 3 * j, mh)
            mc = free[n] = act(CC[b], ps, ACT.Copy, [m, cat.get(j - 2)])
            n, ps, m = project("foxst", 3 * j + 1, mh)
            mu = free[n] = tt(U[b][:, 2:258], ps, CC[b], ALU.mult, [m, mc, ms[b], cat.get(j - 2)])
            cw = C("convw", 3 * j, 3 * j + 3)
            m1 = ts(T0[b], U[b][:, 0:256], cw[:, 0:1], None, ALU.mult, w=[mu, cat.get(j - 2)])
            m1 = stt(T0[b], U[b][:, 1:257], cw[:, 1:2], T0[b], ALU.mult, ALU.add, [m1])
            m1 = stt(T0[b], U[b][:, 2:258], cw[:, 2:3], T0[b], ALU.mult, ALU.add, [m1])
            n, ps, m = project("foxst", 3 * j + 2, mh)
            m1 = free[n] = tt(T0[b], ps, T0[b], ALU.mult, [m, m1])
            cat[j] = split(CAT[0][:, j, :], CAT[1][:, j, :], T0[b], [m1])
            background(2)
        for j in range(8):
            n, ps, m = project("foxst", 12 + j, mh)
            run_later()
            dst = QT[:, j, :] if j < 4 else KT[:, j - 4, :]
            head_norm(n, ps, m, dst, gq if j < 4 else C("foxkg"), SQ[j % 2], RR[j % 2], qk, j, [mg])
            background(2)
        n, ps, m = project("foxf", 0, mh)
        run_later()
        m = free[n] = ts(F[0], ps, C("bf"), None, ALU.add, w=[m])
        m = log1p_exp(F[1], F[0], F[2], F[3], FR, [m])
        m = stt(F[1], F[0], 0.0, F[1], ALU.min, ALU.subtract, [m])
        m2 = mset(F[3], 1.0, [m])
        m = DVE.put(lambda e: e.tensor_tensor_scan(F[2], F[3], F[1], 0.0, ALU.mult, ALU.add), [m, m2])
        mF = []
        for q in (0, 64):
            mF.append(copy(FL[q:q + 32, :], F[2][q:q + 32, :], [m]))
            mF.append(mset(FL[q + 32:q + 64, :], 1.0))
            mF.append(mset(FR[q:q + 32, :], 1.0, [m]))
            mF.append(ts(FR[q + 32:q + 64, :], F[2][q + 32:q + 64, :], -1.0, None, ALU.mult, w=[m]))
        m = rows512("foxv", mh)
        mv = []
        for t in range(2):
            mk = act(V[:, t, :], Y[t], ACT.Copy, [m])
            free[t] = mk
            mv.append(mk)
        H = Heads(T00 + 10000)
        H.next = ("foxo", 8, CAT, cat)
        H.rows = [(k, 1 + k) for k in range(4)]
        rh_free = [None, None]
        for h in range(8):
            pr = slice(64 * (h % 2), 64 * (h % 2) + 64)
            r = RH[h % 2][pr, :]
            mr = ts(r, FR[pr, :], C("headsel")[pr, h:h + 1], None, ALU.mult, w=[mF, rh_free[h % 2]])

            def scores(ps, fr, h=h, pr=pr, r=r, mr=mr):
                w = [fr, qk[h // 2], qk[4 + h // 2]]
                mm(ps[:, 0:128], QT[pr, h // 2, 0:128], KT[pr, h // 2, 0:128], True, False, w, inc=False)
                mm(ps[:, 0:128], FL[pr, 0:128], r[:, 0:128], False, True, [mr, mF], inc=False)
                mm(ps[:, 128:384], QT[pr, h // 2, 128:256], KT[pr, h // 2, :], True, False, inc=False)
                m = mm(ps[:, 128:384], FL[pr, 128:256], r, False, True)
                rh_free[h % 2] = m
                return m

            after = None
            if h % 2:
                def after(mk, n, ps, o, h=h):
                    cat[4 + h // 2] = free[n] = split(CAT[0][:, 4 + h // 2, :], CAT[1][:, 4 + h // 2, :],
                                                      ps[:, 0:256], [mk])
                    H.rows.append((4 + h // 2, H.i + 1))
            H.add(scores, C("causal"), lambda kb, h=h: V[:, kb, h * 64:h * 64 + 64],
                  (h % 2, mv, True, True, after), wmask=mca)
        H.step(True)
        mk = H.mk
        while bg:
            background()
        residual(1.0, True, mk, w=[mod_done[2]])

    def nsa():
        mods = MOD[:, 32:48]
        _, *fr_ = scope("nsa", ("a", 30000, F32), ("h", 2048, F32R), ("l", 2048, F32R))
        CAT = [f[:, :].rearrange("p (c t) -> p c t", c=8) for f in fr_]
        GB[0] = A(T00, 1024)
        stage_pack("nsa", T00 + 23500)
        local["causal"] = A(T00 + 1024, 384)
        local["cmpok"], local["cmpneg"] = A(T00 + 1408, 120), A(T00 + 1528, 120)
        QT = A(T00 + 2048, 2048).rearrange("p (c t) -> p c t", c=8)
        KK = [A(T00 + 4096 + 512 * n, 512).rearrange("p (c t) -> p c t", c=2) for n in range(4)]
        V = A(T00 + 6144, 1024).rearrange("p (b n) -> p b n", b=2)
        Z = [A(T00 + 7168 + 960 * n, 960) for n in range(2)]
        TB = A(T00 + 9088, 6144).rearrange("p (h k) -> p h k", h=16)
        CB = A(T00 + 15232, 480)
        G3 = A(T00 + 15712, 96).rearrange("p (t n) -> p t n", t=2)
        GS = A(T00 + 15808, 256)
        SQ = [A(T00 + 16064 + 256 * n, 256) for n in range(2)]
        RR = [A(T00 + 16576 + 256 * n, 256) for n in range(2)]
        HB = A(T00 + 17088, 128)
        KC = A(T00 + 17216, 64)
        H1R = A(T00 + 17280, 512)
        VC = A(T00 + 24000, 1024).rearrange("p (g j d) -> p g j d", g=4, j=4)
        PC = [A(T00 + 18048 + 256 * n, 256) for n in range(2)]
        PCT = A(T00 + 18560, 1024).rearrange("p (g t) -> p g t", g=4)
        mca = load(C("causal"), ins["causal"])
        mca = [mca, load(C("cmpok"), ins["cmpok"]), load(C("cmpneg"), ins["cmpneg"])]
        mtb = load(TB, ins["toep"].rearrange("p (h k) -> p h k", h=16))
        mcb = load(CB, ins["cmpb"])
        mh = make_h(mods[:, 0:8], mods[:, 8:16], [mod_done[6], mod_done[7]])
        z1 = mset(H1R, 0.0)
        z2 = [mset(PC[n], 0.0) for n in range(2)]
        ca = C("causal").unsqueeze(1).broadcast_to([128, 2, 384])
        mtl, mtb = mtb, []
        cn = C("cmpneg").unsqueeze(1).broadcast_to([128, 4, 120])
        cb4 = CB.rearrange("p (g n) -> p g n", g=4)
        mcb = tt(cb4, cb4, cn, ALU.add, [mcb, mca], q=PO)
        gq = stat(1)
        mg = ts(gq, C("nsaqg"), 0.125, None, ALU.mult)
        mz = []
        for j in range(8):
            n, ps, m = project("nsac", j, mh)
            kv, g = divmod(j, 4)
            zz = Z[kv].rearrange("p (l g n) -> p l g n", l=16, g=4)
            for par in range(2):
                pp = slice(64 * par, 64 * par + 64)
                src = bass_window(ps, pp, par)
                po = C("pos", 16 * kv, 16 * kv + 16)[pp, :].unsqueeze(2).broadcast_to([64, 16, 15])
                mk = tt(zz[pp, :, g, :], src, po, ALU.add, [m])
            free[n] = mk
            mz.append(mk)
            background()
        n, ps, m = project("nsag", 0, mh)
        m = free[n] = act(GS[0:48, :], ps[0:48, :], ACT.Sigmoid, [m], bias=C("bgate")[0:48, :])
        n, ps, fr = bank()
        for t in range(2):
            mk = tp(ps[:, t * 64:t * 64 + 48], GS[0:48, t * 128:t * 128 + 128], [fr, m], n=48)
        mgate = None
        for t in range(2):
            mgate = free[n] = copy(G3[:, t, :], ps[:, t * 64:t * 64 + 48], [mk])
        qk, kn = {}, {}
        for j in range(8):
            n, ps, m = project("nsaq", j, mh)
            run_later()
            head_norm(n, ps, m, QT[:, j, :], gq, SQ[j % 2], RR[j % 2], qk, j, [mg])
            mtb.append(tt(TB[:, 2 * j:2 * j + 2, :], TB[:, 2 * j:2 * j + 2, :], ca, ALU.add, [mtl, mca]))
            background()
        for j in range(4):
            n, ps, m = project("nsak", j, mh)
            run_later()
            head_norm(n, ps, m, KK[2 * (j // 2)][:, j % 2, :], C("nsakg", 1 + j // 2, 2 + j // 2),
                      SQ[j % 2], RR[j % 2], kn, j)
        for kv in range(2):
            w, mw, s = take("nsaw1", kv)
            n, ps, fr = bank()
            for l in range(16):
                mk = mm(ps[0:64, 0:60], w[:, l * 64:l * 64 + 64], Z[kv][:, l * 60:l * 60 + 60], l == 0, l == 15,
                        [fr, mw, mz[4 * kv + 3]])
            give(s, mk)
            if kv == 0:
                run_later()
                m = free[n] = act(HB[0:64, 0:60], ps[0:64, 0:60], ACT.Gelu_apprx_tanh, [mk])
                n, ps, fr = bank()
                m = mm(ps[:, 0:60], C("w2k")[0:64, :], HB[0:64, 0:60], True, True, [fr, m])
                a = act(KC[:, 0:60], ps[:, 0:60], ACT.Copy, [m])
                b = free[n] = act(SQ[0][:, 0:60], ps[:, 0:60], ACT.Square, [m, sq_free.get(id(SQ[0]))])
                n, ps, fr = bank()
                m = mm(ps[:, 0:60], C("bd64"), SQ[0][:, 0:60], True, True, [fr, b])
                c = free[n] = ts(RR[0][:, 0:60], ps[:, 0:60], 1.0 / 64, EPS, ALU.mult, ALU.add,
                                 w=[m, rr_free.get(id(RR[0]))])
                c = rec(RR[0][:, 0:60], RR[0][:, 0:60], [act(RR[0][:, 0:60], RR[0][:, 0:60], ACT.Sqrt, [c])])
                mkc = stt(KC[:, 0:60], KC[:, 0:60], C("nsakg", 0, 1), RR[0][:, 0:60], ALU.mult, ALU.mult, [a, c])
            else:
                m = free[n] = act(HB[0:64, 64:124], ps[0:64, 0:60], ACT.Gelu_apprx_tanh, [mk])
                h1 = H1R[0:64, :].rearrange("p (g j n) -> p g j n", g=4, j=4)
                for g in range(4):
                    m2 = copy(h1[:, g, :, 0:15],
                              HB[0:64, 64 + 15 * g:79 + 15 * g].unsqueeze(1).broadcast_to([64, 4, 15]), [m, z1])
                n, ps, fr = bank()
                for g in range(4):
                    m = mm(ps[:, g * 64:g * 64 + 64], H1R[0:64, g * 128:g * 128 + 128], C("w2v")[0:64, :], True,
                           True, [fr, m2])
                for j in range(4):
                    mvc = free[n] = ts(VC[:, :, j, :], ps[:, 0:256].rearrange("p (g d) -> p g d", g=4),
                                       C("rowsel")[:, j:j + 1], None, ALU.mult, w=[m])
        msw = []
        s_sw = new_sem("swap")
        for n in range(2):
            for hf in range(2):
                o = KK[2 * n + 1][64 * hf:64 * hf + 64, :, :]
                i = KK[2 * n][64 - 64 * hf:128 - 64 * hf, :, :]
                PO.dma(lambda e, o=o, i=i: e.dma_start(o, i), [kn[2 * n], kn[2 * n + 1]], s_sw)
        msw = (s_sw, 64)
        m = rows512("nsav", mh)
        mv = []
        for t in range(2):
            mk = act(V[:, t, :], Y[t], ACT.Copy, [m])
            free[t] = mk
            mv.append(mk)
        mpc = {}
        pcf = [z2[0], z2[1]]
        for g in range(4):
            sc = A(T00 + 19600 + 128 * (g % 2), 120).rearrange("p (j n) -> p j n", n=15)
            sc3 = A(T00 + 19600 + 128 * (g % 2), 120).rearrange("p (t j n) -> p t j n", t=2, n=15)
            cb3 = CB[:, g * 120:g * 120 + 120].rearrange("p (t j n) -> p t j n", t=2, n=15)
            ma = []
            for odd in range(2):
                pr = slice(64 * odd, 64 * odd + 64)
                n, ps, fr = bank()
                for j in range(2):
                    for t in range(2):
                        m = mm(ps[:, (t * 2 + j) * 16:][:, 0:15], QT[pr, 2 * g + j, t * 128:t * 128 + 128],
                               KC[pr, 15 * g:15 * g + 15], True, True, [fr, mkc, qk[7]])
                pv = ps[:, 0:64].rearrange("p (t j n) -> p t j n", t=2, n=16)[:, :, :, 0:15]
                free[n] = tt(sc3[:, :, odd:4:2, :], pv, cb3[:, :, odd:4:2, :], ALU.add, [m, mcb])
                ma.append(free[n])
            m = ma
            s8 = stat(16)
            mx, sm = s8[:, 0:8], s8[:, 8:16]
            m = red(mx, sc, ALU.max, [m], neg=True)
            m = tt(sc, sc, mx.unsqueeze(2).broadcast_to([128, 8, 15]), ALU.add, [m])
            m = act(sc, sc, ACT.Exp, [m])
            m = red(sm, sc, ALU.add, [m])
            m = rec(sm, sm, [m])
            gt = G3[:, :, 12 * g:12 * g + 12].rearrange("p t (j c) -> p t j c", c=3)[:, :, :, 0]
            m = tt(sm.rearrange("p (t j) -> p t j", t=2), sm.rearrange("p (t j) -> p t j", t=2), gt, ALU.mult,
                   [m, mgate])
            m = tt(sc, sc, sm.unsqueeze(2).broadcast_to([128, 8, 15]), ALU.mult, [m])
            pc = PC[g % 2].rearrange("p (j n) -> p j n", n=32)[:, :, 0:15]
            m = tt(pc, sc, C("cmpok").rearrange("p (j n) -> p j n", n=15), ALU.mult, [m, pcf[g % 2]])
            n, ps, fr = bank()
            for t in range(2):
                mk = tp(ps[:, t * 128:t * 128 + 128], PC[g % 2][:, t * 128:t * 128 + 128], [fr, m])
            pcf[g % 2] = mk
            mpc[g] = free[n] = act(PCT[:, g, :], ps[:, 0:256], ACT.Copy, [mk])
        H = Heads(T00 + 20000)
        cat = {}
        H.next = ("nsao", 8, CAT, cat)
        for h in range(16):
            g, j = divmod(h, 4)
            pr = slice(64 * (h % 2), 64 * (h % 2) + 64)
            for b in range(2):
                src = KK[2 * b + (0 if g % 2 == h % 2 else 1)]

                def scores(ps, fr, h=h, pr=pr, src=src, g=g, b=b):
                    w = [fr, qk[h // 2], kn[2 * b + g // 2], msw]
                    mm(ps[:, 0:128], QT[pr, h // 2, 0:128], src[pr, g // 2, 0:128], True, True, w, inc=False)
                    return mm(ps[:, 128:384], QT[pr, h // 2, 128:256], src[pr, g // 2, :], True, True)

                after = None
                if b == 1:
                    def after(mk, n, ps, o, h=h, g=g, j=j):
                        m = mm(o, VC[:, g, j, :], PCT[:, g, :], False, True, [mpc[g], mvc])
                        if h % 2:
                            cat[h // 2] = free[n] = split(CAT[0][:, h // 2, :], CAT[1][:, h // 2, :],
                                                          ps[:, 0:256], [m])
                            H.rows.append((h // 2, H.i + 1))
                gt = G3[:, :, 3 * h + 1 + b]
                H.add(scores, TB[:, h, :], lambda kb, g=g, b=b: V[:, kb, b * 256 + g * 64:b * 256 + g * 64 + 64],
                      (h % 2, mv, b == 0, False, after), gate=(gt, mgate), wmask=mtb)
        H.step(True)
        mk = H.mk
        while bg:
            background()
        residual(1.0, True, mk, w=[mod_done[8]])

    def bass_window(ps, pp, par):
        base = ps[pp, par:par + 1]
        return bass.AP(base.tensor, base.offset, [base.ap[0], [2, 16], [16, 15]])

    def peer(l):
        p0 = 6 * l
        mods = MOD[:, 16 * (2 * l + 1):16 * (2 * l + 1) + 16]
        *_, OXt = scope(f"peer{l}x", ("a", 32768, F32), ("tij", 768, F32), ("oh", 512, F32), ("ox", 1024, F32))
        _, TIJt, OHt, WHt, WLt = scope(f"peer{l}", ("a", 32768, F32), ("tij", 768, F32), ("oh", 512, F32),
                                       ("wh", 512, F32R), ("wl", 512, F32R))
        B = 16384
        local.clear()
        KEYS = A(B, 256)
        mkey = load(KEYS, ins[f"keys{l}"])
        QT = A(T00, 2048).rearrange("p (c t) -> p c t", c=8)
        mh = make_h(mods[:, 0:8], mods[:, 8:16], [mod_done[p0 + 3], mod_done[p0 + 4]])
        qd = {}
        lo_q[0] = PO
        for j in range(8):
            n, ps, m = project(f"pq{l}", j, mh)
            qd[j] = free[n] = act(QT[:, j, :], ps, ACT.Copy, [m])
        SB = [A(T00 + 2048 + 2048 * t, 2048) for t in range(2)]
        EQ = A(0, 2048).rearrange("p (k a) -> p k a", a=16)
        E2 = A(2048, 2048).rearrange("p (k a) -> p k a", a=16)
        SI = A(10240, 512).bitcast(U32)
        SV = A(10752, 512)
        SF = A(11264, 512)
        CV = A(11776, 256)
        CI = A(12032, 256).bitcast(U32)
        CA, CBf = A(12288, 256), A(12544, 256)
        CU = A(12800, 256).bitcast(U32)
        EI = A(13056, 256)
        EJ = A(13312, 256)
        GG = A(13568, 256)
        TI = [TIJt[:, 256 * n:256 * n + 256] for n in range(3)]
        ms = {}
        for t in range(2):
            for hp in range(4):
                n, ps, fr = bank()
                for h in range(2):
                    m = mm(ps[:, h * 256:h * 256 + 256], QT[:, 2 * hp + h, t * 128:t * 128 + 128], KEYS,
                           True, True, [fr, qd[2 * hp + h], mkey])
                S = SB[t].rearrange("p (s k) -> p s k", s=16)
                ms[t, hp] = free[n] = act(S[:, 4 * hp:4 * hp + 4, :], ps.rearrange("p (s k) -> p s k", s=4),
                                          ACT.Copy, [m])
        last_key = m

        def top16(src, v, ix, w):
            a, b = v[:, 0:8], v[:, 8:16]
            i0, i1 = ix[:, 0:8], ix[:, 8:16]
            m = DVE.put(lambda e: e.max(a, src), w)
            m = DVE.put(lambda e: e.max_index(i0, a, src), [m])
            m = DVE.put(lambda e: e.match_replace(src, a, src, NEG * 1e6), [m])
            m = DVE.put(lambda e: e.max(b, src), [m])
            return DVE.put(lambda e: e.max_index(i1, b, src), [m])

        def experts(t):
            S = SB[t].rearrange("p (s k) -> p s k", s=16)
            sv = SV[:, 256 * t:256 * t + 256].rearrange("p (s k) -> p s k", s=16)
            si = SI[:, 256 * t:256 * t + 256].rearrange("p (s k) -> p s k", s=16)
            for s in range(16):
                m = top16(S[:, s, :], sv[:, s, :], si[:, s, :], [ms[t, s // 4]])
            sf = SF[:, 256 * t:256 * t + 256]
            mf = copy(sf, SI[:, 256 * t:256 * t + 256], [m])
            sv4 = sv.rearrange("p (h q) k -> p h q k", q=2)
            CD = SB[t]
            m = tt(CD.rearrange("p (h a b) -> p h a b", h=8, a=16),
                   sv4[:, :, 0, :].unsqueeze(3).broadcast_to([128, 8, 16, 16]),
                   sv4[:, :, 1, :].unsqueeze(2).broadcast_to([128, 8, 16, 16]), ALU.add, [m])
            cv = CV[:, 128 * t:128 * t + 128].rearrange("p (h k) -> p h k", h=8)
            ci = CI[:, 128 * t:128 * t + 128].rearrange("p (h k) -> p h k", h=8)
            mc = m
            for h in range(8):
                m = top16(CD[:, h * 256:h * 256 + 256], cv[:, h, :], ci[:, h, :], [mc])
            cit, cut = CI[:, 128 * t:128 * t + 128], CU[:, 128 * t:128 * t + 128]
            ca, cb = CA[:, 128 * t:128 * t + 128], CBf[:, 128 * t:128 * t + 128]
            m1 = ts(cut, cit, 4, None, ALU.logical_shift_right, w=[m])
            m1 = copy(ca, cut, [m1])
            m2 = ts(cut, cit, 15, None, ALU.bitwise_and, w=[m1])
            m2 = copy(cb, cut, [m2])
            s4 = sf.rearrange("p (h q k) -> p h q k", h=8, q=2)
            io = C("iota")[:, 0:16].unsqueeze(1).broadcast_to([128, 128, 16])
            for q, (src, dst, eq) in enumerate(((ca, EI, EQ), (cb, EJ, E2))):
                m = tt(eq, src.unsqueeze(2).broadcast_to([128, 128, 16]), io, ALU.is_equal, [m2])
                eq4 = eq.rearrange("p (h k) a -> p h k a", h=8)
                m = tt(eq4, eq4, s4[:, :, q, :].unsqueeze(2).broadcast_to([128, 8, 16, 16]), ALU.mult, [m, mf])
                me = red(dst[:, 128 * t:128 * t + 128], eq, ALU.add, [m])
            gg = GG[:, 128 * t:128 * t + 128].rearrange("p (h k) -> p h k", h=8)
            return gg, tt(gg, cv, cv[:, :, 0:1].broadcast_to([128, 8, 16]), ALU.subtract, [me])

        def softmax(t, gg, m):
            m = act(gg, gg, ACT.Exp, [m])
            st = stat(8)
            m = red(st, gg, ALU.add, [m])
            m = rec(st, st, [m])
            return tt(gg, gg, st.unsqueeze(2).broadcast_to([128, 8, 16]), ALU.mult, [m])

        def turned(t, mg):
            n, ps, fr = bank()
            for q, src in enumerate((EI, EJ, GG)):
                mk = tp(ps[:, q * 128:q * 128 + 128], src[:, 128 * t:128 * t + 128], [fr, mg])
            for q in range(3):
                mti = free[n] = copy(TI[q][:, t * 128:t * 128 + 128], ps[:, q * 128:q * 128 + 128], [mk])
            return mti

        G1 = A(0, B).rearrange("p (t j) -> p t j", j=64)
        G2 = A(B, B).rearrange("p (t j) -> p t j", j=64)
        io = C("iota")
        OH = [(v[:, c:c + 128], v[:, c + 128:c + 256]) for v, c in
              [(OHt, 0), (OHt, 256)] + [(OXt, 256 * n) for n in range(4)]]
        ohf = [None] * 6
        mti = []

        gs = {}

        def gate(t, part, dst, w):
            if t % 4 == 0:
                gs["bank"] = bank()
            n, ps, fr = gs["bank"]
            b, q = t % (2 if part else 6), t % 4
            o1, o2 = OH[b]
            a = ts(o1, io, TI[0][:, t:t + 1], None, ALU.is_equal, w=[mti, ohf[b]])
            c = ts(o2, io, TI[1][:, t:t + 1], TI[2][:, t:t + 1], ALU.is_equal, ALU.mult, w=[mti, ohf[b]])
            ohf[b] = mm(ps[:, q * 128:q * 128 + 128], o1, o2, True, True, [fr, a, c])
            if q == 3:
                gs["m"] = free[n] = act(dst[:, t - 3:t + 1, :],
                                        ps.rearrange("p (t j) -> p t j", t=4)[:, :, 64 * part:64 * part + 64],
                                        ACT.Copy, [ohf[b], w])

        mge = {}

        def up(j, dst, w, between=None):
            n, ps, mk = project(f"pu{l}", j, mh, between)
            free[n] = act(dst, ps, ACT.Gelu_apprx_tanh, [mk, w])
            return free[n]

        gt = [0]

        def some_gates():
            for _ in range(2):
                if gt[0] < 256:
                    gate(gt[0], 0, G1, mti)
                    gt[0] += 1

        for j in range(64):
            mge[j] = up(j, A(B + 256 * j, 256), [last_key], some_gates if j > SECOND_T else None)
            if j == 0:
                me = [experts(0), experts(1)]
            if j == SECOND_T:
                for t in range(2):
                    mti.append(turned(t, softmax(t, *me[t])))
        while gt[0] < 256:
            some_gates()
        mg1 = gs["m"]
        WH = [WHt[:, 256 * n:256 * n + 256] for n in range(2)]
        WL = [WLt[:, 256 * n:256 * n + 256] for n in range(2)]
        wtf, wt_m = [None, None], {}

        def weigh_hi(j, ge, g, w):
            b = j % 2
            m = tt(ge, ge, g, ALU.mult, w)
            wt_m[j] = [act(WH[b], ge, ACT.Copy, [m, wtf[b]])]

        def weigh_lo(j, ge):
            b = j % 2
            wt_m[j].append(tt(WL[b], ge, f32(WH[b]), ALU.subtract, [wt_m[j][0]]))

        def weigh(j, ge, g, w):
            weigh_hi(j, ge, g, w)
            weigh_lo(j, ge)

        def down(j, between=None):
            b = j % 2
            wtf[b] = rows_slot(j, 128, take(f"pv{l}", j), [WH[b], WL[b]], wt_m[j], between)
            return wtf[b]

        weigh(0, A(B, 256), G1[:, :, 0], [mge[0], mg1])
        for j in range(63):
            left = [4 * j]

            def one_gate():
                gate(left[0], 1, G2, wt_m[left[0] // 4])
                left[0] += 1
                n = (left[0] - 1) // 4 + 1
                if (left[0] - 1) % 4 == WAT[0]:
                    weigh_hi(n, A(B + 256 * n, 256), G1[:, :, n], [mge[n], mg1])
                if (left[0] - 1) % 4 == WAT[1]:
                    weigh_lo(n, A(B + 256 * n, 256))

            down(j, one_gate)
            if len(bg) > 10 and j % 2:
                background()
        down(63)
        for t in range(252, 256):
            gate(t, 1, G2, wt_m[63])
        mg2 = gs["m"]
        GB[0] = A(HR, 1024)
        GE = [TIJt[:, 256 * n:256 * n + 256] for n in range(3)]
        total = len(bg)
        gef = [ohf[0:2], ohf[0:2], ohf[0:2]]
        for q in (PE, DVE, SC, PO):
            q.pending = q.pending + [wt_m[63], mg2]
        for j in range(64, 128):
            lo_q[0] = DVE
            m = up(j, GE[j % 3], gef[j % 3])
            weigh(j, GE[j % 3], G2[:, :, j - 64], [m, mg2])
            gef[j % 3] = wt_m[j]
            lo_q[0] = PO
            if j > 64:
                down(j - 1)
            lo_q[0] = DVE
            if j % 3 == 0:
                background()
        lo_q[0] = PO
        mk = down(127)
        lo_q[0] = DVE
        while bg:
            background()
        residual(1.0, True, mk, w=[mod_done[p0 + 5], wt_m[127]])

    def ffn(nm, l):
        _, *fr_ = scope(f"ffn{nm}{l}", ("a", 6000, F32), ("h", 22 * 256, F32R), ("l", 22 * 256, F32R))
        AC = [f[:, :].rearrange("p (c t) -> p c t", c=22) for f in fr_]
        stage_pack(f"ffn{nm}{l}", 5000)
        mh = make_h(C(f"fn{'1' if nm == 'A' else '2'}_{l}"), None, None)
        SG = [A(T00 + 256 * n, 256) for n in range(2)]
        ma = {}
        for j in range(22):
            n, ps, m = project(f"fg{nm}{l}", j, mh)
            g = free[n] = act(SG[j % 2], ps, ACT.Silu, [m, ma.get(j - 2)])
            n, ps, m = project(f"fu{nm}{l}", j, mh)
            g = free[n] = tt(SG[j % 2], ps, SG[j % 2], ALU.mult, [m, g])
            ma[j] = split(AC[0][:, j, :], AC[1][:, j, :], SG[j % 2], [g])
        mk = rows_out(f"fd{nm}{l}", 22, lambda k: [AC[0][:, k, :], AC[1][:, k, :]], lambda k: ma[k])
        residual(0.5, False, mk)

    def ssd(l):
        _, *fr_ = scope(f"ssd{l}", ("a", 26624 + places[f"ssd{l}"]["width"], F32), ("h", 4096, F32R), ("l", 4096, F32R))
        CAT = [f[:, :].rearrange("p (c t) -> p c t", c=16) for f in fr_]
        XC = A(0, 4096).rearrange("p (c t) -> p c t", c=16)
        XT = A(4096, 2048).rearrange("p (c n) -> p c n", c=2)
        XD = A(6144, 2048).rearrange("p (c n) -> p c n", c=2)
        ZS = A(8192, 2048).rearrange("p (c n) -> p c n", c=2)
        BT = A(10240, 512)
        ST = A(10752, 1024)
        XE = A(11776, 1024)
        YS = A(12800, 2048).rearrange("p (c n) -> p c n", c=2)
        QT = A(14848, 2048).rearrange("p (c t) -> p c t", c=8)
        KT = A(16896, 2048).rearrange("p (c t) -> p c t", c=8)
        V = A(18944, 2048).rearrange("p (b n) -> p b n", b=2)
        XB = [A(20992 + 260 * n, 259) for n in range(2)]
        T0 = [A(21512 + 256 * n, 256) for n in range(2)]
        SQ = [A(22024 + 256 * n, 256) for n in range(2)]
        RR = [A(22536 + 256 * n, 256) for n in range(2)]
        D = [A(23048 + 256 * n, 256) for n in range(5)]
        stage_pack(f"ssd{l}", 26624)
        local["le"], local["gt"] = A(18944, 128), A(19072, 128)
        mlg = load(A(18944, 256), ins["legt"])
        local["dilmask"], local["dilmult"] = A(23048, 384), A(23432, 384)
        DT = A(24328, 64)
        EA = A(24392, 32)
        CM = A(20992, 1024)
        mh = make_h(C(f"mixn_{l}"), None, None)
        an = stat(1)
        ma = act(an[0:16, :], C(f"alog_{l}")[0:16, :], ACT.Exp)
        mxc = {}
        mz = [mset(XB[n][:, 0:3], 0.0) for n in range(2)]
        for j in range(16):
            b = j % 2
            n, ps, m = project(f"sx{l}", j, mh)
            mk = free[n] = act(XB[b][:, 3:259], ps, ACT.Copy, [m, mz[b], mxc.get(j - 2)])
            cw, cb = C(f"cw_{l}", 4 * j, 4 * j + 4), C(f"cb_{l}", j, j + 1)
            mk = ts(T0[b], XB[b][:, 0:256], cw[:, 0:1], cb, ALU.mult, ALU.add, w=[mk, mxc.get(j - 2)])
            for k in range(1, 4):
                mk = stt(T0[b], XB[b][:, k:k + 256], cw[:, k:k + 1], T0[b], ALU.mult, ALU.add, [mk])
            mxc[j] = act(XC[:, j, :], T0[b], ACT.Silu, [mk])
        dt = DT[:, 0:32].rearrange("p (t h) -> p t h", t=2)
        ad = DT[:, 32:64].rearrange("p (t h) -> p t h", t=2)
        n, ps, m = project(f"sd{l}", 0, mh)
        x = D[0][0:16, :]
        m = free[n] = ts(x, ps[0:16, :], C(f"dtb_{l}")[0:16, :], None, ALU.add, w=[m])
        m = log1p_exp(D[1][0:16, :], x, D[2][0:16, :], D[3][0:16, :], D[4][0:16, :], [m])
        m = stt(D[0][0:16, :], x, 0.0, D[1][0:16, :], ALU.max, ALU.add, [m])
        mdt = ts(D[1][0:16, :], D[0][0:16, :], an[0:16, :], -1.0, ALU.mult, ALU.mult, w=[m, ma])
        m = rows_out(f"sz{l}", 8, ht, lambda k: mh)
        for t in range(2):
            for hf in range(2):
                mzs = free[2 * t + hf] = act(ZS[:, t, hf * 512:hf * 512 + 512], Y[2 * t + hf], ACT.Silu, [m])
        n2, p2, fr = bank()
        for q in range(2):
            for t in range(2):
                mk = tp(p2[:, (2 * q + t) * 16:][:, 0:16], D[q][0:16, t * 128:t * 128 + 128], [fr, mdt],
                        n=16)
        mDT = free[n2] = copy(DT, p2[:, 0:64], [mk])
        mxt = []
        for t in range(2):
            for c4 in range(2):
                n, ps, fr = bank()
                for c in range(4):
                    mk = tp(ps[:, c * 128:c * 128 + 128], XC[:, 4 * c4 + c, t * 128:t * 128 + 128],
                            [fr, mxc[4 * c4 + c]])
                free[n] = act(XT[:, t, c4 * 512:c4 * 512 + 512], ps, ACT.Copy, [mk])
                mxt.append(free[n])
        n, ps, fr = bank()
        for c in range(4):
            mk = tp(ps[:, c * 128:c * 128 + 128], XC[:, 8 + c, 0:128], [fr, mxc[11]])
        mbt = free[n] = act(BT, ps, ACT.Copy, [mk])
        mxd = []
        for t in range(2):
            mxd.append(tt(XD[:, t, :].rearrange("p (h e) -> p h e", h=16),
                          XT[:, t, :].rearrange("p (h e) -> p h e", h=16),
                          dt[:, t, :].unsqueeze(2).broadcast_to([128, 16, 64]), ALU.mult, [mxt, mDT]))
        n, ps, fr = bank()
        mm(ps[:, 0:16], C("gt"), ad[:, 0, :], True, True, [fr, mDT, mlg])
        m = mm(ps[:, 16:32], C("le"), ad[:, 1, :], True, True)
        mea = free[n] = act(EA, ps[:, 0:32], ACT.Exp, [m])
        mxe = tt(XE.rearrange("p (h e) -> p h e", h=16), XD[:, 0, :].rearrange("p (h e) -> p h e", h=16),
                 EA[:, 0:16].unsqueeze(2).broadcast_to([128, 16, 64]), ALU.mult, [mxd[0], mea], q=PO)
        mcm = {}
        for c in range(2):
            n, ps, fr = bank()
            for g in range(4):
                mk = mm(ps[:, g * 128:g * 128 + 128], XC[:, 8 + g, c * 128:c * 128 + 128],
                        XC[:, 12 + g, c * 128:c * 128 + 128], True, True, [fr, mxc[15]])
            mcm[c] = free[n] = tt(CM[:, c * 512:c * 512 + 512].rearrange("p (g l) -> p g l", g=4),
                                  ps.rearrange("p (g l) -> p g l", g=4),
                                  C("le").unsqueeze(1).broadcast_to([128, 4, 128]), ALU.mult, [mk, mlg])
        for hf in range(2):
            n, ps, fr = bank()
            for q in range(2):
                g = 2 * hf + q
                mk = mm(ps[:, q * 256:q * 256 + 256], BT[:, g * 128:g * 128 + 128], XE[:, g * 256:g * 256 + 256],
                        True, True, [fr, mbt, mxe])
            mst = free[n] = act(ST[:, hf * 512:hf * 512 + 512], ps, ACT.Copy, [mk])
        dsk = C(f"dsk_{l}").unsqueeze(2).broadcast_to([128, 16, 64])
        mys = []
        for t in range(2):
            mys.append(tt(YS[:, t, :].rearrange("p (h e) -> p h e", h=16),
                          XT[:, t, :].rearrange("p (h e) -> p h e", h=16), dsk, ALU.mult, [mxt], q=PO))
        gq = stat(1)
        mg = ts(gq, C(f"dqg_{l}"), 0.125, None, ALU.mult)
        qk, qkj = {}, [0]

        def qk_slot():
            j = qkj[0]
            if j == 16:
                return
            qkj[0] += 1
            n, ps, m = project(f"sqk{l}", j, mh)
            run_later()
            dst = QT[:, j, :] if j < 8 else KT[:, j - 8, :]
            head_norm(n, ps, m, dst, gq if j < 8 else C(f"dkg_{l}"), SQ[j % 2], RR[j % 2], qk, j, [mg])

        WB = [A(24576, 512), A(25088, 512)]
        EB = [A(25600, 512), A(26112, 512)]
        wbf, ebf = [None, None], [None, None]
        todo = []

        def diag(c, g, e, me):
            for r in range(4):
                h = 4 * g + r
                yo = Y[2 * c + h // 8][:, (h % 8) * 64:(h % 8) * 64 + 64]
                mk = mm(yo, e[:, r * 128:r * 128 + 128], XD[:, c, h * 64:h * 64 + 64], True, True,
                        [me, mxd[c]] + [free[2 * c + h // 8]])
            return mk

        mdg = {}
        def seg(i):
            c, g = divmod(i, 4)
            return tt(WB[i % 2].rearrange("p (r s) -> p r s", r=4), C("gt").unsqueeze(1).broadcast_to([128, 4, 128]),
                      ad[:, c, 4 * g:4 * g + 4].unsqueeze(2).broadcast_to([128, 4, 128]), ALU.mult,
                      [mDT, wbf[i % 2], mlg], q=PO)

        mseg = {0: seg(0)}
        for i in range(8):
            c, g = divmod(i, 4)
            b = i % 2
            if i < 7:
                mseg[i + 1] = seg(i + 1)
            m = mseg[i]
            n, ps, fr = bank()
            for r in range(4):
                mk = mm(ps[:, r * 128:r * 128 + 128], WB[b][:, r * 128:r * 128 + 128], C("le"), True, True,
                        [fr, m])
            wbf[b] = mk
            me = free[n] = act(EB[b], ps, ACT.Exp, [mk, ebf[b]])
            me = tt(EB[b].rearrange("p (r l) -> p r l", r=4), EB[b].rearrange("p (r l) -> p r l", r=4),
                    CM[:, c * 512 + g * 128:c * 512 + g * 128 + 128].unsqueeze(1).broadcast_to([128, 4, 128]),
                    ALU.mult, [me, mcm[c]])
            if todo:
                i2, args = todo.pop()
                mdg[i2] = ebf[i2 % 2] = diag(*args)
            todo.append((i, (c, g, EB[b], me)))
            qk_slot()
        i2, args = todo.pop()
        mdg[i2] = diag(*args)
        moff = []
        qk_slot()
        for hf in range(2):
            n, ps, fr = bank()
            for q in range(2):
                g = 2 * hf + q
                mk = mm(ps[:, q * 256:q * 256 + 256], XC[:, 12 + g, 128:256], ST[:, g * 256:g * 256 + 256], True,
                        True, [fr, mst])
            tmp = XE[:, hf * 512:hf * 512 + 512]
            m = free[n] = tt(tmp.rearrange("p (h e) -> p h e", h=8), ps.rearrange("p (h e) -> p h e", h=8),
                             EA[:, 16 + 8 * hf:24 + 8 * hf].unsqueeze(2).broadcast_to([128, 8, 64]), ALU.mult,
                             [mk, mea, mst])
            ys = YS[:, 1, hf * 512:hf * 512 + 512]
            moff.append(tt(ys, ys, tmp, ALU.add, [m, mys[1]]))
        st = stat(16)
        m2 = None
        for t in range(2):
            for hf in range(2):
                ys = YS[:, t, hf * 512:hf * 512 + 512]
                m = free[2 * t + hf] = tt(ys, ys, Y[2 * t + hf], ALU.add, [mdg[7], mdg[4 * t + 3], mys[t], moff])
                m = tt(ys, ys, ZS[:, t, hf * 512:hf * 512 + 512], ALU.mult, [m, mzs])
                qk_slot()
            for g in range(4):
                m2 = act(XE[:, g * 256:g * 256 + 256], YS[:, t, g * 256:g * 256 + 256], ACT.Square,
                         [m, moff, m2],
                         acc=st[:, 4 * t + g:4 * t + g + 1])
        m = ts(st[:, 0:8], st[:, 0:8], 1.0 / 256, EPS, ALU.mult, ALU.add, w=[m2], q=PO)
        mr = tt(st[:, 8:16], st[:, 0:8], NH(8), ALU.pow, [m], q=PO)
        mn = []
        for t in range(2):
            mn.append(tt(YS[:, t, :].rearrange("p (g e) -> p g e", g=4),
                         YS[:, t, :].rearrange("p (g e) -> p g e", g=4),
                         st[:, 8 + 4 * t:12 + 4 * t].unsqueeze(2).broadcast_to([128, 4, 256]), ALU.mult, [mr],
                         q=PO if t else DVE))
        while qkj[0] < 16:
            qk_slot()
        cat = {}
        run_later()
        m = rows_out(f"sv{l}", 8, ht, lambda k: mh)
        for t in range(2):
            for hf in range(2):
                mv = free[2 * t + hf] = act(V[:, t, hf * 512:hf * 512 + 512], Y[2 * t + hf], ACT.Copy,
                                            [m, mdg[7], mcm[1], me])
        def ssd_part():
            mk = None
            for c2 in range(4):
                n, ps, fr = bank()
                for q in range(2):
                    for t in range(2):
                        c = 2 * c2 + q
                        mk = tp(ps[:, q * 256 + t * 128:][:, 0:128], YS[:, t, c * 128:c * 128 + 128], [fr, mn])
                for q in range(2):
                    c = 2 * c2 + q
                    src, g1 = ps[:, q * 256:q * 256 + 256], C(f"ssdn_{l}")[:, c:c + 1]
                    a = act(CAT[0][:, c, :], src, ACT.Copy, [mk], scale=g1)
                    b = free[n] = stt(CAT[1][:, c, :], src, g1, f32(CAT[0][:, c, :]), ALU.mult, ALU.subtract, [a])
                    mk = [mk, b]
                    cat[c] = [a, b]

        H = Heads(0)
        H.next = (f"so{l}", 16, CAT, cat)
        H.sf = [[mxc[15], mst, mdg[7], mk, moff]] * 4
        H.pf = [[mdg[7], mst, mk, mk, moff]] * 4
        mdm = [load(C("dilmask"), ins["dilmask"], [mDT, mdt]), load(C("dilmult"), ins["dilmult"], [mDT, mdt])]
        for h in range(16):
            pr = slice(64 * (h % 2), 64 * (h % 2) + 64)

            def scores(ps, fr, h=h, pr=pr):
                w = [fr, qk[h // 2], qk[8 + h // 2]]
                mm(ps[:, 0:128], QT[pr, h // 2, 0:128], KT[pr, h // 2, 0:128], True, True, w, inc=False)
                return mm(ps[:, 128:384], QT[pr, h // 2, 128:256], KT[pr, h // 2, :], True, True)

            after = None
            if h % 2:
                def after(mk, n, ps, o, h=h):
                    cat[8 + h // 2] = free[n] = split(CAT[0][:, 8 + h // 2, :], CAT[1][:, 8 + h // 2, :],
                                                      ps[:, 0:256], [mk])
                    H.rows.append((8 + h // 2, H.i + 1))
            H.add(scores, C("dilmask"), lambda kb, h=h: V[:, kb, h * 64:h * 64 + 64],
                  (h % 2, mv, True, True, after), mult=C("dilmult"), wmask=mdm)
            if h == 1:
                ssd_part()
                H.rows = [(k, k + 2) for k in range(8)]
        H.step(True)
        mk = H.mk
        residual(1.0, False, mk)

    need = [s for s in stages]
    if need and need[0] in ("mix0", "peer0", "mix1", "peer1"):
        sg = stat(8)
        m = act(sg, C("c"), ACT.Sigmoid)
        sc_m[0] = tt(silu_c, C("c"), sg, ALU.mult, [m])
    for s in stages:
        l = int(s[-1])
        lo_q[0] = DVE if s[:3] == "ffn" else PO
        if s == "mix0":
            scope("fox", ("a", 20000, F32), ("h", 2048, F32R), ("l", 2048, F32R))
            begin = [ada_piece(p, A(HR + 1024 + 1024 * p, 1024)) for p in (0, 1)]
            for part in (slice(0, 1), slice(1, 9), slice(9, 10)):
                for steps in begin:
                    for f in steps[part]:
                        f()
            for p in (2, 3, 4):
                bg.extend(ada_piece(p))
            fox()
        elif s == "mix1":
            if stages[0] == "mix1":
                for p in (6, 7):
                    for f in ada_piece(p):
                        f()
                for p in (8, 9, 10):
                    bg.extend(ada_piece(p))
            nsa()
        elif s[:4] == "peer":
            p0 = 6 * l
            if stages[0] == s:
                for p in (6 * l + 3, 6 * l + 4):
                    for f in ada_piece(p):
                        f()
            if l == 0 and "mix1" in stages:
                for p in (6, 7, 9, 10):
                    bg.extend(ada_piece(p))
            bg.extend(ada_piece(p0 + 5))
            peer(l)
            if l == 0 and "mix1" in stages:
                bg.extend(ada_piece(8))
        elif s[:3] == "ffn":
            ffn(s[3], l)
        else:
            ssd(l)
        fence()
    s_out = new_sem("out")
    for t in range(2):
        o = out.rearrange("a (t p) n -> (a t) p n", p=128)[t]
        SC.pending = []
        SC.dma(lambda e, o=o, t=t: e.dma_start(o, X[:, t, :]), [m_x[t]], s_out)
    SC.ops.append(("wait", s_out, 32))

    for n, src in enumerate(stream):
        w = [raw_free.get(n - NR)]
        o = RINGt[:, (n % NR) * 1024:(n % NR + 1) * 1024]
        SP.dma(lambda e, o=o, src=src: e.dma_start(o, src), w, ring_sem[n % NR])
    return (PE, DVE, SC, PO, SP), order


def kernel(**inputs):
    import concourse.bacc as _bacc
    from concourse.bass_utils import run_bass_kernel_spmd as _run

    nc = _bacc.Bacc("TRN2", target_bir_lowering=False, num_devices=1)
    arrays = lay_out(inputs)
    ins = {k: nc.dram_tensor(f"in_{k}", v.shape, F32, kind="ExternalInput").ap() for k, v in arrays.items()}
    out = nc.dram_tensor("out_x", (1, 256, 1024), F32, kind="ExternalOutput").ap()
    build(nc, ins, out)
    r = _run(nc, [{f"in_{k}": v for k, v in arrays.items()}], core_ids=[0])
    return r.results[0]["out_x"]
```
